# Optimizing a Trainium2 kernel written in Bass

```python
import math
import jax, jax.numpy as jnp
from jax import lax
import numpy as np

D_MODEL = 1024
BATCH = 1
SEQ = 512
DEPTH = 2
DEC_BATCH = 8
DEC_SEQ = 1
PAST_LEN = 4096
PAGE_SIZE = 128

N_EVEN = (DEPTH + 1) // 2
N_ODD = DEPTH // 2
GLA_HEADS = 4
GLA_DK = D_MODEL // 16
GLA_DV = D_MODEL // 8
GLA_K_WIDTH = GLA_HEADS * GLA_DK
GLA_V_WIDTH = GLA_HEADS * GLA_DV
GATE_RANK = 16
GATE_NORMALIZER = 16.0
POOL_WINDOWS = (2, 4, 8, 16)
POOL_GROUPS = len(POOL_WINDOWS)
POOL_WIDTH = D_MODEL // 2
POOL_GROUP_WIDTH = POOL_WIDTH // POOL_GROUPS
POOL_BUF = max(POOL_WINDOWS) - 1
EVEN_IN = 2 * GLA_K_WIDTH + 2 * GLA_V_WIDTH + GATE_RANK + POOL_WIDTH
RET_HEADS = 4
RET_DK = D_MODEL // RET_HEADS
RET_DV = 2 * RET_DK
RET_QK_WIDTH = RET_HEADS * RET_DK
RET_V_WIDTH = RET_HEADS * RET_DV
ODD_IN = 2 * RET_QK_WIDTH + 2 * RET_V_WIDTH
ROPE_BASE = 10000.0
D_FF = -(-8 * D_MODEL // (3 * 256)) * 256
CHUNK = 64
EPS = 1e-6

kernel_name = "hybrid_gla_pool_retnet_step"

def rms_norm(x, gain=None):
    x32 = x.astype(jnp.float32)
    y = x32 * lax.rsqrt(jnp.mean(x32 * x32, axis=-1, keepdims=True) + EPS)
    if gain is not None:
        y = y * gain.astype(jnp.float32)
    return y.astype(x.dtype)

def gated_linear_recurrence(q, k, v, log_a, s0):
    B, H, L, dk = q.shape
    dv = v.shape[-1]
    c = CHUNK if L >= CHUNK else L
    n = -(-L // c)
    pad = n * c - L
    f32 = jnp.float32
    q, k, v, log_a = (t.astype(f32) for t in (q, k, v, log_a))
    if pad:
        pw = ((0, 0), (0, 0), (0, pad), (0, 0))
        q, k, v, log_a = (jnp.pad(t, pw) for t in (q, k, v, log_a))

    def to_chunks(t):
        return t.reshape(B, H, n, c, t.shape[-1]).transpose(2, 0, 1, 3, 4)

    mask = jnp.tril(jnp.ones((c, c), dtype=bool))

    def step(S, inp):
        qc, kc, vc, gc = inp
        b = jnp.cumsum(gc, axis=2)
        qe = qc * jnp.exp(b)
        ke = kc * jnp.exp(-b)
        att = jnp.where(mask, jnp.einsum('bhtd,bhsd->bhts', qe, ke), 0.0)
        o = jnp.einsum('bhtd,bhdv->bhtv', qe, S) + jnp.einsum('bhts,bhsv->bhtv', att, vc)
        b_last = b[:, :, -1:, :]
        S = jnp.exp(b_last[:, :, 0, :])[..., None] * S + jnp.einsum(
            'bhsd,bhsv->bhdv', kc * jnp.exp(b_last - b), vc)
        return S, o

    S, o = lax.scan(step, s0.astype(f32),
                    (to_chunks(q), to_chunks(k), to_chunks(v), to_chunks(log_a)))
    o = o.transpose(1, 2, 0, 3, 4).reshape(B, H, n * c, dv)[:, :, :L]
    return o, S

def multiscale_pool(u, buf, n_past, pool_w, pool_scale):
    B, L, P = u.shape
    f32 = jnp.float32
    ext = jnp.concatenate([buf.astype(f32), u.astype(f32)], axis=1)
    cs = jnp.concatenate([jnp.zeros((B, 1, P), f32), jnp.cumsum(ext, axis=1)], axis=1)
    end = cs[:, POOL_BUF + 1:]
    idx = jnp.arange(L, dtype=jnp.int32)
    means = []
    for g, w in enumerate(POOL_WINDOWS):
        sl = slice(g * POOL_GROUP_WIDTH, (g + 1) * POOL_GROUP_WIDTH)
        start = cs[:, POOL_BUF + 1 - w: POOL_BUF + 1 - w + L, sl]
        count = jnp.minimum(w, n_past + idx + 1).astype(f32)[None, :, None]
        means.append((end[..., sl] - start) / count)
    pooled = jnp.concatenate(means, axis=-1) - u.astype(f32)
    pooled = jnp.einsum('blgc,gcd->blgd',
                        pooled.reshape(B, L, POOL_GROUPS, POOL_GROUP_WIDTH),
                        pool_w.astype(f32)).reshape(B, L, P)
    pooled = pooled * pool_scale.astype(f32)
    return pooled.astype(u.dtype), ext[:, -POOL_BUF:]

def gla_pool_mixer(h, s_gla, s_pool, pos0, w_in, w_gate_b, b_gate, gla_gain,
                   pool_w, pool_scale, w_out):
    B, L, _ = h.shape
    proj = h @ w_in
    cuts = [GLA_K_WIDTH, 2 * GLA_K_WIDTH, 2 * GLA_K_WIDTH + GLA_V_WIDTH,
            2 * GLA_K_WIDTH + 2 * GLA_V_WIDTH, 2 * GLA_K_WIDTH + 2 * GLA_V_WIDTH + GATE_RANK]
    q, k, v, g, a, u = jnp.split(proj, cuts, axis=-1)

    def heads(t, d):
        return t.reshape(B, L, GLA_HEADS, d).transpose(0, 2, 1, 3)

    log_a = jax.nn.log_sigmoid((a @ w_gate_b + b_gate).astype(jnp.float32)) / GATE_NORMALIZER
    o, s_new = gated_linear_recurrence(heads(q, GLA_DK) * (GLA_DK ** -0.5), heads(k, GLA_DK),
                                       heads(v, GLA_DV), heads(log_a, GLA_DK), s_gla)
    o = rms_norm(o, gla_gain).astype(h.dtype)
    o = o.transpose(0, 2, 1, 3).reshape(B, L, GLA_V_WIDTH) * jax.nn.silu(g)
    p, buf_new = multiscale_pool(u, s_pool, pos0, pool_w, pool_scale)
    y = jnp.concatenate([o, p], axis=-1) @ w_out
    return y, s_new, buf_new

def theta_shift(x, sin, cos):
    x1 = x[..., 0::2]
    x2 = x[..., 1::2]
    rot = jnp.stack([-x2, x1], axis=-1).reshape(x.shape)
    return x * cos + rot * sin

def retention_mixer(h, s_ret, pos0, w_in, w_out):
    B, L, _ = h.shape
    f32 = jnp.float32
    proj = h @ w_in
    q, k, v, g = jnp.split(proj, [RET_QK_WIDTH, 2 * RET_QK_WIDTH,
                                  2 * RET_QK_WIDTH + RET_V_WIDTH], axis=-1)

    def heads(t, d):
        return t.reshape(B, L, RET_HEADS, d).transpose(0, 2, 1, 3).astype(f32)

    pos = pos0 + jnp.arange(L, dtype=f32)
    angle = jnp.repeat(1.0 / (ROPE_BASE ** jnp.linspace(0.0, 1.0, RET_DK // 2, dtype=f32)), 2)
    ang = pos[:, None] * angle[None, :]
    sin, cos = jnp.sin(ang), jnp.cos(ang)
    qh = theta_shift(heads(q, RET_DK), sin, cos)
    kh = theta_shift(heads(k, RET_DK) * (RET_DK ** -0.5), sin, cos)
    log_gamma = jnp.log(1.0 - 2.0 ** (-5.0 - jnp.arange(RET_HEADS, dtype=f32)))
    log_a = jnp.broadcast_to(log_gamma[None, :, None, None], (B, RET_HEADS, L, RET_DK))
    o, s_new = gated_linear_recurrence(qh, kh, heads(v, RET_DV), log_a, s_ret)
    o = rms_norm(o).astype(h.dtype)
    o = o.transpose(0, 2, 1, 3).reshape(B, L, RET_V_WIDTH) * jax.nn.silu(g)
    return o @ w_out, s_new

def swiglu(h, w_gate, w_up, w_down):
    return (jax.nn.silu(h @ w_gate) * (h @ w_up)) @ w_down

def run_trunk(x, s_gla, s_pool, s_ret, pos0, norm_mix, norm_ffn, norm_final,
              w_in_even, w_gate_b, b_gate, gla_gain, pool_w, pool_scale, w_out_even,
              w_in_odd, w_out_odd, w_ffn_gate, w_ffn_up, w_ffn_down):
    new_gla, new_pool, new_ret = [], [], []
    for i in range(DEPTH):
        h = rms_norm(x, norm_mix[i])
        if i % 2 == 0:
            e = i // 2
            y, sg, sp = gla_pool_mixer(h, s_gla[e], s_pool[e], pos0, w_in_even[e], w_gate_b[e],
                                       b_gate[e], gla_gain[e], pool_w[e], pool_scale[e],
                                       w_out_even[e])
            new_gla.append(sg)
            new_pool.append(sp)
        else:
            o = i // 2
            y, sr = retention_mixer(h, s_ret[o], pos0, w_in_odd[o], w_out_odd[o])
            new_ret.append(sr)
        x = x + y
        x = x + swiglu(rms_norm(x, norm_ffn[i]), w_ffn_gate[i], w_ffn_up[i], w_ffn_down[i])
    return rms_norm(x, norm_final), jnp.stack(new_gla), jnp.stack(new_pool), jnp.stack(new_ret)

def setup_inputs(seed: int = 0) -> dict:
    key = jax.random.key(seed)
    ks = jax.random.split(key, 24)
    f32 = jnp.float32

    def nrm(k, shape, scale):
        return jax.random.normal(k, shape, f32) * scale

    return {
        "x_prompt": nrm(ks[0], (BATCH, SEQ, D_MODEL), 1.0),
        "x_sample": nrm(ks[1], (DEC_BATCH, DEC_SEQ, D_MODEL), 1.0),
        "state_gla": nrm(ks[2], (N_EVEN, DEC_BATCH, GLA_HEADS, GLA_DK, GLA_DV), 0.5),
        "state_pool": nrm(ks[3], (N_EVEN, DEC_BATCH, POOL_BUF, POOL_WIDTH), 1.0),
        "state_ret": nrm(ks[4], (N_ODD, DEC_BATCH, RET_HEADS, RET_DK, RET_DV), 1.0),
        "norm_mix": 1.0 + nrm(ks[5], (DEPTH, D_MODEL), 0.02),
        "norm_ffn": 1.0 + nrm(ks[6], (DEPTH, D_MODEL), 0.02),
        "norm_final": 1.0 + nrm(ks[7], (D_MODEL,), 0.02),
        "w_in_even": nrm(ks[8], (N_EVEN, D_MODEL, EVEN_IN), D_MODEL ** -0.5),
        "w_gate_b": nrm(ks[9], (N_EVEN, GATE_RANK, GLA_K_WIDTH), GATE_RANK ** -0.5),
        "b_gate": nrm(ks[10], (N_EVEN, GLA_K_WIDTH), 0.1),
        "gla_gain": 1.0 + nrm(ks[11], (N_EVEN, GLA_DV), 0.02),
        "pool_w": nrm(ks[12], (N_EVEN, POOL_GROUPS, POOL_GROUP_WIDTH, POOL_GROUP_WIDTH),
                       POOL_GROUP_WIDTH ** -0.5),
        "pool_scale": 1.0 + nrm(ks[13], (N_EVEN, POOL_WIDTH), 0.02),
        "w_out_even": nrm(ks[14], (N_EVEN, GLA_V_WIDTH + POOL_WIDTH, D_MODEL),
                          (GLA_V_WIDTH + POOL_WIDTH) ** -0.5),
        "w_in_odd": nrm(ks[15], (N_ODD, D_MODEL, ODD_IN), D_MODEL ** -0.5),
        "w_out_odd": nrm(ks[16], (N_ODD, RET_V_WIDTH, D_MODEL), RET_V_WIDTH ** -0.5),
        "w_ffn_gate": nrm(ks[17], (DEPTH, D_MODEL, D_FF), D_MODEL ** -0.5),
        "w_ffn_up": nrm(ks[18], (DEPTH, D_MODEL, D_FF), D_MODEL ** -0.5),
        "w_ffn_down": nrm(ks[19], (DEPTH, D_FF, D_MODEL), D_FF ** -0.5),
    }

def reference(x_prompt, x_sample, state_gla, state_pool, state_ret, norm_mix, norm_ffn,
              norm_final, w_in_even, w_gate_b, b_gate, gla_gain, pool_w, pool_scale,
              w_out_even, w_in_odd, w_out_odd, w_ffn_gate, w_ffn_up, w_ffn_down):
    weights = (norm_mix, norm_ffn, norm_final, w_in_even, w_gate_b, b_gate, gla_gain, pool_w,
               pool_scale, w_out_even, w_in_odd, w_out_odd, w_ffn_gate, w_ffn_up, w_ffn_down)
    B = x_prompt.shape[0]
    z_gla = jnp.zeros((N_EVEN, B, GLA_HEADS, GLA_DK, GLA_DV), jnp.float32)
    z_pool = jnp.zeros((N_EVEN, B, POOL_BUF, POOL_WIDTH), x_prompt.dtype)
    z_ret = jnp.zeros((N_ODD, B, RET_HEADS, RET_DK, RET_DV), jnp.float32)
    y_prompt, gla_p, pool_p, ret_p = run_trunk(x_prompt, z_gla, z_pool, z_ret, 0, *weights)
    y_sample, gla_s, pool_s, ret_s = run_trunk(x_sample, state_gla, state_pool, state_ret,
                                               PAST_LEN, *weights)
    return (y_prompt, y_sample,
            gla_p.astype(state_gla.dtype), gla_s.astype(state_gla.dtype),
            pool_p.astype(state_pool.dtype), pool_s.astype(state_pool.dtype),
            ret_p.astype(state_ret.dtype), ret_s.astype(state_ret.dtype))


_drawn_inputs = setup_inputs


def setup_inputs(seed=0):
    import zlib

    import numpy as np

    out = dict(_drawn_inputs(seed))
    spreads = {}
    factors = {'norm_ffn': 2.875, 'norm_final': 2.864, 'gla_gain': 5.311, 'pool_scale': 3.709}
    for name, (base, spread) in spreads.items():
        noise = np.random.default_rng([zlib.crc32(name.encode()), seed]).standard_normal(out[name].shape)
        drawn = base * np.exp(spread * noise) if base else spread * noise
        out[name] = __import__('jax').numpy.asarray(drawn.astype(out[name].dtype))
    for name, factor in factors.items():
        out[name] = (out[name] * factor).astype(out[name].dtype)
    return out
```

```python
from contextlib import ExitStack

import numpy as np

import concourse.bass as bass
from concourse import mybir

F32 = mybir.dt.float32
F32R = mybir.dt.float32r
ACT = mybir.ActivationFunctionType
ALU = mybir.AluOpType
ds = bass.ds

P = 128
DM, KT = 1024, 8
NP_, NS, T = 512, 8, 520
HT = T // 2
BLK = NP_ // P
FT = 22
CH = 64
NCH = NP_ // CH
W_FULL, W_DOWN = 2048, 11 * P
HEADS = 4
EPS = 1e-6

N_E, N_EO, N_F, N_D, N_OI, N_OO = 8, 4, FT, 16, 24, 8
C_E = 0
C_EO = C_E + N_E
C_F = [C_EO + N_EO, 0]
C_D = [C_F[0] + N_F, 0]
C_OI = C_D[0] + N_D
C_OO = C_OI + N_OI
C_F[1] = C_OO + N_OO
C_D[1] = C_F[1] + N_F
E_ORDER = ["a", "q0", "q1", "k0", "z0", "k1", "z1", "v0", "v1", "v2", "v3", "u0", "u1", "p0", "u2", "p1",
           "u3", "g0", "p2", "g1", "p3", "g2", "g3"]
E_AT = {n: i for i, n in enumerate(E_ORDER)}
E_TILES = ["q0", "q1", "k0", "k1", "v0", "v1", "v2", "v3", "u0", "u1", "u2", "u3", "g0", "g1", "g2", "g3"]
M_EO = len(E_ORDER)
M_F = [M_EO + 8, 0]
M_D = [M_F[0] + 2 * FT, 0]
M_OI = M_D[0] + 8
M_OO = M_OI + 48
M_F[1] = M_OO + 8
M_D[1] = M_F[1] + 2 * FT
OO_ORDER = [8, 9, 10, 11, 4, 5, 0, 1, 2, 3, 6, 7, 12, 13, 14, 15]
AFTER_O, AFTER_OD = "g2", "g3"
V_GAIN, V_GLA, V_PS, V_BG, V_KS, V_GM, V_N = 0, 40, 41, 45, 47, 63, 67


def build(nc, io):
    at = nc.alloc_sbuf_tensor_at
    cursor = [16544]

    def fixed(name, shape, dt):
        t = at(name, shape, dt, offset=cursor[0])
        cursor[0] += (int(np.prod(shape[1:])) * 4 + 31) // 32 * 32
        return t

    TB = T * 4
    raw = [fixed(f"raw{i}", [P, W_FULL], F32) for i in range(2)]
    whi = [fixed(f"whi{i}", [P, W_FULL], F32R) for i in range(2)]
    wlo = [fixed(f"wlo{i}", [P, W_FULL], F32R) for i in range(2)]
    x = fixed("x", [P, KT, T], F32)
    h = [fixed("h_hi", [P, KT, T], F32R), fixed("h_lo", [P, KT, T], F32R)]
    rstd, acc, sq, rs, t0, t1, t2, t3 = [fixed(n, [P, T], F32)
                                         for n in ("rstd", "acc", "sq", "rs", "t0", "t1", "t2", "t3")]
    tmp = [t0, t1, t2, t3]
    RS_OFF = cursor[0] - 5 * ((TB + 31) // 32 * 32)
    ident = fixed("ident", [P, P], F32)
    ones = fixed("ones", [P, 16], F32)
    vec = fixed("vec", [P, V_N], F32)
    eps = fixed("eps", [P, 8], F32)
    rt = fixed("rt", [P, 20], F32)
    rr = fixed("rr", [P, 20], F32)
    R, TOP = cursor[0], 229344

    def region(name, shape, dt, off):
        size = int(np.prod(shape[1:])) * 4
        assert R + off + size <= TOP, (name, R + off + size - TOP)
        return at(name, shape, dt, offset=R + off), off + size

    hid_hi, o = region("hid_hi", [P, FT, T], F32R, 0)
    hid_lo, o = region("hid_lo", [P, FT, T], F32R, o)
    eq, o = region("eq", [P, 2, T], F32, 0)
    ek, o = region("ek", [P, 2, T], F32, o)
    eb, o2 = region("eb", [P, 2, T], F32, o)
    et, o3 = region("et", [P, 2, T], F32, o2)
    states, _ = region("states", [P, 2, NCH, P], F32, o)
    ex, o = region("ex", [P, 2, T], F32, o3)
    kdtok, _ = region("kdtok", [P, BLK, 256], F32, o3)
    ke, o = region("ke", [P, 2, T], F32, o)
    ev, op_off = region("ev", [P, 4, T], F32, o)
    op_hi, o = region("op_hi", [P, KT, T], F32R, op_off)
    gsil, _ = region("gsil", [P, 4, T], F32, o)
    op_lo, end = region("op_lo", [P, KT, T], F32R, o)
    pbuf, o = region("pbuf", [P, 4, NS, 15], F32, op_off)
    wa_raw, o2 = region("wa_raw", [P, KT * P], F32, o)
    evs, _ = region("evs", [NS, 512], F32, o)
    wa_hi, o = region("wa_hi", [P, KT * P], F32R, o2)
    wa_lo, o = region("wa_lo", [P, KT * P], F32R, o)
    reset, o = region("reset", [P, NP_], F32, o)
    wgb, o = region("wgb", [16, 256], F32, o)
    a16, o = region("a16", [16, T], F32, o)
    assert o <= end
    att, o = region("att", [P, 4, BLK, P], F32, end)
    evtok, o = region("evtok", [P, BLK, 512], F32, o)
    gs, o = region("gs", [P, 2, NS, P], F32, o)
    poolw, o = region("poolw", [P, 4, P], F32, o)
    elast, o = region("elast", [P, 2, NCH], F32, o)
    eas, o = region("eas", [P, 2, NS], F32, o)
    invc, o = region("invc", [P, 4, 16], F32, o)
    pout, o = region("pout", [P, 4, NS + 1, 15], F32, o)
    o32, oh = region("o32", [P, 16, T], F32, 0)
    o_lo, _ = region("o_lo", [P, 16, T], F32R, 0)
    o_hi, _ = region("o_hi", [P, 16, T], F32R, oh)
    rq, o = region("rq", [P, 2, T], F32, oh)
    rst, _ = region("rst", [P, 2, 512], F32, o)
    rk, o = region("rk", [P, 2, T], F32, o)
    PROB_OFF = o
    prob, _ = region("prob", [P, 1280], F32, o)
    rv, o = region("rv", [P, 4, T], F32, o)
    vtok, o = region("vtok", [P, BLK, 512], F32, o)
    ktok, o = region("ktok", [P, BLK, 256], F32, o)
    rg, o = region("rg", [P, 4, T], F32, o)
    dec, o = region("dec", [P, NP_], F32, o)
    cs, o = region("cs", [P, 2, T], F32, o)
    sring, o = region("sring", [P, 4, 2, 512], F32, o)
    vs, o = region("vs", [64, 512], F32R, o)
    ks, o = region("ks", [P, 2, NS], F32, o)
    qs, o = region("qs", [P, 2, NS], F32, o)
    vsel, o = region("vsel", [P, NS], F32R, o)
    osel, o = region("osel", [P, P + NS], F32R, o)
    TAIL = 5632
    assert TAIL >= 1280 * 4 and TAIL + 2048 <= 4 * TB
    th, _ = region("th", [P, 512], F32R, PROB_OFF + TAIL)
    tl = at("tl", [P, 512], F32R, offset=RS_OFF)

    with ExitStack() as ctx:
        def sem(name):
            return ctx.enter_context(nc.semaphore(name))

        ps = [ctx.enter_context(nc.psum_tensor(f"ps{i}", [P, 2, 512], F32)) for i in range(2)]
        ax = [ctx.enter_context(nc.psum_tensor(f"ax{i}", [P, 512], F32)) for i in range(4)]
        s_raw = [sem("raw0_loaded"), sem("raw1_loaded")]
        s_whi, s_wlo = sem("weights_hi"), sem("weights_lo")
        s_mm, s_out, s_half = sem("mtile_done"), sem("mtile_taken"), sem("half_mtile_done")
        s_x = [sem(f"x{i}_loaded") for i in range(4)]
        s_vec, s_ones, s_id, s_wa = sem("vec_loaded"), sem("ones_loaded"), sem("ident_loaded"), sem("wa_loaded")
        s_reset, s_wgb, s_gsl, s_poolw, s_pbuf, s_invc = [sem(n + "_loaded") for n in
                                                         ("reset", "wgb", "gs", "poolw", "pbuf", "invc")]
        s_eps = sem("eps_set")
        s_hhi, s_hlo = sem("h_hi_written"), sem("h_lo_written")
        s_sq, s_acc = sem("x_squared"), sem("squares_summed")
        s_ms, s_rt, s_rr, s_bc, s_rstd = (sem("mean_square"), sem("rms"), sem("rms_inverted"),
                                          sem("rstd_spread"), sem("rstd_written"))
        s_sg, s_hid, s_hidhi, s_hidlo = sem("silu_gate"), sem("hidden"), sem("hidden_hi"), sem("hidden_lo")
        s_wah, s_wal, s_z1, s_sp, s_la, s_b, s_eb, s_enb = [sem(n) for n in (
            "wa_hi_written", "wa_lo_written", "z_written", "softplus_step", "log_decay", "decay_summed",
            "decay_exp", "decay_exp_inv")]
        s_qe, s_ke, s_dl, s_edl, s_kd, s_gsd = [sem(n) for n in (
            "q_decayed", "k_decayed", "decay_to_end", "decay_to_end_exp", "k_decayed_to_end", "gla_dec_decayed")]
        s_vt, s_vtc, s_at, s_atc, s_am = [sem(n) for n in (
            "gla_v_turned", "gla_v_taken", "gla_att", "gla_att_taken", "gla_att_masked")]
        s_kt, s_ktc, s_vb, s_dn, s_u, s_st = [sem(n) for n in (
            "gla_kv_turned", "gla_kv_taken", "gla_v_spread", "gla_dec_state", "gla_chunk_kv", "gla_states")]
        s_o, s_oc, s_od, s_odc, s_osq = [sem(n) for n in (
            "gla_o", "gla_o_taken", "gla_dec_o", "gla_dec_o_taken", "gla_o_squared")]
        s_oms, s_ort, s_orr, s_obc, s_on = [sem(n) for n in (
            "gla_ms", "gla_rms", "gla_rms_inverted", "gla_rstd_spread", "gla_o_normed")]
        s_gs, s_og, s_ophi, s_oplo = sem("gla_silu"), sem("gla_gated"), sem("op_hi_written"), sem("op_lo_written")
        s_pl, s_pm, s_rows = sem("pool_step"), sem("pooled"), sem("pool_rows_written")
        s_es = sem("even_stores")
        r_cs, r_csr, r_d = sem("ret_tables_loaded"), sem("ret_tables_scaled"), sem("ret_decay_loaded")
        r_rp, r_rot, r_ks = sem("ret_rope_products"), sem("ret_rotated"), sem("ret_dec_k")
        r_tr, r_trc, r_sc, r_p = sem("ret_turned"), sem("ret_turned_taken"), sem("ret_scores"), sem("ret_probs")
        r_pv, r_pvc, r_st, r_stc, r_sto = [sem(n) for n in (
            "ret_pv", "ret_pv_taken", "ret_state", "ret_state_taken", "ret_state_stored")]
        r_in = [sem(f"ret_dec_in{i}") for i in range(4)]
        r_so = [sem(f"ret_dec_stored{i}") for i in range(4)]
        r_g, r_vb, r_sn, r_os, r_osc = [sem(n) for n in (
            "ret_dec_decayed", "ret_v_spread", "ret_dec_state", "ret_dec_o", "ret_dec_o_taken")]
        r_z = sem("ret_dec_v_zeroed")
        r_vl, r_sel, r_ta, r_qs, r_th, r_tl, r_osr, r_ot, r_rc = [sem(n) for n in (
            "ret_dec_v_lo", "ret_selectors", "ret_dec_q0", "ret_dec_qsum", "ret_dec_sum_hi", "ret_dec_sum_lo",
            "ret_dec_o_rows", "ret_dec_o_turned", "ret_rstd_copied")]
        r_sq, r_acc, r_ms, r_rt, r_rr, r_bc = [sem(n) for n in (
            "ret_o_squared", "ret_squares", "ret_ms", "ret_rms", "ret_rms_inverted", "ret_rstd_spread")]
        r_sg, r_on, r_gd = sem("ret_silu"), sem("ret_normed"), sem("ret_gated")
        s_ohi, s_olo = sem("o_hi_written"), sem("o_lo_written")
        s_y, s_yst = sem("y_written"), sem("y_stored")
        s_astep, s_pstep, s_tstep = sem("scalar_step"), sem("gpsimd_step"), sem("tensor_step")
        block = ctx.enter_context(nc.Block())

        def halves(t, i):
            return t[:, ds(i, 1), :].rearrange("p a (b n) -> p (a b) n", b=2)

        def flat(t, i):
            return t[:, ds(i, 1), :].rearrange("p a n -> p (a n)")

        def two(t):
            return t[:].rearrange("p (b n) -> p b n", b=2)

        def mt(m):
            return ps[m % 2][:, :, 0:HT]

        def want(eng, s, v):
            if not isinstance(v, int) or v > 0:
                eng.wait_ge(s, v)

        def gain(n, m):
            return vec[:, ds(V_GAIN + 8 * n + m, 1)]

        BLOCKS = [(0, 0, P), (P, 0, P), (2 * P, 0, P), (3 * P, 0, P), (T - P, P - NS, NS)]

        @block.sync
        def _(sp):
            def load(c, slot, src, idx, n):
                if not isinstance(c, int) or c >= 2:
                    sp.wait_ge(s_whi, c - 1)
                    sp.wait_ge(s_wlo, c - 1)
                sp.dma_start(raw[slot][:, 0:n],
                             src[ds(idx, 1)].rearrange("a p n -> p (a n)")).then_inc(s_raw[slot], 16)

            def phase(c0, n, src, size, first=0):
                with sp.Fori(first // 2, n // 2) as i:
                    for j in range(2):
                        load(c0 + 2 * i + j, j, src, 2 * i + j, size)

            sp.dma_start(vec[:], io["vec"]).then_inc(s_vec, 16)
            sp.dma_start(wa_raw[:], io["w_a"]).then_inc(s_wa, 16)
            for q in range(4):
                sp.dma_start(x[:, 2 * q:2 * q + 2, :], io["x"][:, 2 * q:2 * q + 2, :]).then_inc(s_x[q], 16)
            for c in range(2):
                load(c, c, io["w_e"], c, W_FULL)
            for dst, name, s in ((ones, "ones", s_ones), (ident, "ident", s_id), (reset, "reset", s_reset),
                                 (wgb, "wgb", s_wgb), (gs, "gs", s_gsl), (poolw, "poolw", s_poolw),
                                 (pbuf, "pbuf", s_pbuf), (invc, "invc", s_invc)):
                sp.dma_start(dst[:], io[name]).then_inc(s, 16)
            phase(C_E, N_E, io["w_e"], W_FULL, 2)
            phase(C_EO, N_EO, io["w_eo"], W_FULL)
            phase(C_F[0], N_F, io["w_f0"], W_FULL)
            phase(C_D[0], N_D, io["w_d0"], W_DOWN)
            for j in range(2):
                load(C_OI + j, j, io["w_oi"], j, W_FULL)
            sp.wait_ge(s_mm, M_OI)
            sp.dma_start(cs[:], io["cs"]).then_inc(r_cs, 16)
            phase(C_OI, N_OI, io["w_oi"], W_FULL, 2)
            phase(C_OO, N_OO, io["w_oo"], W_FULL)
            phase(C_F[1], N_F, io["w_f1"], W_FULL)
            phase(C_D[1], N_D, io["w_d1"], W_DOWN)
            for m in range(KT):
                sp.wait_ge(s_y, m + 1)
                sp.dma_start(io["y"][:, m, :], x[:, m, :]).then_inc(s_yst, 16)
            sp.wait_ge(s_yst, 16 * KT)
            sp.wait_ge(s_es, 16 * 3)
            sp.wait_ge(r_sto, 16 * HEADS)
            for q in range(4):
                sp.wait_ge(r_so[q], 16 * HEADS * NS // 4)

        @block.scalar
        def _(act):
            def hi(c, slot, size, used):
                act.wait_ge(s_raw[slot], 8 * (c - slot) + 16)
                if used is not None:
                    act.wait_ge(*used)
                act.activation(whi[slot][:, 0:size], raw[slot][:, 0:size], ACT.Copy).then_inc(s_whi, 1)

            def settled():
                act.sem_inc(s_astep, 1)

            def h_hi(n, m, ready):
                act.wait_ge(*ready)
                settled()
                act.activation(flat(h[0], m), flat(x, m), ACT.Copy, scale=gain(n, m)).then_inc(s_hhi, 1)

            def root(n):
                act.wait_ge(s_ms, n + 1)
                act.activation(rt[:, 0:5], ax[3][:, 64:69], ACT.Sqrt, bias=eps[:, 0:1]).then_inc(s_rt, 1)
                act.wait_ge(s_bc, n + 1)
                act.activation(rstd[:, 0:NP_], ax[2][:], ACT.Copy)
                act.activation(rstd[:, NP_:T], ax[3][:, 72:72 + NS], ACT.Copy).then_inc(s_rstd, 1)

            act.wait_ge(s_wa, 16)
            act.activation(wa_hi[:], wa_raw[:], ACT.Copy).then_inc(s_wah, 1)
            act.wait_ge(s_vec, 16)
            for m in range(KT):
                h_hi(0, m, (s_x[m // 2], 16))
            for c in range(2):
                hi(c, c, W_FULL, None)
            act.wait_ge(s_eps, 1)
            root(0)

            def e_hi(n):
                hi(n + 2, n % 2, W_FULL, (s_mm, E_AT[E_TILES[2 * n + 1]] + 1))

            e_hi(0)
            e_hi(1)
            act.wait_ge(s_z1, 2)
            act.activation(et[:], ex[:], ACT.Abs).then_inc(s_sp, 1)
            act.wait_ge(s_sp, 1)
            act.activation(et[:], et[:], ACT.Exp, scale=-1.0).then_inc(s_sp, 1)
            act.wait_ge(s_sp, 2)
            act.activation(et[:], et[:], ACT.Ln, bias=1.0).then_inc(s_sp, 1)
            e_hi(2)
            act.wait_ge(s_b, 3)
            act.activation(eb[:], et[:], ACT.Exp, scale=1.0 / 16).then_inc(s_eb, 1)
            act.activation(ex[:], et[:], ACT.Exp, scale=-1.0 / 16).then_inc(s_enb, 1)
            act.wait_ge(s_dl, 2)
            act.activation(ex[:, :, 0:NP_], ex[:, :, 0:NP_], ACT.Exp, scale=1.0 / 16).then_inc(s_edl, 1)
            e_hi(3)
            for b in range(BLK):
                act.wait_ge(s_vt, b + 1)
                act.activation(evtok[:, b, :], ax[b][:], ACT.Copy).then_inc(s_vtc, 1)
            e_hi(4)

            def silu_g(q):
                act.wait_ge(s_out, E_AT[f"g{q}"] + 1)
                act.activation(gsil[:, q, :], gsil[:, q, :], ACT.Silu).then_inc(s_gs, 1)

            def pool_hi(q):
                act.wait_ge(s_mm, E_AT[f"p{q}"] + 1)
                act.activation(halves(op_hi, 4 + q), mt(E_AT[f"p{q}"]), ACT.Copy,
                               scale=vec[:, V_PS + q:V_PS + q + 1]).then_inc(s_ophi, 1)

            for q in range(4):
                act.wait_ge(s_at, q + 1)
                act.activation(att[:, q].rearrange("p b n -> p (b n)"), ax[q][:], ACT.Copy).then_inc(s_atc, 1)
            for q in range(2):
                act.wait_ge(s_kt, q + 1)
                act.activation(kdtok[:, 2 * q:2 * q + 2, :].rearrange("p b n -> p (b n)"), ax[q][:],
                               ACT.Copy).then_inc(s_ktc, 1)
                if q == 0:
                    pool_hi(0)
            act.wait_ge(s_kt, 3)
            act.activation(evs[:], ax[2][0:NS, :], ACT.Copy).then_inc(s_ktc, 1)
            pool_hi(1)
            e_hi(5)

            for name in E_ORDER[E_AT["g0"]:]:
                q = int(name[1])
                silu_g(q) if name[0] == "g" else pool_hi(q)
                if name == "g1":
                    e_hi(6)
                if name == AFTER_O:
                    for k in range(HEADS):
                        act.wait_ge(s_o, k + 1)
                        act.activation(ev[:, k, 0:NP_], ax[k][:], ACT.Copy).then_inc(s_oc, 1)
                if name == AFTER_OD:
                    act.wait_ge(s_od, 1)
                    for r in range(2):
                        a = act.activation(ev[:, r:4:2, NP_:T], ax[r][:, 0:16].rearrange("p (i b) -> p i b", i=2), ACT.Copy)
                    a.then_inc(s_odc, 1)
            e_hi(7)
            act.wait_ge(s_oms, 4)
            act.activation(rt[:], ax[3][:, 64:84], ACT.Sqrt, bias=eps[:, 0:1], scale=8.0).then_inc(s_ort, 1)
            for q in range(HEADS):
                act.wait_ge(s_og, q + 1)
                act.activation(op_hi[:, q, :], tmp[q][:], ACT.Copy).then_inc(s_ophi, 1)
            for n in range(N_EO):
                for j in range(2):
                    h_hi(1, 2 * n + j, (s_out, M_EO + 2 * n + j + 1))
                hi(C_EO + n + 2, n % 2, W_FULL, (s_mm, M_EO + 2 * n + 2))

            def ffn(l):
                c0, m0, d0, dm = C_F[l], M_F[l], C_D[l], M_D[l]
                nrm = 1 + 2 * l

                def pair(i, size, first=False):
                    for j in range(2):
                        n = 2 * i + j
                        g = FT * l + n
                        if first and j == 0:
                            root(1 + 2 * l)
                        act.wait_ge(s_out, m0 + 2 * n + 1)
                        want(act, s_hid, g)
                        act.activation(t1[:], t0[:], ACT.Silu).then_inc(s_sg, 1)
                        hi(c0 + n + 2, j, size, (s_mm, m0 + 2 * n + 2))
                        act.wait_ge(s_hid, g + 1)
                        settled()
                        act.activation(flat(hid_hi, n), t3[:], ACT.Copy).then_inc(s_hidhi, 1)

                pair(0, W_FULL, first=True)
                with act.Fori(1, N_F // 2 - 1) as i:
                    pair(i, W_FULL)
                pair(N_F // 2 - 1, W_DOWN)

                def down(m, size):
                    if size:
                        hi(d0 + 2 * m + 2, 0, size, (s_half, KT * l + m + 1))
                    if l == 0:
                        h_hi(2, m, (s_out, dm + m + 1))
                    if size:
                        hi(d0 + 2 * m + 3, 1, size, (s_mm, dm + m + 1))

                with act.Fori(0, KT - 1) as m:
                    down(m, W_DOWN)
                down(KT - 1, W_FULL if l == 0 else 0)

            ffn(0)

            act.wait_ge(s_mm, M_OI)
            act.activation(vsel[:], ones[:, 8:16], ACT.Copy).then_inc(r_sel, 1)
            act.wait_ge(s_out, M_OI)
            act.activation(osel[:], rstd[:, 0:P + NS], ACT.Copy, scale=0.0).then_inc(r_sel, 1)
            act.wait_ge(r_sel, 2)
            act.activation(osel[:, NS - 1:NS], ones[:, 1:2], ACT.Copy).then_inc(r_sel, 1)

            def finish_o(hp):
                act.wait_ge(r_os, 8 * hp + 8)
                act.activation(acc[0:NS, 0:512], ax[3][0:NS, :], ACT.Copy).then_inc(r_osr, 1)
                act.wait_ge(r_ot, hp + 1)
                settled()
                act.activation(o32[:, ds(4 * hp, 4), NP_:T], ax[3][:, 0:32].rearrange("p (d b) -> p d b", d=4),
                               ACT.Copy).then_inc(r_osc, 1)

            def finish_root(hp):
                act.wait_ge(r_ms, hp + 1)
                act.activation(rt[:, 0:5], ax[3][:, 64:69], ACT.Sqrt, bias=eps[:, 0:1], scale=2.0).then_inc(r_rt, 1)

            def finish_copy(hp):
                act.wait_ge(r_bc, hp + 1)
                act.activation(rs[:, 0:NP_], ax[2][:], ACT.Copy)
                act.activation(rs[:, NP_:T], ax[3][:, 72:72 + NS], ACT.Copy).then_inc(r_rc, 1)

            def decay(hh, b):
                n = 8 * hh + b
                act.wait_ge(r_in[b % 4], 16 * (2 * hh + b // 4 + 1))
                settled()
                act.activation(sring[:, b % 4].rearrange("p t n -> p (t n)"), sring[:, b % 4].rearrange("p t n -> p (t n)"),
                               ACT.Copy, scale=vec[:, ds(V_GM + hh, 1)]).then_inc(r_g, 1)

            def q_first(hh, b):
                act.wait_ge(r_sn, 8 * hh + b + 1)
                act.activation(sq[:, 0:512], sring[:, b % 4, 0, :], ACT.Copy, scale=qs[:, 0, b:b + 1]).then_inc(r_ta, 1)

            def sum_hi(hh, b):
                want(act, r_os, 8 * hh + b)
                act.wait_ge(r_qs, 8 * hh + b + 1)
                act.activation(th[:], sq[:, 0:512], ACT.Copy).then_inc(r_th, 1)

            def head(hh):
                m0 = M_OI + 12 * hh
                first = isinstance(hh, int) and hh == 0

                def chunk(n):
                    hi(C_OI + 6 * hh + n + 2, n % 2, W_FULL, (s_mm, m0 + 2 * n + 2))

                if first:
                    root(2)
                else:
                    q_first(hh - 1, 7)
                    sum_hi(hh - 1, 7)
                chunk(0)
                if not first:
                    finish_o(hh - 1)
                chunk(1)
                for b in range(BLK):
                    act.wait_ge(r_tr, 7 * hh + b + 1)
                    act.activation(vtok[:, b, :], ax[b % 2][:], ACT.Copy).then_inc(r_trc, 1)
                    if b == 1:
                        chunk(2)
                if not first:
                    finish_root(hh - 1)
                    finish_copy(hh - 1)
                chunk(3)
                act.wait_ge(r_tr, 7 * hh + 5)
                if first:
                    act.wait_ge(r_z, 1)
                act.activation(vs[0:NS, :], ax[3][0:NS, :], ACT.Copy).then_inc(r_trc, 1)
                decay(hh, 0)
                decay(hh, 1)

                def silu(q):
                    act.wait_ge(s_out, m0 + 8 + q + 1)
                    if not first:
                        act.wait_ge(r_gd, 4 * hh)
                    act.activation(rg[:, q, :], tmp[q][:], ACT.Silu).then_inc(r_sg, 1)

                silu(0)
                decay(hh, 2)
                q_first(hh, 0)
                silu(1)
                chunk(4)
                sum_hi(hh, 0)
                decay(hh, 3)
                q_first(hh, 1)
                silu(2)
                for q in range(2):
                    act.wait_ge(r_tr, 7 * hh + 6 + q)
                    settled()
                    for b in range(2):
                        a = act.activation(ktok[:, 2 * q + b, :], ax[q][:, 256 * b:256 * b + 256], ACT.Copy,
                                           scale=vec[:, ds(V_KS + 4 * hh + 2 * q + b, 1)])
                    a.then_inc(r_trc, 1)
                sum_hi(hh, 1)
                q_first(hh, 2)
                silu(3)
                chunk(5)
                sum_hi(hh, 2)
                q_first(hh, 3)

                def pv(q):
                    act.wait_ge(r_pv, 4 * hh + q + 1)
                    settled()
                    act.activation(o32[:, ds(4 * hh + q, 1), 0:NP_].rearrange("p a n -> p (a n)"), ax[q % 2][:],
                                   ACT.Copy).then_inc(r_pvc, 1)

                def state(q):
                    act.wait_ge(r_st, 2 * hh + q + 1)
                    act.activation(rst[:, q, :], ax[q][:], ACT.Copy).then_inc(r_stc, 1)

                pv(0)
                decay(hh, 4)
                pv(1)
                sum_hi(hh, 3)
                q_first(hh, 4)
                pv(2)
                decay(hh, 5)
                pv(3)
                sum_hi(hh, 4)
                q_first(hh, 5)
                decay(hh, 6)
                state(0)
                sum_hi(hh, 5)
                q_first(hh, 6)
                decay(hh, 7)
                state(1)
                sum_hi(hh, 6)

            head(0)
            with act.Fori(1, HEADS) as hh:
                head(hh)
            q_first(HEADS - 1, 7)
            sum_hi(HEADS - 1, 7)

            def out_hi(n):
                k = OO_ORDER[n]
                act.activation(o_hi[:, k, :], o32[:, k, :], ACT.Copy).then_inc(s_ohi, 1)

            for n in range(8):
                out_hi(n)
            act.wait_ge(r_sto, 16 * HEADS)
            out_hi(8)
            out_hi(9)
            finish_o(HEADS - 1)
            out_hi(10)
            out_hi(11)
            finish_root(HEADS - 1)
            finish_copy(HEADS - 1)
            for q in range(4):
                act.wait_ge(r_gd, 4 * (HEADS - 1) + q + 1 if q < 2 else 16)
                out_hi(12 + q)
            with act.Fori(0, N_OO // 2) as i:
                for j in range(2):
                    n = 2 * i + j
                    h_hi(3, n, (s_out, M_OO + n + 1))
                    hi(C_OO + n + 2, j, W_FULL, (s_mm, M_OO + n + 1))
            ffn(1)
            root(4)

        @block.vector
        def _(dve):
            def lo(c, slot, size):
                dve.wait_ge(s_whi, c + 1)
                dve.tensor_tensor(wlo[slot][:, 0:size], raw[slot][:, 0:size], whi[slot][:, 0:size].bitcast(F32),
                                  ALU.subtract).then_inc(s_wlo, 1)

            def h_lo(n, m):
                dve.wait_ge(s_hhi, 8 * n + m + 1)
                dve.scalar_tensor_tensor(out=flat(h[1], m), in0=flat(x, m), scalar=gain(n, m),
                                         in1=flat(h[0], m).bitcast(F32), op0=ALU.mult,
                                         op1=ALU.subtract).then_inc(s_hlo, 1)

            def invert(n):
                dve.wait_ge(s_rt, n + 1)
                dve.reciprocal(rr[:, 0:5], rt[:, 0:5]).then_inc(s_rr, 1)

            def taken(m, par, out, other=None, op=ALU.mult):
                dve.wait_ge(s_mm, m + 1)
                dve.tensor_tensor(out, ps[par][:, :, 0:HT], two(rstd) if other is None else other, op).then_inc(s_out, 1)

            dve.wait_ge(s_wah, 1)
            dve.tensor_tensor(wa_lo[:], wa_raw[:], wa_hi[:].bitcast(F32), ALU.subtract).then_inc(s_wal, 1)
            dve.wait_ge(s_vec, 16)
            for m in range(KT):
                h_lo(0, m)
            for c in range(2):
                lo(c, c, W_FULL)
            invert(0)
            dve.wait_ge(s_rstd, 1)
            steps = {n: [] for n in E_ORDER}

            def e_take(name, out):
                i = E_AT[name]
                taken(i, i % 2, out)

            def z_tile(i):
                m = E_AT[f"z{i}"]
                dve.wait_ge(s_mm, m + 1)
                dve.tensor_scalar(halves(ex, i), mt(m), vec[:, V_BG + i:V_BG + i + 1], None, ALU.add).then_inc(s_out, 1)
                dve.wait_ge(s_out, m + 1)
                dve.sem_inc(s_z1, 1)

            i = E_AT["a"]
            dve.wait_ge(s_mm, i + 1)
            dve.tensor_tensor(a16[:].rearrange("p (b n) -> p b n", b=2), ps[i % 2][0:16, :, 0:HT],
                              rstd[0:16, :].rearrange("p (b n) -> p b n", b=2), ALU.mult).then_inc(s_out, 1)
            e_take("q0", halves(eq, 0))
            e_take("q1", halves(eq, 1))
            lo(2, 0, W_FULL)
            e_take("k0", halves(ek, 0))
            z_tile(0)
            e_take("k1", halves(ek, 1))
            lo(3, 1, W_FULL)
            z_tile(1)
            e_take("v0", halves(ev, 0))
            dve.wait_ge(s_sp, 3)
            dve.scalar_tensor_tensor(out=eb[:], in0=ex[:], scalar=0.0, in1=et[:], op0=ALU.min,
                                     op1=ALU.subtract).then_inc(s_la, 1)
            dve.wait_ge(s_la, 1)
            dve.wait_ge(s_reset, 16)
            for i in range(2):
                dve.tensor_tensor_scan(et[:, i, 0:NP_], reset[:], eb[:, i, 0:NP_], 0.0, ALU.mult, ALU.add).then_inc(s_b, 1)
            dve.tensor_copy(et[:, :, NP_:T], eb[:, :, NP_:T]).then_inc(s_b, 1)
            e_take("v1", halves(ev, 1))
            lo(4, 0, W_FULL)
            dve.wait_ge(s_eb, 1)
            dve.scalar_tensor_tensor(out=eq[:, :, 0:NP_], in0=eq[:, :, 0:NP_], scalar=0.125, in1=eb[:, :, 0:NP_],
                                     op0=ALU.mult, op1=ALU.mult).then_inc(s_qe, 1)
            dve.tensor_scalar(eq[:, :, NP_:T], eq[:, :, NP_:T], 0.125, None, ALU.mult).then_inc(s_qe, 1)
            dve.tensor_copy(elast[:], eb[:, :, CH - 1:NP_:CH]).then_inc(s_qe, 1)
            dve.tensor_copy(eas[:], eb[:, :, NP_:T]).then_inc(s_qe, 1)
            dve.wait_ge(s_enb, 1)
            dve.tensor_tensor(ke[:, :, 0:NP_], ek[:, :, 0:NP_], ex[:, :, 0:NP_], ALU.mult).then_inc(s_ke, 1)
            dve.wait_ge(s_ke, 1)
            for i in range(2):
                dve.tensor_tensor(ex[:, i, 0:NP_].rearrange("p (c n) -> p c n", n=CH),
                                  et[:, i, CH - 1:NP_:CH].unsqueeze(2).to_broadcast([P, NCH, CH]),
                                  et[:, i, 0:NP_].rearrange("p (c n) -> p c n", n=CH), ALU.subtract).then_inc(s_dl, 1)
            e_take("v2", halves(ev, 2))
            dve.wait_ge(s_edl, 1)
            dve.tensor_tensor(ek[:, :, 0:NP_], ek[:, :, 0:NP_], ex[:, :, 0:NP_], ALU.mult).then_inc(s_kd, 1)
            dve.wait_ge(s_gsl, 16)
            dve.wait_ge(s_qe, 4)
            dve.tensor_tensor(gs[:].rearrange("p i b n -> p (i b) n"), gs[:].rearrange("p i b n -> p (i b) n"),
                              eas[:].rearrange("p i b -> p (i b)").unsqueeze(2).to_broadcast([P, 2 * NS, P]),
                              ALU.mult).then_inc(s_gsd, 1)
            e_take("v3", halves(ev, 3))
            lo(5, 1, W_FULL)

            pools = [0]

            def step(ins):
                pools[0] += 1
                ins.then_inc(s_pl, 1)
                dve.wait_ge(s_pl, pools[0])

            def pool_group(g):
                u, wdw = tmp[g % 2], 2 << g
                pooled = (rs, acc)[g % 2]
                dve.wait_ge(s_out, E_AT[f"u{g}"] + 1)
                if g == 0:
                    dve.wait_ge(s_pbuf, 16)
                    dve.wait_ge(s_invc, 16)
                if g >= 2:
                    dve.wait_ge(s_mm, E_AT[f"p{g - 2}"] + 1)
                dve.tensor_copy(pout[:, g, NS, :], u[:, NP_ - 15:NP_])
                dve.tensor_copy(pout[:, g, 0:NS, 14:15].rearrange("p b n -> p (b n)"), u[:, NP_:T])
                dve.tensor_copy(pout[:, g, 0:NS, 0:14], pbuf[:, g, :, 1:15]).then_inc(s_rows, 1)
                cur = u
                for lv in range(g + 1):
                    d, nxt = 1 << lv, (t2, t3)[lv % 2]
                    dve.tensor_copy(nxt[:, 0:d], cur[:, 0:d])
                    step(dve.tensor_tensor(nxt[:, d:NP_], cur[:, d:NP_], cur[:, 0:NP_ - d], ALU.add))
                    cur = nxt
                dve.scalar_tensor_tensor(out=pooled[:, 16:NP_], in0=cur[:, 16:NP_], scalar=1.0 / wdw, in1=u[:, 16:NP_],
                                         op0=ALU.mult, op1=ALU.subtract)
                step(dve.tensor_tensor(cur[:, 0:16], cur[:, 0:16], invc[:, g, :], ALU.mult))
                dve.tensor_tensor(pooled[:, 0:16], cur[:, 0:16], u[:, 0:16], ALU.subtract)
                step(dve.tensor_reduce(cur[:, 16:24], pbuf[:, g, :, 16 - wdw:15], mybir.AxisListType.X, ALU.add))
                step(dve.tensor_tensor(cur[:, 16:24], cur[:, 16:24], u[:, NP_:T], ALU.add))
                dve.scalar_tensor_tensor(out=pooled[:, NP_:T], in0=cur[:, 16:24], scalar=1.0 / wdw, in1=u[:, NP_:T],
                                         op0=ALU.mult, op1=ALU.subtract).then_inc(s_pm, 1)

            def pool_lo(q):
                dve.wait_ge(s_ophi, q + 1)
                m = E_AT[f"p{q}"]
                dve.scalar_tensor_tensor(out=halves(op_lo, 4 + q), in0=mt(m), scalar=vec[:, V_PS + q:V_PS + q + 1],
                                         in1=halves(op_hi, 4 + q).bitcast(F32), op0=ALU.mult, op1=ALU.subtract)\
                   .then_inc(s_out, 1)
                dve.wait_ge(s_out, m + 1)
                dve.sem_inc(s_oplo, 1)

            e_take("u0", two(tmp[0]))
            pool_group(0)
            e_take("u1", two(tmp[1]))
            lo(6, 0, W_FULL)
            pool_group(1)
            pool_lo(0)
            e_take("u2", two(tmp[0]))
            pool_group(2)
            pool_lo(1)
            e_take("u3", two(tmp[1]))
            lo(7, 1, W_FULL)
            for b in range(NS):
                dve.wait_ge(s_vb, b // 2 + 1)
                for i in range(2):
                    dve.scalar_tensor_tensor(out=gs[:, i, b, :],
                                             in0=ax[b // 2][:, 256 * (b % 2) + 128 * i:256 * (b % 2) + 128 * i + 128],
                                             scalar=ek[:, i, NP_ + b:NP_ + b + 1], in1=gs[:, i, b, :], op0=ALU.mult,
                                             op1=ALU.add).then_inc(s_dn, 1)
            e_take("g0", halves(gsil, 0))
            dve.wait_ge(s_kd, 1)
            dve.wait_ge(s_u, 4)
            n = 0
            for c in range(NCH):
                for i in range(2):
                    u = ax[2 * i + c % 2][:, 128 * (c // 2):128 * (c // 2) + 128]
                    if c == 0:
                        dve.tensor_copy(states[:, i, 0, :], u).then_inc(s_st, 1)
                    else:
                        dve.wait_ge(s_st, n - 1)
                        dve.scalar_tensor_tensor(out=states[:, i, c, :], in0=states[:, i, c - 1, :],
                                                 scalar=elast[:, i, c:c + 1], in1=u, op0=ALU.mult,
                                                 op1=ALU.add).then_inc(s_st, 1)
                    n += 1
            pool_group(3)

            for name in E_ORDER[E_AT["g0"] + 1:]:
                q = int(name[1])
                e_take(name, halves(gsil, q)) if name[0] == "g" else pool_lo(q)
                if name == "g1":
                    lo(8, 0, W_FULL)
            lo(9, 1, W_FULL)
            dve.wait_ge(s_ort, 1)
            dve.reciprocal(rr[:], rt[:]).then_inc(s_orr, 1)
            for q in range(HEADS):
                dve.wait_ge(s_obc, q + 1)
                dve.scalar_tensor_tensor(out=ev[:, q, 0:NP_], in0=ev[:, q, 0:NP_], scalar=vec[:, V_GLA:V_GLA + 1],
                                         in1=ax[q % 3][:], op0=ALU.mult, op1=ALU.mult)
                dve.scalar_tensor_tensor(out=ev[:, q, NP_:T], in0=ev[:, q, NP_:T], scalar=vec[:, V_GLA:V_GLA + 1],
                                         in1=ax[3][:, 96 + 8 * q:104 + 8 * q], op0=ALU.mult, op1=ALU.mult).then_inc(s_on, 1)
                dve.wait_ge(s_on, q + 1)
                dve.wait_ge(s_gs, q + 1)
                dve.tensor_tensor(tmp[q][:], ev[:, q, :], gsil[:, q, :], ALU.mult).then_inc(s_og, 1)
                dve.wait_ge(s_ophi, 5 + q)
                dve.tensor_tensor(op_lo[:, q, :], tmp[q][:], op_hi[:, q, :].bitcast(F32), ALU.subtract).then_inc(s_oplo, 1)

            def residual(m, par, row):
                taken(m, par, halves(x, row), halves(x, row), ALU.add)

            for n in range(N_EO):
                for j in range(2):
                    m = 2 * n + j
                    residual(M_EO + m, (M_EO + m) % 2, m)
                    h_lo(1, m)
                lo(C_EO + n + 2, n % 2, W_FULL)

            def ffn(l):
                c0, m0, d0, dm = C_F[l], M_F[l], C_D[l], M_D[l]

                def pair(i, size, first=False):
                    for j in range(2):
                        n = 2 * i + j
                        g = FT * l + n
                        if first and j == 0:
                            invert(1 + 2 * l)
                            dve.wait_ge(s_rstd, 2 + 2 * l)
                            if l == 0:
                                dve.wait_ge(s_es, 48)
                            else:
                                for q in range(4):
                                    dve.wait_ge(r_so[q], 16 * HEADS * NS // 4)
                        want(dve, s_sg, g)
                        taken(m0 + 2 * n, m0 % 2, two(t0))
                        taken(m0 + 2 * n + 1, (m0 + 1) % 2, two(t2))
                        dve.wait_ge(s_out, m0 + 2 * n + 2)
                        dve.wait_ge(s_sg, g + 1)
                        want(dve, s_hidhi, g)
                        dve.tensor_tensor(t3[:], t2[:], t1[:], ALU.mult).then_inc(s_hid, 1)
                        lo(c0 + n + 2, j, size)
                        dve.wait_ge(s_hidhi, g + 1)
                        dve.tensor_tensor(flat(hid_lo, n), t3[:], flat(hid_hi, n).bitcast(F32),
                                          ALU.subtract).then_inc(s_hidlo, 1)

                pair(0, W_FULL, first=True)
                with dve.Fori(1, N_F // 2 - 1) as i:
                    pair(i, W_FULL)
                pair(N_F // 2 - 1, W_DOWN)

                def down(m, par, size):
                    if size:
                        lo(d0 + 2 * m + 2, 0, size)
                    residual(dm + m, par, m)
                    if l == 0:
                        h_lo(2, m)
                    if size:
                        lo(d0 + 2 * m + 3, 1, size)

                with dve.Fori(0, KT // 2 - 1) as i:
                    for j in range(2):
                        down(2 * i + j, (dm + j) % 2, W_DOWN)
                down(KT - 2, dm % 2, W_DOWN)
                down(KT - 1, (dm + 1) % 2, W_FULL if l == 0 else 0)

            ffn(0)

            def finish_invert(hp):
                dve.wait_ge(r_rt, hp + 1)
                dve.reciprocal(rr[:, 0:5], rt[:, 0:5]).then_inc(r_rr, 1)

            def finish_gate(hp, q):
                o = flat(o32, 4 * hp + q)
                dve.wait_ge(r_rc, hp + 1)
                dve.wait_ge(r_sg, 4 * hp + q + 1)
                dve.tensor_tensor(o, o, rs[:], ALU.mult).then_inc(r_on, 1)
                dve.wait_ge(r_on, 4 * hp + q + 1)
                dve.tensor_tensor(o, o, flat(rg, q), ALU.mult).then_inc(r_gd, 1)

            def new_state(hh, b):
                dve.wait_ge(r_vb, 8 * hh + b + 1)
                dve.wait_ge(r_g, 8 * hh + b + 1)
                dve.wait_ge(r_ks, hh + 1)
                for t in range(2):
                    a = dve.scalar_tensor_tensor(out=sring[:, b % 4, t, :], in0=ax[2][:], scalar=ks[:, t, b:b + 1],
                                                 in1=sring[:, b % 4, t, :], op0=ALU.mult, op1=ALU.add)
                a.then_inc(r_sn, 1)

            def q_sum(hh, b):
                dve.wait_ge(r_ta, 8 * hh + b + 1)
                dve.scalar_tensor_tensor(out=sq[:, 0:512], in0=sring[:, b % 4, 1, :], scalar=qs[:, 1, b:b + 1],
                                         in1=sq[:, 0:512], op0=ALU.mult, op1=ALU.add).then_inc(r_qs, 1)

            def sum_lo(hh, b):
                want(dve, r_os, 8 * hh + b)
                dve.wait_ge(r_th, 8 * hh + b + 1)
                dve.tensor_tensor(tl[:], sq[:, 0:512], th[:].bitcast(F32), ALU.subtract).then_inc(r_tl, 1)

            def head(hh):
                m0 = M_OI + 12 * hh
                first = isinstance(hh, int) and hh == 0

                def chunk(n):
                    lo(C_OI + 6 * hh + n + 2, n % 2, W_FULL)

                if first:
                    invert(2)
                    dve.wait_ge(s_rstd, 3)
                    dve.wait_ge(r_cs, 16)
                    for i in range(2):
                        dve.tensor_tensor(cs[:, i, :], cs[:, i, :], rstd[:], ALU.mult).then_inc(r_csr, 1)
                for t in range(4):
                    if t == 2 and not first:
                        dve.wait_ge(r_os, 8 * hh)
                    taken(m0 + t, (M_OI + t) % 2, halves(rv, t))
                    if t == 0 and not first:
                        q_sum(hh - 1, 7)
                        sum_lo(hh - 1, 7)
                    if t == 1:
                        chunk(0)
                    if t == 3:
                        chunk(1)
                dve.wait_ge(r_csr, 2)

                def rope(t, dst, k):
                    want(dve, r_rot, 4 * hh + 2 * k)
                    want(dve, r_sg, 4 * hh)
                    for u in range(2):
                        dve.wait_ge(s_mm, m0 + t + u + 1)
                        src = ps[(M_OI + t + u) % 2][:, :, 0:HT]
                        dve.tensor_tensor(two(tmp[u]), src, halves(cs, 0), ALU.mult)
                        dve.tensor_tensor(two(tmp[2 + u]), src, halves(cs, 1), ALU.mult).then_inc(s_out, 1)
                    dve.wait_ge(s_out, m0 + t + 2)
                    dve.tensor_tensor(dst[:, 0, :], t0[:], t3[:], ALU.subtract).then_inc(r_rot, 1)
                    dve.tensor_tensor(dst[:, 1, :], t1[:], t2[:], ALU.add).then_inc(r_rot, 1)

                rope(4, rq, 0)
                chunk(2)
                if not first:
                    dve.wait_ge(r_sto, 16 * hh)
                    finish_invert(hh - 1)
                rope(6, rk, 1)
                chunk(3)
                dve.wait_ge(r_rot, 4 * hh + 4)
                dve.tensor_copy(qs[:], rq[:, :, NP_:T])
                dve.tensor_scalar(ks[:], rk[:, :, NP_:T], 1.0 / 16, None, ALU.mult).then_inc(r_ks, 1)
                dve.wait_ge(r_trc, 7 * hh + 5)
                dve.wait_ge(r_z, 1)
                dve.tensor_tensor(vs[32:32 + NS, :], ax[3][0:NS, :], vs[0:NS, :].bitcast(F32), ALU.subtract).then_inc(r_vl, 1)
                if not first:
                    for q in range(4):
                        finish_gate(hh - 1, q)

                def g_tile(q):
                    taken(m0 + 8 + q, (M_OI + q) % 2, two(tmp[q]))

                def probs(j):
                    dve.wait_ge(r_sc, 4 * hh + j + 1)
                    dve.wait_ge(r_d, 16 * (hh + 1))
                    n = NP_ - P * j
                    at_ = sum(NP_ - P * i for i in range(j))
                    dve.tensor_tensor(prob[:, at_:at_ + n], ax[j % 2][:, 0:n], dec[:, 0:n], ALU.mult).then_inc(r_p, 1)

                g_tile(0)
                probs(0)
                probs(1)
                new_state(hh, 0)
                q_sum(hh, 0)
                g_tile(1)
                chunk(4)
                probs(2)
                probs(3)
                sum_lo(hh, 0)
                new_state(hh, 1)
                q_sum(hh, 1)
                g_tile(2)
                sum_lo(hh, 1)
                new_state(hh, 2)
                q_sum(hh, 2)
                g_tile(3)
                chunk(5)
                for b in range(2, 7):
                    sum_lo(hh, b)
                    new_state(hh, b + 1)
                    if b < 6:
                        q_sum(hh, b + 1)

            head(0)
            with dve.Fori(1, HEADS) as hh:
                head(hh)
            q_sum(HEADS - 1, 7)
            sum_lo(HEADS - 1, 7)

            def out_lo(n):
                k = OO_ORDER[n]
                dve.wait_ge(s_ohi, n + 1)
                dve.tensor_tensor(o_lo[:, k, :], o32[:, k, :], o_hi[:, k, :].bitcast(F32), ALU.subtract).then_inc(s_olo, 1)

            for n in range(12):
                out_lo(n)
            finish_invert(HEADS - 1)
            for q in range(4):
                finish_gate(HEADS - 1, q)
            for n in range(12, 16):
                out_lo(n)
            with dve.Fori(0, N_OO // 2) as i:
                for j in range(2):
                    n = 2 * i + j
                    residual(M_OO + n, (M_OO + j) % 2, n)
                    h_lo(3, n)
                    lo(C_OO + n + 2, j, W_FULL)
            ffn(1)
            invert(4)
            dve.wait_ge(s_rstd, 5)
            for m in range(KT):
                dve.scalar_tensor_tensor(out=x[:, m, :], in0=x[:, m, :], scalar=gain(4, m), in1=rstd[:], op0=ALU.mult,
                                         op1=ALU.mult).then_inc(s_y, 1)

        @block.gpsimd
        def _(pool):
            pool.memset(eps[:], EPS).then_inc(s_eps, 1)

            def squares(n, m, ready):
                pool.wait_ge(*ready)
                if m == 0:
                    if n:
                        pool.wait_ge(s_ms, n)
                    pool.tensor_tensor(acc[:], x[:, m, :], x[:, m, :], ALU.mult).then_inc(s_acc, 1)
                else:
                    pool.wait_ge(s_acc, 8 * n + m)
                    pool.tensor_tensor(sq[:], x[:, m, :], x[:, m, :], ALU.mult).then_inc(s_sq, 1)
                    pool.wait_ge(s_sq, 7 * n + m)
                    pool.tensor_tensor(acc[:], acc[:], sq[:], ALU.add).then_inc(s_acc, 1)

            for m in range(KT):
                squares(0, m, (s_x[m // 2], 16))
            for q in range(HEADS):
                pool.wait_ge(s_atc, q + 1)
                pool.affine_select(out=att[:, q], in_=att[:, q], compare_op=ALU.is_ge, fill=0.0, base=0,
                                   pattern=[[0, BLK], [1, P]], channel_multiplier=-1).then_inc(s_am, 1)
                pool.wait_ge(s_am, 2 * q + 1)
                pool.memset(att[0:CH, q, :, CH:P], 0.0).then_inc(s_am, 1)
            pool.wait_ge(s_dn, 2 * NS)
            pool.dma_start(io["gla_s"], gs[:]).then_inc(s_es, 16)
            pool.wait_ge(s_st, 2 * NCH)
            pool.dma_start(io["gla_p"], states[:, :, NCH - 1, :]).then_inc(s_es, 16)
            pool.wait_ge(s_rows, 4)
            pool.dma_start(io["rows"], pout[:]).then_inc(s_es, 16)
            pool.wait_ge(s_mm, E_AT["p3"] + 1)
            for q in range(HEADS):
                pool.wait_ge(s_oc, q + 1)
                pool.wait_ge(s_odc, 1)
                if q >= 2:
                    pool.wait_ge(s_oms, q - 1)
                pool.tensor_tensor((sq, acc)[q % 2][:], ev[:, q, :], ev[:, q, :], ALU.mult).then_inc(s_osq, 1)
            pool.wait_ge(s_oms, 4)
            for n, m0 in ((1, M_EO), (2, M_D[0])):
                for m in range(KT):
                    squares(n, m, (s_out, m0 + m + 1))

            def dec_load(hh, b):
                pool.dma_start(sring[:, b % 4, :, :].rearrange("p t n -> p (t n)"),
                               io["ret_in"][ds(4 * b + hh, 1)].rearrange("a p n -> p (a n)")).then_inc(r_in[b % 4], 16)

            def finish_squares(hp):
                pool.wait_ge(r_osc, hp + 1)
                for q in range(4):
                    dst = acc if q == 0 else sq
                    src = flat(o32, 4 * hp + q)
                    if q:
                        pool.wait_ge(r_acc, 4 * hp + q)
                    pool.tensor_tensor(dst[:], src, src, ALU.mult).then_inc(r_sq if q else r_acc, 1)
                    if q:
                        pool.wait_ge(r_sq, 3 * hp + q)
                        pool.tensor_tensor(acc[:], acc[:], sq[:], ALU.add).then_inc(r_acc, 1)

            def head(hh, last=False):
                first = isinstance(hh, int) and hh == 0
                if not first:
                    finish_squares(hh - 1)
                for b in range(NS):
                    pool.wait_ge(r_sn, 8 * hh + b + 1)
                    pool.sem_inc(s_pstep, 1)
                    pool.dma_start(io["ret_s"][ds(4 * b + hh, 1)].rearrange("a p n -> p (a n)"),
                                   sring[:, b % 4, :, :].rearrange("p t n -> p (t n)")).then_inc(r_so[b % 4], 16)
                    if b + 3 < NS or not last:
                        if b or not first:
                            pool.wait_ge(r_so[(b + 3) % 4], 16 * (2 * hh + (b + 3) // 4))
                            pool.wait_ge(r_qs, 8 * hh + b)
                            pool.sem_inc(s_pstep, 1)
                        dec_load(hh + (b + 3) // NS, (b + 3) % NS)
                    if b == 1 and not last:
                        pool.wait_ge(r_p, 4 * hh + 4)
                        pool.sem_inc(s_pstep, 1)
                        pool.dma_start(dec[:], io["dec"][ds(hh + 1, 1)].rearrange("a p n -> p (a n)")).then_inc(r_d, 16)
                pool.wait_ge(r_stc, 2 * hh + 2)
                pool.sem_inc(s_pstep, 1)
                pool.dma_start(io["ret_p"][ds(hh, 1)].rearrange("a p n -> p (a n)"),
                               rst[:].rearrange("p t n -> p (t n)")).then_inc(r_sto, 16)

            pool.wait_ge(s_mm, M_OI)
            pool.memset(vs[:].bitcast(F32), 0.0).then_inc(r_z, 1)
            pool.dma_start(dec[:], io["dec"][0]).then_inc(r_d, 16)
            for b in range(3):
                dec_load(0, b)
            pool.wait_ge(s_ms, 3)
            head(0)
            with pool.Fori(1, HEADS - 1) as hh:
                head(hh)
            head(HEADS - 1, last=True)
            finish_squares(HEADS - 1)
            pool.wait_ge(r_ms, 4)
            for n, m0 in ((3, M_OO), (4, M_D[1])):
                for m in range(KT):
                    squares(n, m, (s_out, m0 + m + 1))

        @block.tensor
        def _(pe):
            def product(m, par, ks_, lhs, rhs, first, last, before=None, after=None, count=True):
                if first:
                    want(pe, s_out, m - 1)
                for n, (kw, kx) in enumerate(ks_):
                    if before:
                        before(kx)
                    for q, (a, b) in enumerate(((0, 0), (0, 1), (1, 0))):
                        for t in range(2):
                            ins = pe.matmul(ps[par][:, t, 0:HT], lhs(a, kw), rhs[b][:, kx, HT * t:HT * t + HT],
                                            start=(first and n == 0 and q == 0), stop=(last and n == len(ks_) - 1 and q == 2))
                    if after:
                        after(n)
                if count:
                    ins.then_inc(s_mm if last else s_half, 1)

            def weights(slot, col, cols, rows=None):
                def lhs(a, k):
                    return (whi, wlo)[a][slot][:, k * cols + col:k * cols + col + P]
                return lhs

            KS = [(k, k) for k in range(KT)]

            def mean_square(src, col, sem_):
                for i, (a, _, _) in enumerate(BLOCKS):
                    ins = pe.matmul(ax[3][:, col + i:col + i + 1], src[:, a:a + P], ones[:, 0:1], start=True, stop=True)
                ins.then_inc(sem_, 1)

            def spread_blocks(bank, col, rcol, blocks):
                for i in blocks:
                    a, c, n = BLOCKS[i]
                    dst = ax[bank][:, a:a + P] if i < BLK else ax[3][:, col:col + NS]
                    ins = pe.matmul(dst, rr[:, rcol + i:rcol + i + 1].to_broadcast([P, P]), ident[:, c:c + n],
                                    start=True, stop=True)
                return ins

            def spread(bank, col, rcol, sem_):
                spread_blocks(bank, col, rcol, range(BLK + 1)).then_inc(sem_, 1)

            def norm_sum(n):
                pe.wait_ge(s_acc, 8 * n + 8)
                if n == 0:
                    pe.wait_ge(s_ones, 16)
                    pe.wait_ge(s_id, 16)
                mean_square(acc, 64, s_ms)

            def norm_spread(n):
                pe.wait_ge(s_rr, n + 1)
                spread(2, 72, 0, s_bc)

            pe.wait_ge(s_wal, 1)

            def h_ready(n):
                return lambda k: pe.wait_ge(s_hlo, 8 * n + k + 1)

            def wa(a, k):
                return (wa_hi, wa_lo)[a][:, k * P:k * P + P]

            def e_tile(name):
                m = E_AT[name]
                if name == "a":
                    product(m, m % 2, KS, wa, h, True, True, before=h_ready(0))
                elif name[0] == "z":
                    i = int(name[1])
                    want(pe, s_out, m - 1)
                    if i == 0:
                        pe.wait_ge(s_wgb, 16)
                        pe.wait_ge(s_out, 1)
                    for t in range(2):
                        ins = pe.matmul(ps[m % 2][:, t, 0:HT], wgb[:, P * i:P * i + P], a16[:, HT * t:HT * t + HT],
                                        start=True, stop=True)
                    ins.then_inc(s_mm, 1)
                elif name[0] == "p":
                    g = int(name[1])
                    want(pe, s_out, m - 1)
                    if g == 0:
                        pe.wait_ge(s_poolw, 16)
                    pe.wait_ge(s_pm, g + 1)
                    src = (rs, acc)[g % 2]
                    for t in range(2):
                        ins = pe.matmul(ps[m % 2][:, t, 0:HT], poolw[:, g, :], src[:, HT * t:HT * t + HT],
                                        start=True, stop=True)
                    ins.then_inc(s_mm, 1)
                else:
                    i = E_TILES.index(name)
                    c = i // 2
                    pe.wait_ge(s_wlo, c + 1)
                    product(m, m % 2, KS, weights(c % 2, P * (i % 2), 256), h, True, True)

            def gla_turn_v():
                for b in range(BLK):
                    pe.wait_ge(s_out, E_AT["v3"] + 1)
                    if b == 3:
                        pe.wait_ge(s_rstd, 1)
                    for q in range(4):
                        ins = pe.transpose(ax[b][:, P * q:P * q + P], ev[:, q, P * b:P * b + P], ident[:])
                    ins.then_inc(s_vt, 1)

            def gla_att():
                pe.wait_ge(s_qe, 2)
                pe.wait_ge(s_ke, 1)
                for q in range(HEADS):
                    pe.wait_ge(s_vtc, q + 1)
                    r = 64 * (q % 2)
                    for b in range(BLK):
                        ins = pe.matmul(ax[q][:, P * b:P * b + P], ke[r:r + 64, q // 2, P * b:P * b + P],
                                        eq[r:r + 64, q // 2, P * b:P * b + P], start=True, stop=True)
                    ins.then_inc(s_at, 1)

            def gla_turn_k():
                pe.wait_ge(s_kd, 1)
                for q in range(2):
                    pe.wait_ge(s_atc, q + 1)
                    for b in range(2):
                        for i in range(2):
                            ins = pe.transpose(ax[q][:, 256 * b + P * i:256 * b + P * i + P],
                                               ek[:, i, P * (2 * q + b):P * (2 * q + b) + P], ident[:])
                    ins.then_inc(s_kt, 1)
                pe.wait_ge(s_atc, 3)
                for q in range(4):
                    ins = pe.transpose(ax[2][0:NS, P * q:P * q + P], ev[:, q, NP_:T], ident[:])
                ins.then_inc(s_kt, 1)

            def gla_spread_v():
                pe.wait_ge(s_ktc, 3)
                pe.wait_ge(s_atc, 4)
                pe.wait_ge(s_gsd, 1)
                for b in range(NS):
                    for r in range(2):
                        v = evs[:].rearrange("p (i r n) -> p i r n", i=2, r=2)[:, :, r, :]
                        ins = pe.matmul(ax[b // 2][64 * r:64 * r + 64, 256 * (b % 2):256 * (b % 2) + 256],
                                        ident[0:NS, b:b + 1].to_broadcast([NS, 64]), v, start=True, stop=True)
                    if b % 2:
                        ins.then_inc(s_vb, 1)

            def gla_chunk_kv():
                pe.wait_ge(s_dn, 2 * NS)
                for i in range(2):
                    for par in range(2):
                        rows = slice(64 * par, 64 * par + 64)
                        for b in range(BLK):
                            for r in range(2):
                                q = 2 * i + r
                                ins = pe.matmul(ax[2 * i + par][64 * r:64 * r + 64, P * b:P * b + P],
                                                kdtok[rows, b, 64 * q:64 * q + 64], evtok[rows, b, P * q:P * q + P],
                                                start=True, stop=True)
                        ins.then_inc(s_u, 1)

            def gla_out():
                pe.wait_ge(s_st, 2 * NCH)
                for q in range(HEADS):
                    pe.wait_ge(s_am, 2 * q + 2)
                    r = 64 * (q % 2)
                    for b in range(BLK):
                        pe.matmul(ax[q][:, P * b:P * b + P], evtok[:, b, P * q:P * q + P], att[:, q, b, :],
                                  start=(b == 0), stop=False, skip_group_check=True)
                    for c in range(1, NCH):
                        ins = pe.matmul(ax[q][:, CH * c:CH * c + CH], states[r:r + 64, q // 2, c - 1, :],
                                        eq[r:r + 64, q // 2, CH * c:CH * c + CH], start=False, stop=(c == NCH - 1),
                                        skip_group_check=True)
                    ins.then_inc(s_o, 1)

            def gla_dec_out():
                for r in range(2):
                    pe.wait_ge(s_oc, r + 1)
                    for i in range(2):
                        for b in range(NS):
                            ins = pe.matmul(ax[r][:, NS * i + b:NS * i + b + 1], gs[64 * r:64 * r + 64, i, b, :],
                                            eq[64 * r:64 * r + 64, i, NP_ + b:NP_ + b + 1], start=True, stop=True)
                ins.then_inc(s_od, 1)

            for name in E_ORDER:
                e_tile(name)
                if name == "a":
                    norm_sum(0)
                if name == "q0":
                    norm_spread(0)
                if name == "u0":
                    gla_turn_v()
                if name == "u1":
                    gla_att()
                if name == "u2":
                    gla_turn_k()
                if name == "u3":
                    gla_spread_v()
                if name == "g0":
                    gla_chunk_kv()
                if name == AFTER_O:
                    gla_out()
                if name == AFTER_OD:
                    gla_dec_out()
            for q in range(HEADS):
                pe.wait_ge(s_oc, 4)
                pe.wait_ge(s_osq, q + 1)
                mean_square((sq, acc)[q % 2], 64 + 5 * q, s_oms)
            pe.wait_ge(s_orr, 1)
            pe.wait_ge(s_odc, 1)
            for q in range(HEADS):
                spread_blocks(3, 96 + 8 * q, 5 * q, [BLK])
            for q in range(HEADS):
                if q == 3:
                    pe.wait_ge(s_on, 1)
                spread_blocks(q % 3, 0, 5 * q, range(BLK)).then_inc(s_obc, 1)
            EO_KS = [(k, k) for k in (4, 5, 6, 7, 0, 1, 2, 3)]
            for n in range(N_EO):
                pe.wait_ge(s_wlo, C_EO + n + 1)
                for j in range(2):
                    m = M_EO + 2 * n + j
                    product(m, m % 2, EO_KS, weights(n % 2, P * j, 256), (op_hi, op_lo), True, True,
                            before=(lambda k: pe.wait_ge(s_oplo, (k - 4 if k >= 4 else k + 4) + 1)) if n + j == 0 else None)

            def norm_inside(n):
                def after(k):
                    if k == 4:
                        norm_sum(n)
                    if k == KT - 1:
                        norm_spread(n)
                return after

            def ffn(l):
                c0, m0, d0, dm = C_F[l], M_F[l], C_D[l], M_D[l]

                def pair(i, first=False):
                    for j in range(2):
                        n = 2 * i + j
                        pe.wait_ge(s_wlo, c0 + n + 1)
                        for u in range(2):
                            start = first and j == 0 and u == 0
                            product(m0 + 2 * n + u, (m0 + u) % 2, KS, weights(j, P * u, 256), h, True, True,
                                    before=h_ready(1 + 2 * l) if start else None,
                                    after=norm_inside(1 + 2 * l) if start else None)

                pair(0, first=True)
                with pe.Fori(1, N_F // 2) as i:
                    pair(i)

                def hid_ready(k):
                    if k >= FT - 4:
                        pe.wait_ge(s_hidlo, FT * l + k + 1)

                with pe.Fori(0, KT // 2) as i:
                    for u in range(2):
                        m = 2 * i + u
                        for half in range(2):
                            pe.wait_ge(s_wlo, d0 + 2 * m + half + 1)
                            product(dm + m, (dm + u) % 2, [(k, 11 * half + k) for k in range(11)], weights(half, 0, P),
                                    (hid_hi, hid_lo), half == 0, half == 1, before=hid_ready if u == 0 else None)

            ffn(0)

            def dec_out(hh, b):
                if b == 0:
                    pe.wait_ge(r_vl, hh + 1)
                    if isinstance(hh, int) and hh == 0:
                        pe.wait_ge(r_sel, 3)
                pe.wait_ge(r_tl, 8 * hh + b + 1)
                for part in (th, tl):
                    ins = pe.matmul(ax[3][:], osel[:, NS - 1 - b:NS - 1 - b + P], part[:], start=(b == 0 and part is th),
                                    stop=(b == NS - 1 and part is tl))
                ins.then_inc(r_os, 1)

            def turn_out(hp):
                pe.wait_ge(r_osr, hp + 1)
                pe.sem_inc(s_tstep, 1)
                for d in range(4):
                    ins = pe.transpose(ax[3][:, NS * d:NS * d + NS], acc[0:NS, P * d:P * d + P], ident[0:NS, 0:NS])
                ins.then_inc(r_ot, 1)

            def finish_sum(hp):
                pe.wait_ge(r_acc, 4 * hp + 4)
                mean_square(acc, 64, r_ms)

            def finish_spread(hp):
                pe.wait_ge(r_rr, hp + 1)
                spread(2, 72, 0, r_bc)

            def head(hh):
                m0 = M_OI + 12 * hh
                first = isinstance(hh, int) and hh == 0

                def tile_(t):
                    if t % 2 == 0:
                        pe.wait_ge(s_wlo, C_OI + 6 * hh + t // 2 + 1)
                    start = first and t == 0
                    product(m0 + t, (M_OI + t) % 2, KS, weights((t // 2) % 2, P * (t % 2), 256), h, True, True,
                            before=h_ready(2) if start else None, after=norm_inside(2) if start else None)

                def turn_v(b):
                    if b < 2:
                        if not first:
                            pe.wait_ge(r_stc, 2 * hh - 1 + b)
                    else:
                        pe.wait_ge(r_trc, 7 * hh + b - 1)
                    pe.wait_ge(s_out, m0 + 4)
                    for q in range(4):
                        ins = pe.transpose(ax[b % 2][:, P * q:P * q + P], rv[:, q, P * b:P * b + P], ident[:])
                    ins.then_inc(r_tr, 1)

                def turn_vs():
                    if not first:
                        pe.wait_ge(r_rc, hh)
                    for q in range(4):
                        ins = pe.transpose(ax[3][0:NS, P * q:P * q + P], rv[:, q, NP_:T], ident[:])
                    ins.then_inc(r_tr, 1)

                def scores(j):
                    pe.wait_ge(r_rot, 4 * hh + 4)
                    pe.wait_ge(*((r_trc, 7 * hh + 3 + j) if j < 2 else (r_p, 4 * hh + j - 1)))
                    for t in range(2):
                        ins = pe.matmul(ax[j % 2][:, 0:NP_ - P * j], rk[:, t, P * j:P * j + P], rq[:, t, P * j:NP_],
                                        start=(t == 0), stop=(t == 1))
                    ins.then_inc(r_sc, 1)

                def turn_k(q):
                    pe.wait_ge(r_p, 4 * hh + 3 + q)
                    for b in range(2):
                        for i in range(2):
                            ins = pe.transpose(ax[q][:, 256 * b + P * i:256 * b + P * i + P],
                                               rk[:, i, P * (2 * q + b):P * (2 * q + b) + P], ident[:])
                    ins.then_inc(r_tr, 1)

                def pv(q):
                    pe.wait_ge(*((r_trc, 7 * hh + 6 + q) if q < 2 else (r_pvc, 4 * hh + q - 1)))
                    at_ = 0
                    for j in range(BLK):
                        n = NP_ - P * j
                        ins = pe.matmul(ax[q % 2][:, P * j:NP_], vtok[:, j, P * q:P * q + P], prob[:, at_:at_ + n],
                                        start=(j == 0), stop=(j == BLK - 1))
                        at_ += n
                    ins.then_inc(r_pv, 1)

                def state(q):
                    pe.wait_ge(r_pvc, 4 * hh + 3 + q)
                    for j in range(BLK):
                        ins = pe.matmul(ax[q][:], ktok[:, j, P * q:P * q + P], vtok[:, j, :], start=(j == 0), stop=(j == BLK - 1))
                    ins.then_inc(r_st, 1)

                def spread_v(b):
                    want(pe, r_sn, 8 * hh + b)
                    if b == 0:
                        pe.wait_ge(r_vl, hh + 1)
                        if first:
                            pe.wait_ge(r_sel, 3)
                            pe.wait_ge(s_rstd, 3)
                    pe.matmul(ax[2][:], vsel[0:64, b:b + 1].to_broadcast([64, P]), vs[:], start=True, stop=True).then_inc(r_vb, 1)

                tile_(0)
                if not first:
                    dec_out(hh - 1, 6)
                tile_(1)
                if not first:
                    dec_out(hh - 1, 7)
                tile_(2)
                if not first:
                    turn_out(hh - 1)
                tile_(3)
                tile_(4)
                turn_v(0)
                turn_v(1)
                tile_(5)
                turn_v(2)
                turn_v(3)
                if not first:
                    finish_sum(hh - 1)
                tile_(6)
                if not first:
                    finish_spread(hh - 1)
                tile_(7)
                turn_vs()
                tile_(8)
                scores(0)
                scores(1)
                spread_v(0)
                tile_(9)
                scores(2)
                scores(3)
                spread_v(1)
                tile_(10)
                turn_k(0)
                turn_k(1)
                dec_out(hh, 0)
                spread_v(2)
                tile_(11)
                dec_out(hh, 1)
                spread_v(3)
                pv(0)
                pv(1)
                dec_out(hh, 2)
                spread_v(4)
                pv(2)
                pv(3)
                dec_out(hh, 3)
                spread_v(5)
                state(0)
                dec_out(hh, 4)
                spread_v(6)
                state(1)
                dec_out(hh, 5)
                spread_v(7)

            head(0)
            with pe.Fori(1, HEADS) as hh:
                head(hh)

            last = HEADS - 1

            def out_part(n, a, b, after=None):
                if a == 0:
                    pe.wait_ge(s_wlo, C_OO + n + 1)
                product(M_OO + n, (M_OO + n) % 2, [(k, k) for k in OO_ORDER[a:b]], weights(n % 2, 0, P), (o_hi, o_lo),
                        a == 0, b == 16, before=(lambda k: pe.wait_ge(s_olo, OO_ORDER.index(k) + 1)) if n == 0 else None,
                        after=after, count=b == 16)

            dec_out(last, 6)
            out_part(0, 0, 12, lambda n: {3: lambda: dec_out(last, 7),
                                          9: lambda: turn_out(last)}.get(n, lambda: None)())
            out_part(1, 0, 12)
            finish_sum(last)
            finish_spread(last)
            out_part(0, 12, 16)
            out_part(1, 12, 16)
            with pe.Fori(1, N_OO // 2) as i:
                for j in range(2):
                    n = 2 * i + j
                    pe.wait_ge(s_wlo, C_OO + n + 1)
                    product(M_OO + n, (M_OO + j) % 2, [(k, k) for k in OO_ORDER], weights(j, 0, P), (o_hi, o_lo), True,
                            True)
            ffn(1)
            norm_sum(4)
            norm_spread(4)


def columns(w, n):
    k = w.shape[0] // P
    return w.reshape(k, P, -1, n).transpose(2, 1, 0, 3).reshape(-1, P, k * n)


def down_chunks(w):
    return w.reshape(2, 11, P, KT, P).transpose(3, 0, 2, 1, 4).reshape(N_D, P, W_DOWN)


def gate_up(gate, up):
    g, u = (m.reshape(KT, P, FT, P) for m in (gate, up))
    return np.stack([g, u], axis=3).transpose(2, 1, 0, 3, 4).reshape(FT, P, W_FULL)


def tables():
    f = np.float32
    angle = (1.0 / (f(10000.0) ** np.linspace(0.0, 1.0, P, dtype=f))).astype(f)
    pos = np.concatenate([np.arange(NP_), np.full(NS, 4096)]).astype(f)
    ang = (angle[:, None] * pos[None, :]).astype(f).astype(np.float64)
    cs = np.stack([np.cos(ang), np.sin(ang)], axis=1).astype(f)
    gamma = 1.0 - 2.0 ** (-5.0 - np.arange(HEADS))
    s, t = np.arange(P)[:, None], np.arange(NP_)[None, :]
    dec = np.stack([np.where(t >= s, g ** np.maximum(t - s, 0).astype(np.float64), 0.0) / 16 for g in gamma]).astype(f)
    kscale = np.stack([g ** (NP_ - 1.0 - P * b - np.arange(P)) / 16 for g in gamma for b in range(BLK)], axis=1)
    gm = np.tile(gamma[None, :], (P, 1))
    reset = np.ones((P, NP_), f)
    reset[:, ::CH] = 0
    inv = np.stack([1.0 / np.minimum(2 << g, np.arange(16) + 1.0) for g in range(4)])
    return dict(cs=cs, dec=dec, kscale=kscale.astype(f), gm=gm.astype(f), reset=reset,
                invc=np.tile(inv[None], (P, 1, 1)).astype(f), ident=np.eye(P, dtype=f),
                ones=np.concatenate([np.full((P, 1), 1.0 / DM), np.ones((P, 7)),
                                     (np.arange(P)[:, None] % 32 == np.arange(8)) & (np.arange(P)[:, None] < 64)],
                                    axis=1).astype(f))


def kernel(**inputs):
    import concourse.bacc as bacc
    from concourse.bass_utils import run_bass_kernel_spmd

    v = {k: np.asarray(a) for k, a in inputs.items()}
    c = tables()
    tiles = lambda a: a.reshape(-1, P).T
    we, wo = v["w_in_even"][0], v["w_in_odd"][0]
    cols = []
    for hh in range(HEADS):
        q, k = hh * 256, 1024 + hh * 256
        cols += [np.arange(2048 + 512 * hh, 2560 + 512 * hh)]
        cols += [np.arange(s + e, s + 256, 2) for s in (q, k) for e in (0, 1)]
        cols += [np.arange(4096 + 512 * hh, 4608 + 512 * hh)]
    arrays = dict(
        x=np.concatenate([v["x_prompt"][0], v["x_sample"][:, 0]]).T.reshape(KT, P, T).transpose(1, 0, 2),
        vec=np.concatenate([tiles(v["norm_mix"][0]), tiles(v["norm_ffn"][0]), tiles(v["norm_mix"][1]),
                            tiles(v["norm_ffn"][1]), tiles(v["norm_final"]), tiles(v["gla_gain"][0]),
                            tiles(v["pool_scale"][0]), tiles(v["b_gate"][0]), c["kscale"], c["gm"]], axis=1),
        w_a=np.pad(we[:, 1536:1552], ((0, 0), (0, P - 16))).reshape(KT, P, P).transpose(1, 0, 2).reshape(P, KT * P),
        w_e=columns(np.concatenate([we[:, 0:1024], we[:, 1552:2064], we[:, 1024:1536]], axis=1), 256),
        w_eo=columns(v["w_out_even"][0], 256),
        w_f0=gate_up(v["w_ffn_gate"][0], v["w_ffn_up"][0]), w_d0=down_chunks(v["w_ffn_down"][0]),
        w_oi=columns(wo[:, np.concatenate(cols)], 256), w_oo=columns(v["w_out_odd"][0], P),
        w_f1=gate_up(v["w_ffn_gate"][1], v["w_ffn_up"][1]), w_d1=down_chunks(v["w_ffn_down"][1]),
        wgb=v["w_gate_b"][0], poolw=v["pool_w"][0].transpose(1, 0, 2),
        gs=v["state_gla"][0].reshape(NS, 2, P, P).transpose(2, 1, 0, 3),
        pbuf=v["state_pool"][0].reshape(NS, 15, 4, P).transpose(3, 2, 0, 1),
        ret_in=v["state_ret"][0].reshape(NS * HEADS, P, 1024),
        cs=c["cs"], dec=c["dec"], reset=c["reset"], invc=c["invc"], ident=c["ident"], ones=c["ones"])
    outs = dict(y=(P, KT, T), gla_p=(P, 2, P), gla_s=(P, 2, NS, P), rows=(P, 4, NS + 1, 15),
                ret_p=(HEADS, P, 1024), ret_s=(NS * HEADS, P, 1024))
    nc = bacc.Bacc("TRN2", target_bir_lowering=False, num_devices=1)
    arrays = {"in_" + n: np.ascontiguousarray(a) for n, a in arrays.items()}
    io = {n[3:]: nc.dram_tensor(n, a.shape, F32, kind="ExternalInput").ap() for n, a in arrays.items()}
    io.update({n: nc.dram_tensor("out_" + n, s, F32, kind="ExternalOutput").ap() for n, s in outs.items()})
    build(nc, io)
    r = run_bass_kernel_spmd(nc, [arrays], core_ids=[0]).results[0]
    y = r["out_y"].transpose(2, 1, 0).reshape(T, DM)
    rows = r["out_rows"].transpose(2, 3, 1, 0).reshape(NS + 1, 15, 512)
    return (y[None, :NP_], y[NP_:, None],
            r["out_gla_p"].transpose(1, 0, 2).reshape(1, 1, HEADS, 64, P),
            r["out_gla_s"].transpose(2, 1, 0, 3).reshape(1, NS, HEADS, 64, P),
            rows[None, NS:], rows[None, :NS],
            r["out_ret_p"].reshape(1, 1, HEADS, 256, 512),
            r["out_ret_s"].reshape(1, NS, HEADS, 256, 512))
```

```python
from contextlib import ExitStack

import numpy as np

import concourse.bass as bass
from concourse import mybir

F32 = mybir.dt.float32
F32R = mybir.dt.float32r
ACT = mybir.ActivationFunctionType
ALU = mybir.AluOpType
ds = bass.ds

P = 128
DM, KT = 1024, 8
NP_, NS, T = 512, 8, 520
HT = T // 2
BLK = NP_ // P
FT = 22
CH = 64
NCH = NP_ // CH
W_FULL, W_DOWN = 2048, 11 * P
HEADS = 4
EPS = 1e-6

N_E, N_EO, N_F, N_D, N_OI, N_OO = 8, 4, FT, 16, 24, 8
C_E = 0
C_EO = C_E + N_E
C_F = [C_EO + N_EO, 0]
C_D = [C_F[0] + N_F, 0]
C_OI = C_D[0] + N_D
C_OO = C_OI + N_OI
C_F[1] = C_OO + N_OO
C_D[1] = C_F[1] + N_F
E_ORDER = ["a", "q0", "q1", "k0", "z0", "k1", "z1", "v0", "v1", "v2", "v3", "u0", "u1", "p0", "u2", "p1",
           "u3", "g0", "p2", "g1", "p3", "g2", "g3"]
E_AT = {n: i for i, n in enumerate(E_ORDER)}
E_TILES = ["q0", "q1", "k0", "k1", "v0", "v1", "v2", "v3", "u0", "u1", "u2", "u3", "g0", "g1", "g2", "g3"]
M_EO = len(E_ORDER)
M_F = [M_EO + 8, 0]
M_D = [M_F[0] + 2 * FT, 0]
M_OI = M_D[0] + 8
M_OO = M_OI + 48
M_F[1] = M_OO + 8
M_D[1] = M_F[1] + 2 * FT
OO_ORDER = [8, 9, 10, 11, 4, 5, 0, 1, 2, 3, 6, 7, 12, 13, 14, 15]
Y_DVE, Y_POOL, Y_ORDER = (0, 1, 2, 3, 4, 7), (5, 6), (0, 1, 5, 2, 3, 6, 4, 7)
NORM_0_AFTER, GLA_SUM_AFTER, GLA_SPREAD_AFTER = 4, 6, (3, 6)
AFTER_O = "g1"
V_GAIN, V_GLA, V_PS, V_BG, V_KS, V_GM, V_N = 0, 40, 41, 45, 47, 63, 67


def build(nc, io):
    at = nc.alloc_sbuf_tensor_at
    cursor = [16544]

    def fixed(name, shape, dt):
        t = at(name, shape, dt, offset=cursor[0])
        cursor[0] += (int(np.prod(shape[1:])) * 4 + 31) // 32 * 32
        return t

    TB = T * 4
    raw = [fixed(f"raw{i}", [P, W_FULL], F32) for i in range(2)]
    whi = [fixed(f"whi{i}", [P, W_FULL], F32R) for i in range(2)]
    wlo = [fixed(f"wlo{i}", [P, W_FULL], F32R) for i in range(2)]
    x = fixed("x", [P, KT, T], F32)
    h = [fixed("h_hi", [P, KT, T], F32R), fixed("h_lo", [P, KT, T], F32R)]
    rstd, acc, sq, rs, t0, t1, t2, t3 = [fixed(n, [P, T], F32)
                                         for n in ("rstd", "acc", "sq", "rs", "t0", "t1", "t2", "t3")]
    tmp = [t0, t1, t2, t3]
    osq = [sq, t0, rs, acc]
    qbuf = [sq, acc]
    RS_OFF = cursor[0] - 5 * ((TB + 31) // 32 * 32)
    ident = fixed("ident", [P, P], F32)
    ones = fixed("ones", [P, 16], F32)
    vec = fixed("vec", [P, V_N], F32)
    eps = fixed("eps", [P, 8], F32)
    rt = fixed("rt", [P, 20], F32)
    rr = fixed("rr", [P, 20], F32)
    R, TOP = cursor[0], 229344

    def region(name, shape, dt, off):
        size = int(np.prod(shape[1:])) * 4
        assert R + off + size <= TOP, (name, R + off + size - TOP)
        return at(name, shape, dt, offset=R + off), off + size

    hid_hi, o = region("hid_hi", [P, FT, T], F32R, 0)
    hid_lo, o = region("hid_lo", [P, FT, T], F32R, o)
    eq, o = region("eq", [P, 2, T], F32, 0)
    ek, o = region("ek", [P, 2, T], F32, o)
    eb, o2 = region("eb", [P, 2, T], F32, o)
    et, o3 = region("et", [P, 2, T], F32, o2)
    states, _ = region("states", [P, 2, NCH, P], F32, o)
    ex, o = region("ex", [P, 2, T], F32, o3)
    kdtok, _ = region("kdtok", [P, BLK, 256], F32, o3)
    ke, o = region("ke", [P, 2, T], F32, o)
    ev, op_off = region("ev", [P, 4, T], F32, o)
    op_hi, o = region("op_hi", [P, KT, T], F32R, op_off)
    gsil, _ = region("gsil", [P, 4, T], F32, o)
    op_lo, end = region("op_lo", [P, KT, T], F32R, o)
    pbuf, o = region("pbuf", [P, 4, NS, 15], F32, op_off)
    wa_raw, o2 = region("wa_raw", [P, KT * P], F32, o)
    evs, _ = region("evs", [NS, 512], F32, o)
    wa_hi, o = region("wa_hi", [P, KT * P], F32R, o2)
    wa_lo, o = region("wa_lo", [P, KT * P], F32R, o)
    reset, o = region("reset", [P, NP_], F32, o)
    wgb, o = region("wgb", [16, 256], F32, o)
    a16, o = region("a16", [16, T], F32, o)
    assert o <= end
    att, o = region("att", [P, 4, BLK, P], F32, end)
    evtok, o = region("evtok", [P, BLK, 512], F32, o)
    gs, o = region("gs", [P, 2, NS, P], F32, o)
    poolw, o = region("poolw", [P, 4, P], F32, o)
    elast, o = region("elast", [P, 2, NCH], F32, o)
    eas, o = region("eas", [P, 2, NS], F32, o)
    invc, o = region("invc", [P, 4, 16], F32, o)
    qmask, o = region("qmask", [P, 2, NS, 2], F32, o)
    pout, o = region("pout", [P, 4, NS + 1, 15], F32, o)
    o32, oh = region("o32", [P, 16, T], F32, 0)
    o_lo, _ = region("o_lo", [P, 16, T], F32R, 0)
    o_hi, _ = region("o_hi", [P, 16, T], F32R, oh)
    rq, o = region("rq", [P, 2, T], F32, oh)
    rst, _ = region("rst", [P, 2, 512], F32, o)
    rk, o = region("rk", [P, 2, T], F32, o)
    PROB_OFF = o
    prob, _ = region("prob", [P, 1280], F32, o)
    rv, o = region("rv", [P, 4, T], F32, o)
    vtok, o = region("vtok", [P, BLK, 512], F32, o)
    ktok, o = region("ktok", [P, BLK, 256], F32, o)
    rg, o = region("rg", [P, 4, T], F32, o)
    dec, o = region("dec", [P, NP_], F32, o)
    cs, o = region("cs", [P, 2, T], F32, o)
    sring, o = region("sring", [P, 4, 2, 512], F32, o)
    vs, o = region("vs", [64, 512], F32R, o)
    ks, o = region("ks", [P, 2, NS], F32, o)
    qs, o = region("qs", [P, 2, NS], F32, o)
    vsel, o = region("vsel", [P, NS], F32R, o)
    osel, o = region("osel", [P, P + NS], F32R, o)
    TAIL = 5632
    assert TAIL >= 1280 * 4 and TAIL + 2048 <= 4 * TB
    th, _ = region("th", [P, 512], F32R, PROB_OFF + TAIL)
    tl = at("tl", [P, 512], F32R, offset=RS_OFF)

    with ExitStack() as ctx:
        def sem(name):
            return ctx.enter_context(nc.semaphore(name))

        ps = [ctx.enter_context(nc.psum_tensor(f"ps{i}", [P, 2, 512], F32)) for i in range(2)]
        ax = [ctx.enter_context(nc.psum_tensor(f"ax{i}", [P, 512], F32)) for i in range(4)]
        s_raw = [sem("raw0_loaded"), sem("raw1_loaded")]
        s_whi, s_wlo = sem("weights_hi"), sem("weights_lo")
        s_mm, s_out, s_half = sem("mtile_done"), sem("mtile_taken"), sem("half_mtile_done")
        s_x = [sem(f"x{i}_loaded") for i in range(4)]
        s_vec, s_ones, s_id, s_wa = sem("vec_loaded"), sem("ones_loaded"), sem("ident_loaded"), sem("wa_loaded")
        s_reset, s_wgb, s_gsl, s_poolw, s_pbuf, s_invc = [sem(n + "_loaded") for n in
                                                         ("reset", "wgb", "gs", "poolw", "pbuf", "invc")]
        s_eps, s_qz, s_qm = sem("eps_set"), sem("gla_dec_q_zeroed"), sem("gla_dec_q_masked")
        s_hhi, s_hlo = sem("h_hi_written"), sem("h_lo_written")
        s_sq, s_acc = sem("x_squared"), sem("squares_summed")
        s_ms, s_rt, s_rr, s_bc, s_rstd = (sem("mean_square"), sem("rms"), sem("rms_inverted"),
                                          sem("rstd_spread"), sem("rstd_written"))
        s_sg, s_hid, s_hidhi, s_hidlo = sem("silu_gate"), sem("hidden"), sem("hidden_hi"), sem("hidden_lo")
        s_wah, s_wal, s_z1, s_sp, s_la, s_b, s_eb, s_enb = [sem(n) for n in (
            "wa_hi_written", "wa_lo_written", "z_written", "softplus_step", "log_decay", "decay_summed",
            "decay_exp", "decay_exp_inv")]
        s_qe, s_ke, s_dl, s_edl, s_kd, s_gsd = [sem(n) for n in (
            "q_decayed", "k_decayed", "decay_to_end", "decay_to_end_exp", "k_decayed_to_end", "gla_dec_decayed")]
        s_vt, s_vtc, s_at, s_atc, s_am = [sem(n) for n in (
            "gla_v_turned", "gla_v_taken", "gla_att", "gla_att_taken", "gla_att_masked")]
        s_kt, s_ktc, s_vb, s_dn, s_u, s_st = [sem(n) for n in (
            "gla_kv_turned", "gla_kv_taken", "gla_v_spread", "gla_dec_state", "gla_chunk_kv", "gla_states")]
        s_o, s_oc, s_od, s_odc, s_osq = [sem(n) for n in (
            "gla_o", "gla_o_taken", "gla_dec_o", "gla_dec_o_taken", "gla_o_squared")]
        s_oms, s_ort, s_orr, s_obc, s_on = [sem(n) for n in (
            "gla_ms", "gla_rms", "gla_rms_inverted", "gla_rstd_spread", "gla_o_normed")]
        s_gs, s_og, s_ophi, s_oplo = sem("gla_silu"), sem("gla_gated"), sem("op_hi_written"), sem("op_lo_written")
        s_pl, s_pm, s_rows = sem("pool_step"), sem("pooled"), sem("pool_rows_written")
        s_es = sem("even_stores")
        r_cs, r_csr, r_d = sem("ret_tables_loaded"), sem("ret_tables_scaled"), sem("ret_decay_loaded")
        r_rp, r_rot, r_ks = sem("ret_rope_products"), sem("ret_rotated"), sem("ret_dec_k")
        r_tr, r_trc, r_sc, r_p = sem("ret_turned"), sem("ret_turned_taken"), sem("ret_scores"), sem("ret_probs")
        r_pv, r_pvc, r_st, r_stc, r_sto = [sem(n) for n in (
            "ret_pv", "ret_pv_taken", "ret_state", "ret_state_taken", "ret_state_stored")]
        r_in = [sem(f"ret_dec_in{i}") for i in range(4)]
        r_so = [sem(f"ret_dec_stored{i}") for i in range(4)]
        r_g, r_vb, r_sn, r_os, r_osc = [sem(n) for n in (
            "ret_dec_decayed", "ret_v_spread", "ret_dec_state", "ret_dec_o", "ret_dec_o_taken")]
        r_z = sem("ret_dec_v_zeroed")
        r_vl, r_sel, r_ta, r_qs, r_th, r_tl, r_osr, r_ot, r_rc = [sem(n) for n in (
            "ret_dec_v_lo", "ret_selectors", "ret_dec_q0", "ret_dec_qsum", "ret_dec_sum_hi", "ret_dec_sum_lo",
            "ret_dec_o_rows", "ret_dec_o_turned", "ret_rstd_copied")]
        r_sq, r_acc, r_ms, r_rt, r_rr, r_bc = [sem(n) for n in (
            "ret_o_squared", "ret_squares", "ret_ms", "ret_rms", "ret_rms_inverted", "ret_rstd_spread")]
        r_sg, r_on, r_gd = sem("ret_silu"), sem("ret_normed"), sem("ret_gated")
        s_ohi, s_olo = sem("o_hi_written"), sem("o_lo_written")
        s_sql, s_xg = sem("last_x_squared"), sem("x_gained")
        s_y, s_yp, s_yst = sem("y_written"), sem("y_written_by_gpsimd"), sem("y_stored")
        s_astep, s_pstep, s_tstep = sem("scalar_step"), sem("gpsimd_step"), sem("tensor_step")
        block = ctx.enter_context(nc.Block())

        def halves(t, i):
            return t[:, ds(i, 1), :].rearrange("p a (b n) -> p (a b) n", b=2)

        def flat(t, i):
            return t[:, ds(i, 1), :].rearrange("p a n -> p (a n)")

        def two(t):
            return t[:].rearrange("p (b n) -> p b n", b=2)

        def mt(m):
            return ps[m % 2][:, :, 0:HT]

        def want(eng, s, v):
            if not isinstance(v, int) or v > 0:
                eng.wait_ge(s, v)

        def gain(n, m):
            return vec[:, ds(V_GAIN + 8 * n + m, 1)]

        BLOCKS = [(0, 0, P), (P, 0, P), (2 * P, 0, P), (3 * P, 0, P), (T - P, P - NS, NS)]

        @block.sync
        def _(sp):
            def load(c, slot, src, idx, n):
                if not isinstance(c, int) or c >= 2:
                    sp.wait_ge(s_whi, c - 1)
                    sp.wait_ge(s_wlo, c - 1)
                sp.dma_start(raw[slot][:, 0:n],
                             src[ds(idx, 1)].rearrange("a p n -> p (a n)")).then_inc(s_raw[slot], 16)

            def phase(c0, n, src, size, first=0):
                with sp.Fori(first // 2, n // 2) as i:
                    for j in range(2):
                        load(c0 + 2 * i + j, j, src, 2 * i + j, size)

            sp.dma_start(vec[:], io["vec"]).then_inc(s_vec, 16)
            sp.dma_start(wa_raw[:], io["w_a"]).then_inc(s_wa, 16)
            for q in range(4):
                sp.dma_start(x[:, 2 * q:2 * q + 2, :], io["x"][:, 2 * q:2 * q + 2, :]).then_inc(s_x[q], 16)
            for c in range(2):
                load(c, c, io["w_e"], c, W_FULL)
            for dst, name, s in ((ones, "ones", s_ones), (ident, "ident", s_id), (reset, "reset", s_reset),
                                 (wgb, "wgb", s_wgb), (gs, "gs", s_gsl), (poolw, "poolw", s_poolw),
                                 (pbuf, "pbuf", s_pbuf), (invc, "invc", s_invc)):
                sp.dma_start(dst[:], io[name]).then_inc(s, 16)
            phase(C_E, N_E, io["w_e"], W_FULL, 2)
            phase(C_EO, N_EO, io["w_eo"], W_FULL)
            phase(C_F[0], N_F, io["w_f0"], W_FULL)
            phase(C_D[0], N_D, io["w_d0"], W_DOWN)
            for j in range(2):
                load(C_OI + j, j, io["w_oi"], j, W_FULL)
            sp.wait_ge(s_mm, M_OI)
            sp.dma_start(cs[:], io["cs"]).then_inc(r_cs, 16)
            phase(C_OI, N_OI, io["w_oi"], W_FULL, 2)
            phase(C_OO, N_OO, io["w_oo"], W_FULL)
            phase(C_F[1], N_F, io["w_f1"], W_FULL)
            phase(C_D[1], N_D, io["w_d1"], W_DOWN)
            for m in Y_ORDER:
                sp.wait_ge(*((s_yp, Y_POOL.index(m) + 1) if m in Y_POOL else (s_y, Y_DVE.index(m) + 1)))
                sp.dma_start(io["y"][:, m, :], x[:, m, :]).then_inc(s_yst, 16)
            sp.wait_ge(s_yst, 16 * KT)
            sp.wait_ge(s_es, 16 * 3)
            sp.wait_ge(r_sto, 16 * HEADS)
            for q in range(4):
                sp.wait_ge(r_so[q], 16 * HEADS * NS // 4)

        @block.scalar
        def _(act):
            def hi(c, slot, size, used):
                act.wait_ge(s_raw[slot], 8 * (c - slot) + 16)
                if used is not None:
                    act.wait_ge(*used)
                act.activation(whi[slot][:, 0:size], raw[slot][:, 0:size], ACT.Copy).then_inc(s_whi, 1)

            def settled():
                act.sem_inc(s_astep, 1)

            def h_hi(n, m, ready):
                act.wait_ge(*ready)
                settled()
                act.activation(flat(h[0], m), flat(x, m), ACT.Copy, scale=gain(n, m)).then_inc(s_hhi, 1)

            def root(n):
                act.wait_ge(s_ms, n + 1)
                act.activation(rt[:, 0:5], ax[3][:, 64:69], ACT.Sqrt, bias=eps[:, 0:1]).then_inc(s_rt, 1)
                act.wait_ge(s_bc, n + 1)
                act.activation(rstd[:, 0:NP_], ax[2][:], ACT.Copy)
                act.activation(rstd[:, NP_:T], ax[3][:, 72:72 + NS], ACT.Copy).then_inc(s_rstd, 1)

            act.wait_ge(s_wa, 16)
            act.activation(wa_hi[:], wa_raw[:], ACT.Copy).then_inc(s_wah, 1)
            act.wait_ge(s_vec, 16)
            for m in range(KT):
                h_hi(0, m, (s_x[m // 2], 16))
            for c in range(2):
                hi(c, c, W_FULL, None)
            act.wait_ge(s_eps, 1)
            act.activation(t1[:, 0:8], eps[:], ACT.Sqrt)
            root(0)

            def e_hi(n):
                hi(n + 2, n % 2, W_FULL, (s_mm, E_AT[E_TILES[2 * n + 1]] + 1))

            e_hi(0)
            e_hi(1)
            act.wait_ge(s_z1, 2)
            act.activation(et[:], ex[:], ACT.Abs).then_inc(s_sp, 1)
            act.wait_ge(s_sp, 1)
            act.activation(et[:], et[:], ACT.Exp, scale=-1.0).then_inc(s_sp, 1)
            act.wait_ge(s_sp, 2)
            act.activation(et[:], et[:], ACT.Ln, bias=1.0).then_inc(s_sp, 1)
            e_hi(2)
            act.wait_ge(s_b, 3)
            act.activation(eb[:], et[:], ACT.Exp, scale=1.0 / 16).then_inc(s_eb, 1)
            act.activation(ex[:], et[:], ACT.Exp, scale=-1.0 / 16).then_inc(s_enb, 1)
            act.wait_ge(s_dl, 2)
            act.activation(ex[:, :, 0:NP_], ex[:, :, 0:NP_], ACT.Exp, scale=1.0 / 16).then_inc(s_edl, 1)
            e_hi(3)
            for b in range(BLK):
                act.wait_ge(s_vt, b + 1)
                act.activation(evtok[:, b, :], ax[b][:], ACT.Copy).then_inc(s_vtc, 1)
            e_hi(4)

            def silu_g(q):
                act.wait_ge(s_out, E_AT[f"g{q}"] + 1)
                act.activation(gsil[:, q, :], gsil[:, q, :], ACT.Silu).then_inc(s_gs, 1)

            def pool_hi(q):
                act.wait_ge(s_mm, E_AT[f"p{q}"] + 1)
                act.activation(halves(op_hi, 4 + q), mt(E_AT[f"p{q}"]), ACT.Copy,
                               scale=vec[:, V_PS + q:V_PS + q + 1]).then_inc(s_ophi, 1)

            for q in range(4):
                act.wait_ge(s_at, q + 1)
                act.activation(att[:, q].rearrange("p b n -> p (b n)"), ax[q][:], ACT.Copy).then_inc(s_atc, 1)
            for q in range(2):
                act.wait_ge(s_kt, q + 1)
                act.activation(kdtok[:, 2 * q:2 * q + 2, :].rearrange("p b n -> p (b n)"), ax[q][:],
                               ACT.Copy).then_inc(s_ktc, 1)
                if q == 0:
                    pool_hi(0)
            act.wait_ge(s_kt, 3)
            act.activation(evs[:], ax[2][0:NS, :], ACT.Copy).then_inc(s_ktc, 1)
            pool_hi(1)
            e_hi(5)

            silu_g(0)
            pool_hi(2)
            silu_g(1)
            e_hi(6)
            for k in range(HEADS):
                act.wait_ge(s_o, k + 1)
                act.activation(ev[:, k, 0:NP_], ax[k][:], ACT.Copy).then_inc(s_oc, 1)
            act.wait_ge(s_od, 1)
            for i in range(2):
                a = act.activation(ev[:, 2 * i:2 * i + 2, NP_:T],
                                   ax[0][:, 16 * i:16 * i + 16].rearrange("p (b r) -> p r b", r=2), ACT.Copy)
            a.then_inc(s_odc, 1)
            pool_hi(3)
            act.wait_ge(s_oms, 4)
            act.activation(rt[:], ax[3][:, 64:84], ACT.Sqrt, bias=eps[:, 0:1], scale=8.0).then_inc(s_ort, 1)
            silu_g(2)

            def head_hi(q):
                act.wait_ge(s_og, q + 1)
                act.activation(op_hi[:, q, :], tmp[q][:], ACT.Copy).then_inc(s_ophi, 1)

            for q in range(3):
                head_hi(q)
            silu_g(3)
            head_hi(3)
            e_hi(7)
            for n in range(N_EO):
                for j in range(2):
                    h_hi(1, 2 * n + j, (s_out, M_EO + 2 * n + j + 1))
                hi(C_EO + n + 2, n % 2, W_FULL, (s_mm, M_EO + 2 * n + 2))

            def ffn(l):
                c0, m0, d0, dm = C_F[l], M_F[l], C_D[l], M_D[l]
                nrm = 1 + 2 * l

                def pair(i, size, first=False):
                    for j in range(2):
                        n = 2 * i + j
                        g = FT * l + n
                        if first and j == 0:
                            root(1 + 2 * l)
                        act.wait_ge(s_out, m0 + 2 * n + 1)
                        want(act, s_hid, g)
                        act.activation(t1[:], t0[:], ACT.Silu).then_inc(s_sg, 1)
                        hi(c0 + n + 2, j, size, (s_mm, m0 + 2 * n + 2))
                        act.wait_ge(s_hid, g + 1)
                        settled()
                        act.activation(flat(hid_hi, n), t3[:], ACT.Copy).then_inc(s_hidhi, 1)

                pair(0, W_FULL, first=True)
                with act.Fori(1, N_F // 2 - 1) as i:
                    pair(i, W_FULL)
                pair(N_F // 2 - 1, W_DOWN)

                def down(m, size):
                    if size:
                        hi(d0 + 2 * m + 2, 0, size, (s_half, KT * l + m + 1))
                    if l == 0:
                        h_hi(2, m, (s_out, dm + m + 1))
                    if size:
                        hi(d0 + 2 * m + 3, 1, size, (s_mm, dm + m + 1))

                with act.Fori(0, KT - 1) as m:
                    down(m, W_DOWN)
                down(KT - 1, W_FULL if l == 0 else 0)

            ffn(0)

            act.wait_ge(s_mm, M_OI)
            act.activation(vsel[:], ones[:, 8:16], ACT.Copy).then_inc(r_sel, 1)
            act.wait_ge(s_out, M_OI)
            act.activation(osel[:], rstd[:, 0:P + NS], ACT.Copy, scale=0.0).then_inc(r_sel, 1)
            act.wait_ge(r_sel, 2)
            act.activation(osel[:, NS - 1:NS], ones[:, 1:2], ACT.Copy).then_inc(r_sel, 1)

            def finish_rows(hp):
                act.wait_ge(r_sg, 4 * hp + 4)
                act.wait_ge(r_os, 8 * hp + 8)
                act.activation(t2[0:NS, 0:512], ax[3][0:NS, :], ACT.Copy).then_inc(r_osr, 1)

            def finish_turned(hp):
                act.wait_ge(r_ot, hp + 1)
                settled()
                act.activation(o32[:, ds(4 * hp, 4), NP_:T], ax[3][:, 0:32].rearrange("p (d b) -> p d b", d=4),
                               ACT.Copy).then_inc(r_osc, 1)

            def finish_root(hp):
                act.wait_ge(r_ms, hp + 1)
                act.activation(rt[:, 0:5], ax[3][:, 64:69], ACT.Sqrt, bias=eps[:, 0:1], scale=2.0).then_inc(r_rt, 1)

            def finish_copy(hp):
                act.wait_ge(r_bc, hp + 1)
                act.activation(rs[:, 0:NP_], ax[2][:], ACT.Copy)
                act.activation(rs[:, NP_:T], ax[3][:, 72:72 + NS], ACT.Copy).then_inc(r_rc, 1)

            def decay(hh, b):
                n = 8 * hh + b
                act.wait_ge(r_in[b % 4], 16 * (2 * hh + b // 4 + 1))
                settled()
                act.activation(sring[:, b % 4].rearrange("p t n -> p (t n)"), sring[:, b % 4].rearrange("p t n -> p (t n)"),
                               ACT.Copy, scale=vec[:, ds(V_GM + hh, 1)]).then_inc(r_g, 1)

            def q_first(hh, b):
                act.wait_ge(r_sn, 8 * hh + b + 1)
                act.activation(qbuf[b % 2][:, 0:512], sring[:, b % 4, 0, :], ACT.Copy, scale=qs[:, 0, b:b + 1]).then_inc(r_ta, 1)

            def sum_hi(hh, b):
                want(act, r_os, 8 * hh + b)
                act.wait_ge(r_qs, 8 * hh + b + 1)
                act.activation(th[:], qbuf[b % 2][:, 0:512], ACT.Copy).then_inc(r_th, 1)

            def head(hh):
                m0 = M_OI + 12 * hh
                first = isinstance(hh, int) and hh == 0

                def chunk(n):
                    hi(C_OI + 6 * hh + n + 2, n % 2, W_FULL, (s_mm, m0 + 2 * n + 2))

                if first:
                    root(2)
                else:
                    q_first(hh - 1, 7)
                    sum_hi(hh - 1, 7)
                chunk(0)
                if not first:
                    finish_rows(hh - 1)
                    finish_turned(hh - 1)
                chunk(1)
                if not first:
                    finish_root(hh - 1)
                for b in range(BLK):
                    act.wait_ge(r_tr, 7 * hh + b + 1)
                    act.activation(vtok[:, b, :], ax[b % 2][:], ACT.Copy).then_inc(r_trc, 1)
                    if b == 1:
                        chunk(2)
                    if b == 0 and not first:
                        finish_copy(hh - 1)
                chunk(3)
                act.wait_ge(r_tr, 7 * hh + 5)
                if first:
                    act.wait_ge(r_z, 1)
                act.activation(vs[0:NS, :], ax[3][0:NS, :], ACT.Copy).then_inc(r_trc, 1)
                decay(hh, 0)
                decay(hh, 1)

                def silu(q):
                    act.wait_ge(s_out, m0 + 8 + q + 1)
                    if not first:
                        act.wait_ge(r_gd, 4 * hh)
                    act.activation(rg[:, q, :], tmp[q][:], ACT.Silu).then_inc(r_sg, 1)

                silu(0)
                decay(hh, 2)
                q_first(hh, 0)
                silu(1)
                sum_hi(hh, 0)
                decay(hh, 3)
                q_first(hh, 1)
                chunk(4)
                for q in range(2):
                    act.wait_ge(r_tr, 7 * hh + 6 + q)
                    settled()
                    for b in range(2):
                        a = act.activation(ktok[:, 2 * q + b, :], ax[q][:, 256 * b:256 * b + 256], ACT.Copy,
                                           scale=vec[:, ds(V_KS + 4 * hh + 2 * q + b, 1)])
                    a.then_inc(r_trc, 1)
                sum_hi(hh, 1)
                silu(2)
                q_first(hh, 2)
                silu(3)
                sum_hi(hh, 2)
                q_first(hh, 3)
                decay(hh, 4)

                def pv(q):
                    act.wait_ge(r_pv, 4 * hh + q + 1)
                    settled()
                    act.activation(o32[:, ds(4 * hh + q, 1), 0:NP_].rearrange("p a n -> p (a n)"), ax[q % 2][:],
                                   ACT.Copy).then_inc(r_pvc, 1)

                def state(q):
                    act.wait_ge(r_st, 2 * hh + q + 1)
                    act.activation(rst[:, q, :], ax[q][:], ACT.Copy).then_inc(r_stc, 1)

                pv(0)
                pv(1)
                chunk(5)
                sum_hi(hh, 3)
                q_first(hh, 4)
                decay(hh, 5)
                pv(2)
                pv(3)
                sum_hi(hh, 4)
                q_first(hh, 5)
                decay(hh, 6)
                state(0)
                sum_hi(hh, 5)
                q_first(hh, 6)
                decay(hh, 7)
                state(1)
                sum_hi(hh, 6)

            head(0)
            with act.Fori(1, HEADS) as hh:
                head(hh)

            def out_hi(n):
                k = OO_ORDER[n]
                act.activation(o_hi[:, k, :], o32[:, k, :], ACT.Copy).then_inc(s_ohi, 1)

            out_hi(0)
            q_first(HEADS - 1, 7)
            out_hi(1)
            sum_hi(HEADS - 1, 7)
            out_hi(2)
            out_hi(3)
            finish_rows(HEADS - 1)
            out_hi(4)
            out_hi(5)
            finish_turned(HEADS - 1)
            out_hi(6)
            out_hi(7)
            finish_root(HEADS - 1)
            act.wait_ge(r_sto, 16 * HEADS)
            for n in range(8, 12):
                out_hi(n)
            finish_copy(HEADS - 1)
            for q in range(4):
                act.wait_ge(r_on, 4 * (HEADS - 1) + q + 1)
                out_hi(12 + q)
            with act.Fori(0, N_OO // 2) as i:
                for j in range(2):
                    n = 2 * i + j
                    h_hi(3, n, (s_out, M_OO + n + 1))
                    hi(C_OO + n + 2, j, W_FULL, (s_mm, M_OO + n + 1))
            ffn(1)
            act.activation(t1[:, 0:8], eps[:], ACT.Sqrt)
            for m in Y_POOL:
                act.wait_ge(s_acc, 8 * 4 + m + 1)
                act.activation(x[:, m, :], x[:, m, :], ACT.Copy, scale=gain(4, m)).then_inc(s_xg, 1)
            root(4)

        @block.vector
        def _(dve):
            def lo(c, slot, size):
                dve.wait_ge(s_whi, c + 1)
                dve.tensor_tensor(wlo[slot][:, 0:size], raw[slot][:, 0:size], whi[slot][:, 0:size].bitcast(F32),
                                  ALU.subtract).then_inc(s_wlo, 1)

            def h_lo(n, m):
                dve.wait_ge(s_hhi, 8 * n + m + 1)
                dve.scalar_tensor_tensor(out=flat(h[1], m), in0=flat(x, m), scalar=gain(n, m),
                                         in1=flat(h[0], m).bitcast(F32), op0=ALU.mult,
                                         op1=ALU.subtract).then_inc(s_hlo, 1)

            def invert(n):
                dve.wait_ge(s_rt, n + 1)
                dve.reciprocal(rr[:, 0:5], rt[:, 0:5]).then_inc(s_rr, 1)

            def taken(m, par, out, other=None, op=ALU.mult):
                dve.wait_ge(s_mm, m + 1)
                dve.tensor_tensor(out, ps[par][:, :, 0:HT], two(rstd) if other is None else other, op).then_inc(s_out, 1)

            dve.wait_ge(s_wah, 1)
            dve.tensor_tensor(wa_lo[:], wa_raw[:], wa_hi[:].bitcast(F32), ALU.subtract).then_inc(s_wal, 1)
            dve.wait_ge(s_vec, 16)
            for m in range(KT):
                h_lo(0, m)
            for c in range(2):
                lo(c, c, W_FULL)
            invert(0)
            dve.wait_ge(s_rstd, 1)
            steps = {n: [] for n in E_ORDER}

            def e_take(name, out):
                i = E_AT[name]
                taken(i, i % 2, out)

            def z_tile(i):
                m = E_AT[f"z{i}"]
                dve.wait_ge(s_mm, m + 1)
                dve.tensor_scalar(halves(ex, i), mt(m), vec[:, V_BG + i:V_BG + i + 1], None, ALU.add).then_inc(s_out, 1)
                dve.wait_ge(s_out, m + 1)
                dve.sem_inc(s_z1, 1)

            i = E_AT["a"]
            dve.wait_ge(s_mm, i + 1)
            for t in range(2):
                a = dve.tensor_tensor(a16[:, HT * t:HT * t + HT], ax[t][0:16, 0:HT], rstd[0:16, HT * t:HT * t + HT], ALU.mult)
            a.then_inc(s_out, 1)
            e_take("q0", halves(eq, 0))
            e_take("q1", halves(eq, 1))
            lo(2, 0, W_FULL)
            e_take("k0", halves(ek, 0))
            z_tile(0)
            e_take("k1", halves(ek, 1))
            lo(3, 1, W_FULL)
            z_tile(1)
            e_take("v0", halves(ev, 0))
            dve.wait_ge(s_sp, 3)
            dve.scalar_tensor_tensor(out=eb[:], in0=ex[:], scalar=0.0, in1=et[:], op0=ALU.min,
                                     op1=ALU.subtract).then_inc(s_la, 1)
            dve.wait_ge(s_la, 1)
            dve.wait_ge(s_reset, 16)
            for i in range(2):
                dve.tensor_tensor_scan(et[:, i, 0:NP_], reset[:], eb[:, i, 0:NP_], 0.0, ALU.mult, ALU.add).then_inc(s_b, 1)
            dve.tensor_copy(et[:, :, NP_:T], eb[:, :, NP_:T]).then_inc(s_b, 1)
            e_take("v1", halves(ev, 1))
            lo(4, 0, W_FULL)
            dve.wait_ge(s_eb, 1)
            dve.scalar_tensor_tensor(out=eq[:, :, 0:NP_], in0=eq[:, :, 0:NP_], scalar=0.125, in1=eb[:, :, 0:NP_],
                                     op0=ALU.mult, op1=ALU.mult).then_inc(s_qe, 1)
            dve.tensor_scalar(eq[:, :, NP_:T], eq[:, :, NP_:T], 0.125, None, ALU.mult).then_inc(s_qe, 1)
            dve.wait_ge(s_qz, 1)
            dve.wait_ge(s_qe, 2)
            for r in range(2):
                half = slice(CH * r, CH * r + CH)
                a = dve.tensor_copy(qmask[half, :, :, r], eq[half, :, NP_:T])
            a.then_inc(s_qm, 1)
            dve.tensor_copy(elast[:], eb[:, :, CH - 1:NP_:CH]).then_inc(s_qe, 1)
            dve.tensor_copy(eas[:], eb[:, :, NP_:T]).then_inc(s_qe, 1)
            dve.wait_ge(s_enb, 1)
            dve.tensor_tensor(ke[:, :, 0:NP_], ek[:, :, 0:NP_], ex[:, :, 0:NP_], ALU.mult).then_inc(s_ke, 1)
            dve.wait_ge(s_ke, 1)
            for i in range(2):
                dve.tensor_tensor(ex[:, i, 0:NP_].rearrange("p (c n) -> p c n", n=CH),
                                  et[:, i, CH - 1:NP_:CH].unsqueeze(2).to_broadcast([P, NCH, CH]),
                                  et[:, i, 0:NP_].rearrange("p (c n) -> p c n", n=CH), ALU.subtract).then_inc(s_dl, 1)
            e_take("v2", halves(ev, 2))
            dve.wait_ge(s_edl, 1)
            dve.tensor_tensor(ek[:, :, 0:NP_], ek[:, :, 0:NP_], ex[:, :, 0:NP_], ALU.mult).then_inc(s_kd, 1)
            dve.wait_ge(s_gsl, 16)
            dve.wait_ge(s_qe, 4)
            dve.tensor_tensor(gs[:].rearrange("p i b n -> p (i b) n"), gs[:].rearrange("p i b n -> p (i b) n"),
                              eas[:].rearrange("p i b -> p (i b)").unsqueeze(2).to_broadcast([P, 2 * NS, P]),
                              ALU.mult).then_inc(s_gsd, 1)
            e_take("v3", halves(ev, 3))
            lo(5, 1, W_FULL)

            pools = [0]

            def step(ins):
                pools[0] += 1
                ins.then_inc(s_pl, 1)
                dve.wait_ge(s_pl, pools[0])

            def pool_group(g):
                u, wdw = tmp[g % 2], 2 << g
                pooled = (rs, acc)[g % 2]
                dve.wait_ge(s_out, E_AT[f"u{g}"] + 1)
                if g == 0:
                    dve.wait_ge(s_pbuf, 16)
                    dve.wait_ge(s_invc, 16)
                if g >= 2:
                    dve.wait_ge(s_mm, E_AT[f"p{g - 2}"] + 1)
                dve.tensor_copy(pout[:, g, NS, :], u[:, NP_ - 15:NP_])
                dve.tensor_copy(pout[:, g, 0:NS, 14:15].rearrange("p b n -> p (b n)"), u[:, NP_:T])
                dve.tensor_copy(pout[:, g, 0:NS, 0:14], pbuf[:, g, :, 1:15]).then_inc(s_rows, 1)
                cur = u
                for lv in range(g + 1):
                    d, nxt = 1 << lv, (t2, t3)[lv % 2]
                    dve.tensor_copy(nxt[:, 0:d], cur[:, 0:d])
                    step(dve.tensor_tensor(nxt[:, d:NP_], cur[:, d:NP_], cur[:, 0:NP_ - d], ALU.add))
                    cur = nxt
                dve.scalar_tensor_tensor(out=pooled[:, 16:NP_], in0=cur[:, 16:NP_], scalar=1.0 / wdw, in1=u[:, 16:NP_],
                                         op0=ALU.mult, op1=ALU.subtract)
                step(dve.tensor_tensor(cur[:, 0:16], cur[:, 0:16], invc[:, g, :], ALU.mult))
                dve.tensor_tensor(pooled[:, 0:16], cur[:, 0:16], u[:, 0:16], ALU.subtract)
                step(dve.tensor_reduce(cur[:, 16:24], pbuf[:, g, :, 16 - wdw:15], mybir.AxisListType.X, ALU.add))
                step(dve.tensor_tensor(cur[:, 16:24], cur[:, 16:24], u[:, NP_:T], ALU.add))
                dve.scalar_tensor_tensor(out=pooled[:, NP_:T], in0=cur[:, 16:24], scalar=1.0 / wdw, in1=u[:, NP_:T],
                                         op0=ALU.mult, op1=ALU.subtract).then_inc(s_pm, 1)

            def pool_lo(q):
                dve.wait_ge(s_ophi, q + 1)
                m = E_AT[f"p{q}"]
                dve.scalar_tensor_tensor(out=halves(op_lo, 4 + q), in0=mt(m), scalar=vec[:, V_PS + q:V_PS + q + 1],
                                         in1=halves(op_hi, 4 + q).bitcast(F32), op0=ALU.mult, op1=ALU.subtract)\
                   .then_inc(s_out, 1)
                dve.wait_ge(s_out, m + 1)
                dve.sem_inc(s_oplo, 1)

            e_take("u0", two(tmp[0]))
            pool_group(0)
            e_take("u1", two(tmp[1]))
            lo(6, 0, W_FULL)
            pool_group(1)
            pool_lo(0)
            e_take("u2", two(tmp[0]))
            pool_group(2)
            pool_lo(1)
            e_take("u3", two(tmp[1]))
            lo(7, 1, W_FULL)
            for b in range(NS):
                dve.wait_ge(s_vb, b // 2 + 1)
                for i in range(2):
                    dve.scalar_tensor_tensor(out=gs[:, i, b, :],
                                             in0=ax[b // 2][:, 256 * (b % 2) + 128 * i:256 * (b % 2) + 128 * i + 128],
                                             scalar=ek[:, i, NP_ + b:NP_ + b + 1], in1=gs[:, i, b, :], op0=ALU.mult,
                                             op1=ALU.add).then_inc(s_dn, 1)
            e_take("g0", halves(gsil, 0))
            dve.wait_ge(s_kd, 1)
            dve.wait_ge(s_u, 4)
            n = 0
            for c in range(NCH):
                for i in range(2):
                    u = ax[2 * i + c % 2][:, 128 * (c // 2):128 * (c // 2) + 128]
                    if c == 0:
                        dve.tensor_copy(states[:, i, 0, :], u).then_inc(s_st, 1)
                    else:
                        dve.wait_ge(s_st, n - 1)
                        dve.scalar_tensor_tensor(out=states[:, i, c, :], in0=states[:, i, c - 1, :],
                                                 scalar=elast[:, i, c:c + 1], in1=u, op0=ALU.mult,
                                                 op1=ALU.add).then_inc(s_st, 1)
                    n += 1
            pool_group(3)

            pool_lo(2)
            e_take("g1", halves(gsil, 1))
            lo(8, 0, W_FULL)
            pool_lo(3)
            dve.wait_ge(s_ort, 1)
            dve.reciprocal(rr[:], rt[:]).then_inc(s_orr, 1)
            e_take("g2", halves(gsil, 2))

            def head_gate(q):
                dve.wait_ge(s_obc, q + 1)
                dve.scalar_tensor_tensor(out=ev[:, q, 0:NP_], in0=ev[:, q, 0:NP_], scalar=vec[:, V_GLA:V_GLA + 1],
                                         in1=ax[q % 3][:], op0=ALU.mult, op1=ALU.mult)
                dve.scalar_tensor_tensor(out=ev[:, q, NP_:T], in0=ev[:, q, NP_:T], scalar=vec[:, V_GLA:V_GLA + 1],
                                         in1=ax[3][:, 96 + 8 * q:104 + 8 * q], op0=ALU.mult, op1=ALU.mult).then_inc(s_on, 1)
                dve.wait_ge(s_on, q + 1)
                dve.wait_ge(s_gs, q + 1)
                dve.tensor_tensor(tmp[q][:], ev[:, q, :], gsil[:, q, :], ALU.mult).then_inc(s_og, 1)

            def head_lo(q):
                dve.wait_ge(s_ophi, 5 + q)
                dve.tensor_tensor(op_lo[:, q, :], tmp[q][:], op_hi[:, q, :].bitcast(F32), ALU.subtract).then_inc(s_oplo, 1)

            head_gate(0)
            head_gate(1)
            head_lo(0)
            head_gate(2)
            head_lo(1)
            e_take("g3", halves(gsil, 3))
            head_lo(2)
            head_gate(3)
            head_lo(3)
            lo(9, 1, W_FULL)

            def residual(m, par, row):
                taken(m, par, halves(x, row), halves(x, row), ALU.add)

            for n in range(N_EO):
                for j in range(2):
                    m = 2 * n + j
                    residual(M_EO + m, (M_EO + m) % 2, m)
                    h_lo(1, m)
                lo(C_EO + n + 2, n % 2, W_FULL)

            def ffn(l):
                c0, m0, d0, dm = C_F[l], M_F[l], C_D[l], M_D[l]

                def pair(i, size, first=False):
                    for j in range(2):
                        n = 2 * i + j
                        g = FT * l + n
                        if first and j == 0:
                            invert(1 + 2 * l)
                            dve.wait_ge(s_rstd, 2 + 2 * l)
                            if l == 0:
                                dve.wait_ge(s_es, 48)
                            else:
                                for q in range(4):
                                    dve.wait_ge(r_so[q], 16 * HEADS * NS // 4)
                        want(dve, s_sg, g)
                        taken(m0 + 2 * n, m0 % 2, two(t0))
                        taken(m0 + 2 * n + 1, (m0 + 1) % 2, two(t2))
                        dve.wait_ge(s_out, m0 + 2 * n + 2)
                        dve.wait_ge(s_sg, g + 1)
                        want(dve, s_hidhi, g)
                        dve.tensor_tensor(t3[:], t2[:], t1[:], ALU.mult).then_inc(s_hid, 1)
                        lo(c0 + n + 2, j, size)
                        dve.wait_ge(s_hidhi, g + 1)
                        dve.tensor_tensor(flat(hid_lo, n), t3[:], flat(hid_hi, n).bitcast(F32),
                                          ALU.subtract).then_inc(s_hidlo, 1)

                pair(0, W_FULL, first=True)
                with dve.Fori(1, N_F // 2 - 1) as i:
                    pair(i, W_FULL)
                pair(N_F // 2 - 1, W_DOWN)

                def down(m, par, size):
                    if size:
                        lo(d0 + 2 * m + 2, 0, size)
                    residual(dm + m, par, m)
                    if l == 0:
                        h_lo(2, m)
                    if size:
                        lo(d0 + 2 * m + 3, 1, size)

                with dve.Fori(0, KT // 2 - 1) as i:
                    for j in range(2):
                        down(2 * i + j, (dm + j) % 2, W_DOWN)
                down(KT - 2, dm % 2, W_DOWN)
                down(KT - 1, (dm + 1) % 2, W_FULL if l == 0 else 0)

            ffn(0)

            def finish_invert(hp):
                dve.wait_ge(r_rt, hp + 1)
                dve.reciprocal(rr[:, 0:5], rt[:, 0:5]).then_inc(r_rr, 1)

            def finish_gate(hp, q):
                o = flat(o32, 4 * hp + q)
                dve.wait_ge(r_acc, 5 * hp + 5)
                dve.wait_ge(r_sg, 4 * hp + q + 1)
                dve.tensor_tensor(o, o, flat(rg, q), ALU.mult).then_inc(r_gd, 1)

            def finish_norm(hp, q):
                o = flat(o32, 4 * hp + q)
                dve.wait_ge(r_rc, hp + 1)
                dve.wait_ge(r_gd, 4 * hp + q + 1)
                dve.tensor_tensor(o, o, rs[:], ALU.mult).then_inc(r_on, 1)

            def new_state(hh, b):
                dve.wait_ge(r_vb, 8 * hh + b + 1)
                dve.wait_ge(r_g, 8 * hh + b + 1)
                dve.wait_ge(r_ks, hh + 1)
                for t in range(2):
                    a = dve.scalar_tensor_tensor(out=sring[:, b % 4, t, :], in0=ax[2][:], scalar=ks[:, t, b:b + 1],
                                                 in1=sring[:, b % 4, t, :], op0=ALU.mult, op1=ALU.add)
                a.then_inc(r_sn, 1)

            def q_sum(hh, b):
                dve.wait_ge(r_ta, 8 * hh + b + 1)
                buf = qbuf[b % 2][:, 0:512]
                dve.scalar_tensor_tensor(out=buf, in0=sring[:, b % 4, 1, :], scalar=qs[:, 1, b:b + 1], in1=buf,
                                         op0=ALU.mult, op1=ALU.add).then_inc(r_qs, 1)

            def sum_lo(hh, b):
                want(dve, r_os, 8 * hh + b)
                dve.wait_ge(r_th, 8 * hh + b + 1)
                dve.tensor_tensor(tl[:], qbuf[b % 2][:, 0:512], th[:].bitcast(F32), ALU.subtract).then_inc(r_tl, 1)

            def head(hh):
                m0 = M_OI + 12 * hh
                first = isinstance(hh, int) and hh == 0

                def chunk(n):
                    lo(C_OI + 6 * hh + n + 2, n % 2, W_FULL)

                if first:
                    invert(2)
                    dve.wait_ge(s_rstd, 3)
                    dve.wait_ge(r_cs, 16)
                    for i in range(2):
                        dve.tensor_tensor(cs[:, i, :], cs[:, i, :], rstd[:], ALU.mult).then_inc(r_csr, 1)
                if not first:
                    q_sum(hh - 1, 7)
                for t in range(4):
                    if t == 2 and not first:
                        dve.wait_ge(r_os, 8 * hh)
                    taken(m0 + t, (M_OI + t) % 2, halves(rv, t))
                    if t == 0 and not first:
                        sum_lo(hh - 1, 7)
                    if t == 1:
                        chunk(0)
                    if t == 3:
                        chunk(1)
                dve.wait_ge(r_csr, 2)
                if not first:
                    finish_invert(hh - 1)

                def rope(t, dst, k):
                    want(dve, r_rot, 4 * hh + 2 * k)
                    want(dve, r_sg, 4 * hh)
                    for u in range(2):
                        dve.wait_ge(s_mm, m0 + t + u + 1)
                        src = ps[(M_OI + t + u) % 2][:, :, 0:HT]
                        dve.tensor_tensor(two(tmp[u]), src, halves(cs, 0), ALU.mult)
                        dve.tensor_tensor(two(tmp[2 + u]), src, halves(cs, 1), ALU.mult).then_inc(s_out, 1)
                    dve.wait_ge(s_out, m0 + t + 2)
                    dve.tensor_tensor(dst[:, 0, :], t0[:], t3[:], ALU.subtract).then_inc(r_rot, 1)
                    dve.tensor_tensor(dst[:, 1, :], t1[:], t2[:], ALU.add).then_inc(r_rot, 1)

                rope(4, rq, 0)
                chunk(2)
                if not first:
                    dve.wait_ge(r_sto, 16 * hh)
                rope(6, rk, 1)
                chunk(3)
                dve.wait_ge(r_rot, 4 * hh + 4)
                dve.tensor_copy(qs[:], rq[:, :, NP_:T])
                dve.tensor_scalar(ks[:], rk[:, :, NP_:T], 1.0 / 16, None, ALU.mult).then_inc(r_ks, 1)
                dve.wait_ge(r_trc, 7 * hh + 5)
                dve.wait_ge(r_z, 1)
                dve.tensor_tensor(vs[32:32 + NS, :], ax[3][0:NS, :], vs[0:NS, :].bitcast(F32), ALU.subtract).then_inc(r_vl, 1)
                if not first:
                    for q in range(4):
                        finish_gate(hh - 1, q)
                    for q in range(4):
                        finish_norm(hh - 1, q)

                def g_tile(q):
                    taken(m0 + 8 + q, (M_OI + q) % 2, two(tmp[q]))

                def probs(j):
                    dve.wait_ge(r_sc, 4 * hh + j + 1)
                    dve.wait_ge(r_d, 16 * (hh + 1))
                    n = NP_ - P * j
                    at_ = sum(NP_ - P * i for i in range(j))
                    dve.tensor_tensor(prob[:, at_:at_ + n], ax[j % 2][:, 0:n], dec[:, 0:n], ALU.mult).then_inc(r_p, 1)

                g_tile(0)
                probs(0)
                probs(1)
                new_state(hh, 0)
                q_sum(hh, 0)

                def sequence(b):
                    new_state(hh, b)
                    sum_lo(hh, b - 1)
                    q_sum(hh, b)

                g_tile(1)
                probs(2)
                probs(3)
                sequence(1)
                chunk(4)
                g_tile(2)
                sequence(2)
                g_tile(3)
                sequence(3)
                new_state(hh, 4)
                chunk(5)
                sum_lo(hh, 3)
                q_sum(hh, 4)
                sequence(5)
                sequence(6)
                new_state(hh, 7)
                sum_lo(hh, 6)

            head(0)
            with dve.Fori(1, HEADS) as hh:
                head(hh)

            def out_lo(n):
                k = OO_ORDER[n]
                dve.wait_ge(s_ohi, n + 1)
                dve.tensor_tensor(o_lo[:, k, :], o32[:, k, :], o_hi[:, k, :].bitcast(F32), ALU.subtract).then_inc(s_olo, 1)

            out_lo(0)
            q_sum(HEADS - 1, 7)
            out_lo(1)
            sum_lo(HEADS - 1, 7)
            for n in range(2, 8):
                out_lo(n)
            for q in range(4):
                finish_gate(HEADS - 1, q)
            finish_invert(HEADS - 1)
            for n in range(8, 12):
                out_lo(n)
            finish_norm(HEADS - 1, 0)
            for q in range(1, 4):
                finish_norm(HEADS - 1, q)
                out_lo(11 + q)
            out_lo(15)
            with dve.Fori(0, N_OO // 2) as i:
                for j in range(2):
                    n = 2 * i + j
                    residual(M_OO + n, (M_OO + j) % 2, n)
                    h_lo(3, n)
                    lo(C_OO + n + 2, j, W_FULL)
            ffn(1)
            dve.wait_ge(s_out, M_D[1] + KT)
            dve.wait_ge(s_acc, 8 * 4 + 7)
            dve.tensor_tensor(sq[:], x[:, KT - 1, :], x[:, KT - 1, :], ALU.mult).then_inc(s_sql, 1)
            invert(4)
            dve.wait_ge(s_rstd, 5)
            for m in Y_DVE:
                dve.scalar_tensor_tensor(out=x[:, m, :], in0=x[:, m, :], scalar=gain(4, m), in1=rstd[:], op0=ALU.mult,
                                         op1=ALU.mult).then_inc(s_y, 1)

        @block.gpsimd
        def _(pool):
            pool.memset(eps[:], EPS).then_inc(s_eps, 1)
            pool.memset(qmask[:], 0.0).then_inc(s_qz, 1)

            def squares(n, m, ready):
                pool.wait_ge(*ready)
                if m == 0:
                    if n:
                        pool.wait_ge(s_ms, n)
                    pool.tensor_tensor(acc[:], x[:, m, :], x[:, m, :], ALU.mult).then_inc(s_acc, 1)
                else:
                    pool.wait_ge(s_acc, 8 * n + m)
                    pool.tensor_tensor(sq[:], x[:, m, :], x[:, m, :], ALU.mult).then_inc(s_sq, 1)
                    pool.wait_ge(s_sq, 7 * n + m)
                    pool.tensor_tensor(acc[:], acc[:], sq[:], ALU.add).then_inc(s_acc, 1)

            for m in range(KT):
                squares(0, m, (s_x[m // 2], 16))
            for q in range(HEADS):
                pool.wait_ge(s_atc, q + 1)
                pool.affine_select(out=att[:, q], in_=att[:, q], compare_op=ALU.is_ge, fill=0.0, base=0,
                                   pattern=[[0, BLK], [1, P]], channel_multiplier=-1).then_inc(s_am, 1)
                pool.wait_ge(s_am, 2 * q + 1)
                pool.memset(att[0:CH, q, :, CH:P], 0.0).then_inc(s_am, 1)
            pool.wait_ge(s_dn, 2 * NS)
            pool.dma_start(io["gla_s"], gs[:]).then_inc(s_es, 16)
            pool.wait_ge(s_st, 2 * NCH)
            pool.dma_start(io["gla_p"], states[:, :, NCH - 1, :]).then_inc(s_es, 16)
            pool.wait_ge(s_rows, 4)
            pool.dma_start(io["rows"], pout[:]).then_inc(s_es, 16)
            pool.wait_ge(s_odc, 1)
            for q in range(HEADS):
                pool.wait_ge(s_oc, q + 1)
                if q == 1:
                    pool.wait_ge(s_pm, 3)
                if q > 1:
                    pool.wait_ge(s_mm, E_AT[f"p{q}"] + 1)
                pool.tensor_tensor(osq[q][:], ev[:, q, :], ev[:, q, :], ALU.mult).then_inc(s_osq, 1)
            pool.wait_ge(s_oms, 4)
            for n, m0 in ((1, M_EO), (2, M_D[0])):
                for m in range(KT):
                    squares(n, m, (s_out, m0 + m + 1))

            def dec_load(hh, b):
                pool.dma_start(sring[:, b % 4, :, :].rearrange("p t n -> p (t n)"),
                               io["ret_in"][ds(4 * b + hh, 1)].rearrange("a p n -> p (a n)")).then_inc(r_in[b % 4], 16)

            def squares_prompt(hh, q):
                src = o32[:, ds(4 * hh + q, 1), 0:NP_].rearrange("p a n -> p (a n)")
                if q == 0:
                    pool.wait_ge(r_sg, 4 * hh + 4)
                else:
                    pool.wait_ge(r_acc, 5 * hh + q)
                pool.wait_ge(r_pvc, 4 * hh + q + 1)
                dst = (t1 if q else t0)[:, 0:NP_]
                pool.tensor_tensor(dst, src, src, ALU.mult).then_inc(r_sq if q else r_acc, 1)
                if q:
                    pool.wait_ge(r_sq, 5 * hh + q)
                    pool.tensor_tensor(t0[:, 0:NP_], t0[:, 0:NP_], t1[:, 0:NP_], ALU.add).then_inc(r_acc, 1)

            def squares_decode(hp):
                pool.wait_ge(r_acc, 5 * hp + 4)
                pool.wait_ge(r_osc, hp + 1)
                src = o32[:, ds(4 * hp, 4), NP_:T]
                pool.tensor_tensor(t1[:, 0:4 * NS].rearrange("p (d b) -> p d b", d=4), src, src, ALU.mult).then_inc(r_sq, 1)
                pool.wait_ge(r_sq, 5 * hp + 4)
                pool.tensor_tensor(t1[:, 4 * NS:6 * NS], t1[:, 0:2 * NS], t1[:, 2 * NS:4 * NS], ALU.add).then_inc(r_sq, 1)
                pool.wait_ge(r_sq, 5 * hp + 5)
                pool.tensor_tensor(t0[:, NP_:T], t1[:, 4 * NS:5 * NS], t1[:, 5 * NS:6 * NS], ALU.add).then_inc(r_acc, 1)

            def head(hh, last=False):
                first = isinstance(hh, int) and hh == 0
                if not first:
                    squares_decode(hh - 1)
                for b in range(NS):
                    pool.wait_ge(r_sn, 8 * hh + b + 1)
                    pool.sem_inc(s_pstep, 1)
                    pool.dma_start(io["ret_s"][ds(4 * b + hh, 1)].rearrange("a p n -> p (a n)"),
                                   sring[:, b % 4, :, :].rearrange("p t n -> p (t n)")).then_inc(r_so[b % 4], 16)
                    if b + 3 < NS or not last:
                        if b or not first:
                            pool.wait_ge(r_so[(b + 3) % 4], 16 * (2 * hh + (b + 3) // 4))
                            pool.wait_ge(r_qs, 8 * hh + b)
                            pool.sem_inc(s_pstep, 1)
                        dec_load(hh + (b + 3) // NS, (b + 3) % NS)
                    if b == 1 and not last:
                        pool.wait_ge(r_p, 4 * hh + 4)
                        pool.sem_inc(s_pstep, 1)
                        pool.dma_start(dec[:], io["dec"][ds(hh + 1, 1)].rearrange("a p n -> p (a n)")).then_inc(r_d, 16)
                    for q in {4: (0, 1), 5: (2,), 6: (3,)}.get(b, ()):
                        squares_prompt(hh, q)
                pool.wait_ge(r_stc, 2 * hh + 2)
                pool.sem_inc(s_pstep, 1)
                pool.dma_start(io["ret_p"][ds(hh, 1)].rearrange("a p n -> p (a n)"),
                               rst[:].rearrange("p t n -> p (t n)")).then_inc(r_sto, 16)

            pool.wait_ge(s_mm, M_OI)
            pool.memset(vs[:].bitcast(F32), 0.0).then_inc(r_z, 1)
            pool.dma_start(dec[:], io["dec"][0]).then_inc(r_d, 16)
            for b in range(3):
                dec_load(0, b)
            pool.wait_ge(s_ms, 3)
            head(0)
            with pool.Fori(1, HEADS - 1) as hh:
                head(hh)
            head(HEADS - 1, last=True)
            squares_decode(HEADS - 1)
            pool.wait_ge(r_ms, 4)
            for n, m0 in ((3, M_OO), (4, M_D[1])):
                for m in range(KT if n == 3 else KT - 1):
                    squares(n, m, (s_out, m0 + m + 1))
            pool.wait_ge(s_xg, len(Y_POOL))
            pool.wait_ge(s_rstd, 5)
            for m in Y_POOL:
                pool.tensor_tensor(x[:, m, :], x[:, m, :], rstd[:], ALU.mult).then_inc(s_yp, 1)

        @block.tensor
        def _(pe):
            def product(m, par, ks_, lhs, rhs, first, last, before=None, after=None, count=True, banks=None):
                dst = banks or [ps[par][:, t, 0:HT] for t in range(2)]
                if first and not (isinstance(m, int) and m == 2):
                    want(pe, s_out, m - 1)
                for n, (kw, kx) in enumerate(ks_):
                    if before:
                        before(kx)
                    for q, (a, b) in enumerate(((0, 0), (0, 1), (1, 0))):
                        for t in range(2):
                            ins = pe.matmul(dst[t], lhs(a, kw), rhs[b][:, kx, HT * t:HT * t + HT],
                                            start=(first and n == 0 and q == 0), stop=(last and n == len(ks_) - 1 and q == 2))
                    if after:
                        after(n)
                if count:
                    ins.then_inc(s_mm if last else s_half, 1)

            def weights(slot, col, cols, rows=None):
                def lhs(a, k):
                    return (whi, wlo)[a][slot][:, k * cols + col:k * cols + col + P]
                return lhs

            KS = [(k, k) for k in range(KT)]

            def mean_square(src, col, sem_):
                for i, (a, _, _) in enumerate(BLOCKS):
                    ins = pe.matmul(ax[3][:, col + i:col + i + 1], src[:, a:a + P], ones[:, 0:1], start=True, stop=True)
                ins.then_inc(sem_, 1)

            def spread_blocks(bank, col, rcol, blocks):
                for i in blocks:
                    a, c, n = BLOCKS[i]
                    dst = ax[bank][:, a:a + P] if i < BLK else ax[3][:, col:col + NS]
                    ins = pe.matmul(dst, rr[:, rcol + i:rcol + i + 1].to_broadcast([P, P]), ident[:, c:c + n],
                                    start=True, stop=True)
                return ins

            def spread(bank, col, rcol, sem_):
                spread_blocks(bank, col, rcol, range(BLK + 1)).then_inc(sem_, 1)

            def norm_sum(n):
                pe.wait_ge(s_acc, 8 * n + 8)
                if n == 0:
                    pe.wait_ge(s_ones, 16)
                    pe.wait_ge(s_id, 16)
                mean_square(acc, 64, s_ms)

            def norm_spread(n):
                pe.wait_ge(s_rr, n + 1)
                spread(2, 72, 0, s_bc)

            pe.wait_ge(s_wal, 1)

            def h_ready(n):
                return lambda k: pe.wait_ge(s_hlo, 8 * n + k + 1)

            def wa(a, k):
                return (wa_hi, wa_lo)[a][:, k * P:k * P + P]

            def e_tile(name):
                m = E_AT[name]
                if name == "a":
                    product(m, m % 2, KS, wa, h, True, True, before=h_ready(0), banks=[ax[t][:, 0:HT] for t in range(2)])
                elif name[0] == "z":
                    i = int(name[1])
                    want(pe, s_out, m - 1)
                    if i == 0:
                        pe.wait_ge(s_wgb, 16)
                        pe.wait_ge(s_out, 1)
                    for t in range(2):
                        ins = pe.matmul(ps[m % 2][:, t, 0:HT], wgb[:, P * i:P * i + P], a16[:, HT * t:HT * t + HT],
                                        start=True, stop=True)
                    ins.then_inc(s_mm, 1)
                elif name[0] == "p":
                    g = int(name[1])
                    want(pe, s_out, m - 1)
                    if g == 0:
                        pe.wait_ge(s_poolw, 16)
                    pe.wait_ge(s_pm, g + 1)
                    src = (rs, acc)[g % 2]
                    for t in range(2):
                        ins = pe.matmul(ps[m % 2][:, t, 0:HT], poolw[:, g, :], src[:, HT * t:HT * t + HT],
                                        start=True, stop=True)
                    ins.then_inc(s_mm, 1)
                else:
                    i = E_TILES.index(name)
                    c = i // 2
                    pe.wait_ge(s_wlo, c + 1)
                    after = {"q1": lambda k: norm_sum(0) if k == NORM_0_AFTER else None,
                             "g2": lambda k: gla_sum() if k == GLA_SUM_AFTER else None,
                             "g3": lambda k: gla_spread(GLA_SPREAD_AFTER.index(k)) if k in GLA_SPREAD_AFTER else None}\
                        .get(name)
                    product(m, m % 2, KS, weights(c % 2, P * (i % 2), 256), h, True, True, after=after)

            def gla_turn_v():
                for b in range(BLK):
                    pe.wait_ge(s_out, E_AT["v3"] + 1)
                    if b == 3:
                        pe.wait_ge(s_rstd, 1)
                    for q in range(4):
                        ins = pe.transpose(ax[b][:, P * q:P * q + P], ev[:, q, P * b:P * b + P], ident[:])
                    ins.then_inc(s_vt, 1)

            def gla_att():
                pe.wait_ge(s_qe, 2)
                pe.wait_ge(s_ke, 1)
                for q in range(HEADS):
                    pe.wait_ge(s_vtc, q + 1)
                    r = 64 * (q % 2)
                    for b in range(BLK):
                        ins = pe.matmul(ax[q][:, P * b:P * b + P], ke[r:r + 64, q // 2, P * b:P * b + P],
                                        eq[r:r + 64, q // 2, P * b:P * b + P], start=True, stop=True)
                    ins.then_inc(s_at, 1)

            def gla_turn_k():
                pe.wait_ge(s_kd, 1)
                for q in range(2):
                    pe.wait_ge(s_atc, q + 1)
                    for b in range(2):
                        for i in range(2):
                            ins = pe.transpose(ax[q][:, 256 * b + P * i:256 * b + P * i + P],
                                               ek[:, i, P * (2 * q + b):P * (2 * q + b) + P], ident[:])
                    ins.then_inc(s_kt, 1)
                pe.wait_ge(s_atc, 3)
                for q in range(4):
                    ins = pe.transpose(ax[2][0:NS, P * q:P * q + P], ev[:, q, NP_:T], ident[:])
                ins.then_inc(s_kt, 1)

            def gla_spread_v():
                pe.wait_ge(s_ktc, 3)
                pe.wait_ge(s_atc, 4)
                pe.wait_ge(s_gsd, 1)
                for b in range(NS):
                    for r in range(2):
                        v = evs[:].rearrange("p (i r n) -> p i r n", i=2, r=2)[:, :, r, :]
                        ins = pe.matmul(ax[b // 2][64 * r:64 * r + 64, 256 * (b % 2):256 * (b % 2) + 256],
                                        ident[0:NS, b:b + 1].to_broadcast([NS, 64]), v, start=True, stop=True)
                    if b % 2:
                        ins.then_inc(s_vb, 1)

            def gla_chunk_kv():
                pe.wait_ge(s_dn, 2 * NS)
                for i in range(2):
                    for par in range(2):
                        rows = slice(64 * par, 64 * par + 64)
                        for b in range(BLK):
                            for r in range(2):
                                q = 2 * i + r
                                ins = pe.matmul(ax[2 * i + par][64 * r:64 * r + 64, P * b:P * b + P],
                                                kdtok[rows, b, 64 * q:64 * q + 64], evtok[rows, b, P * q:P * q + P],
                                                start=True, stop=True)
                        ins.then_inc(s_u, 1)

            def gla_out():
                pe.wait_ge(s_st, 2 * NCH)
                for q in range(HEADS):
                    pe.wait_ge(s_am, 2 * q + 2)
                    r = 64 * (q % 2)
                    for b in range(BLK):
                        pe.matmul(ax[q][:, P * b:P * b + P], evtok[:, b, P * q:P * q + P], att[:, q, b, :],
                                  start=(b == 0), stop=False, skip_group_check=True)
                    for c in range(1, NCH):
                        ins = pe.matmul(ax[q][:, CH * c:CH * c + CH], states[r:r + 64, q // 2, c - 1, :],
                                        eq[r:r + 64, q // 2, CH * c:CH * c + CH], start=False, stop=(c == NCH - 1),
                                        skip_group_check=True)
                    ins.then_inc(s_o, 1)

            def gla_dec_out():
                pe.wait_ge(s_oc, 1)
                pe.wait_ge(s_qm, 1)
                for i in range(2):
                    for b in range(NS):
                        at_ = 2 * (NS * i + b)
                        ins = pe.matmul(ax[0][:, at_:at_ + 2], gs[:, i, b, :], qmask[:, i, b, :], start=True, stop=True)
                ins.then_inc(s_od, 1)

            def gla_sum():
                pe.wait_ge(s_oc, 4)
                for q in range(HEADS):
                    pe.wait_ge(s_osq, q + 1)
                    mean_square(osq[q], 64 + 5 * q, s_oms)

            def gla_spread(part):
                if part == 0:
                    pe.wait_ge(s_orr, 1)
                    pe.wait_ge(s_odc, 1)
                    for q in range(HEADS):
                        spread_blocks(3, 96 + 8 * q, 5 * q, [BLK])
                else:
                    pe.wait_ge(s_on, 1)
                for q in (range(3) if part == 0 else (3,)):
                    spread_blocks(q % 3, 0, 5 * q, range(BLK)).then_inc(s_obc, 1)

            for name in E_ORDER:
                e_tile(name)
                if name == "q1":
                    norm_spread(0)
                if name == "u0":
                    gla_turn_v()
                if name == "u1":
                    gla_att()
                if name == "u2":
                    gla_turn_k()
                if name == "u3":
                    gla_spread_v()
                if name == "g0":
                    gla_chunk_kv()
                if name == AFTER_O:
                    gla_out()
                    gla_dec_out()
            EO_POOL, EO_HEADS = (4, 5, 6, 7), (0, 1, 2, 3)

            def eo_part(n, j, ks_, before=None):
                m = M_EO + 2 * n + j
                product(m, m % 2, [(k, k) for k in ks_], weights(n % 2, P * j, 256), (op_hi, op_lo), ks_[0] == 4,
                        ks_[-1] == 3, before=before, count=ks_[-1] == 3)

            pe.wait_ge(s_wlo, C_EO + 1)
            pe.wait_ge(s_oplo, 4)
            for j in range(2):
                eo_part(0, j, EO_POOL)
            for j in range(2):
                eo_part(0, j, EO_HEADS, before=(lambda k: pe.wait_ge(s_oplo, k + 5)) if j == 0 else None)
            for n in range(1, N_EO):
                pe.wait_ge(s_wlo, C_EO + n + 1)
                for j in range(2):
                    eo_part(n, j, EO_POOL + EO_HEADS)

            def norm_inside(n):
                def after(k):
                    if k == 4:
                        norm_sum(n)
                    if k == KT - 1:
                        norm_spread(n)
                return after

            def ffn(l):
                c0, m0, d0, dm = C_F[l], M_F[l], C_D[l], M_D[l]

                def pair(i, first=False):
                    for j in range(2):
                        n = 2 * i + j
                        pe.wait_ge(s_wlo, c0 + n + 1)
                        for u in range(2):
                            start = first and j == 0 and u == 0
                            product(m0 + 2 * n + u, (m0 + u) % 2, KS, weights(j, P * u, 256), h, True, True,
                                    before=h_ready(1 + 2 * l) if start else None,
                                    after=norm_inside(1 + 2 * l) if start else None)

                pair(0, first=True)
                with pe.Fori(1, N_F // 2) as i:
                    pair(i)

                def hid_ready(k):
                    if k >= FT - 4:
                        pe.wait_ge(s_hidlo, FT * l + k + 1)

                with pe.Fori(0, KT // 2) as i:
                    for u in range(2):
                        m = 2 * i + u
                        for half in range(2):
                            pe.wait_ge(s_wlo, d0 + 2 * m + half + 1)
                            product(dm + m, (dm + u) % 2, [(k, 11 * half + k) for k in range(11)], weights(half, 0, P),
                                    (hid_hi, hid_lo), half == 0, half == 1, before=hid_ready if u == 0 else None)

            ffn(0)

            def dec_out(hh, b):
                if b == 0:
                    pe.wait_ge(r_vl, hh + 1)
                    if isinstance(hh, int) and hh == 0:
                        pe.wait_ge(r_sel, 3)
                pe.wait_ge(r_tl, 8 * hh + b + 1)
                for part in (th, tl):
                    ins = pe.matmul(ax[3][:], osel[:, NS - 1 - b:NS - 1 - b + P], part[:], start=(b == 0 and part is th),
                                    stop=(b == NS - 1 and part is tl))
                ins.then_inc(r_os, 1)

            def turn_out(hp):
                pe.wait_ge(r_osr, hp + 1)
                pe.sem_inc(s_tstep, 1)
                for d in range(4):
                    ins = pe.transpose(ax[3][:, NS * d:NS * d + NS], t2[0:NS, P * d:P * d + P], ident[0:NS, 0:NS])
                ins.then_inc(r_ot, 1)

            def finish_sum(hp):
                pe.wait_ge(r_acc, 5 * hp + 5)
                mean_square(t0, 64, r_ms)

            def finish_spread(hp):
                pe.wait_ge(r_rr, hp + 1)
                spread(2, 72, 0, r_bc)

            def head(hh):
                m0 = M_OI + 12 * hh
                first = isinstance(hh, int) and hh == 0

                def tile_(t):
                    if t % 2 == 0:
                        pe.wait_ge(s_wlo, C_OI + 6 * hh + t // 2 + 1)
                    start = first and t == 0
                    product(m0 + t, (M_OI + t) % 2, KS, weights((t // 2) % 2, P * (t % 2), 256), h, True, True,
                            before=h_ready(2) if start else None, after=norm_inside(2) if start else None)

                def turn_v(b):
                    if b < 2:
                        if not first:
                            pe.wait_ge(r_stc, 2 * hh - 1 + b)
                    else:
                        pe.wait_ge(r_trc, 7 * hh + b - 1)
                    pe.wait_ge(s_out, m0 + 4)
                    for q in range(4):
                        ins = pe.transpose(ax[b % 2][:, P * q:P * q + P], rv[:, q, P * b:P * b + P], ident[:])
                    ins.then_inc(r_tr, 1)

                def turn_vs():
                    if not first:
                        pe.wait_ge(r_rc, hh)
                    for q in range(4):
                        ins = pe.transpose(ax[3][0:NS, P * q:P * q + P], rv[:, q, NP_:T], ident[:])
                    ins.then_inc(r_tr, 1)

                def scores(j):
                    pe.wait_ge(r_rot, 4 * hh + 4)
                    pe.wait_ge(*((r_trc, 7 * hh + 3 + j) if j < 2 else (r_p, 4 * hh + j - 1)))
                    for t in range(2):
                        ins = pe.matmul(ax[j % 2][:, 0:NP_ - P * j], rk[:, t, P * j:P * j + P], rq[:, t, P * j:NP_],
                                        start=(t == 0), stop=(t == 1))
                    ins.then_inc(r_sc, 1)

                def turn_k(q):
                    pe.wait_ge(r_p, 4 * hh + 3 + q)
                    for b in range(2):
                        for i in range(2):
                            ins = pe.transpose(ax[q][:, 256 * b + P * i:256 * b + P * i + P],
                                               rk[:, i, P * (2 * q + b):P * (2 * q + b) + P], ident[:])
                    ins.then_inc(r_tr, 1)

                def pv(q):
                    pe.wait_ge(*((r_trc, 7 * hh + 6 + q) if q < 2 else (r_pvc, 4 * hh + q - 1)))
                    at_ = 0
                    for j in range(BLK):
                        n = NP_ - P * j
                        ins = pe.matmul(ax[q % 2][:, P * j:NP_], vtok[:, j, P * q:P * q + P], prob[:, at_:at_ + n],
                                        start=(j == 0), stop=(j == BLK - 1))
                        at_ += n
                    ins.then_inc(r_pv, 1)

                def state(q):
                    pe.wait_ge(r_pvc, 4 * hh + 3 + q)
                    for j in range(BLK):
                        ins = pe.matmul(ax[q][:], ktok[:, j, P * q:P * q + P], vtok[:, j, :], start=(j == 0), stop=(j == BLK - 1))
                    ins.then_inc(r_st, 1)

                def spread_v(b):
                    want(pe, r_sn, 8 * hh + b)
                    if b == 0:
                        pe.wait_ge(r_vl, hh + 1)
                        if first:
                            pe.wait_ge(r_sel, 3)
                            pe.wait_ge(s_rstd, 3)
                    pe.matmul(ax[2][:], vsel[0:64, b:b + 1].to_broadcast([64, P]), vs[:], start=True, stop=True).then_inc(r_vb, 1)

                tile_(0)
                if not first:
                    dec_out(hh - 1, 6)
                tile_(1)
                if not first:
                    dec_out(hh - 1, 7)
                tile_(2)
                if not first:
                    turn_out(hh - 1)
                tile_(3)
                if not first:
                    finish_sum(hh - 1)
                tile_(4)
                if not first:
                    finish_spread(hh - 1)
                turn_v(0)
                turn_v(1)
                tile_(5)
                turn_v(2)
                turn_v(3)
                tile_(6)
                tile_(7)
                turn_vs()
                tile_(8)
                scores(0)
                scores(1)
                spread_v(0)
                tile_(9)
                scores(2)
                scores(3)
                spread_v(1)
                tile_(10)
                turn_k(0)
                turn_k(1)
                dec_out(hh, 0)
                spread_v(2)
                tile_(11)
                dec_out(hh, 1)
                spread_v(3)
                pv(0)
                pv(1)
                dec_out(hh, 2)
                spread_v(4)
                pv(2)
                pv(3)
                dec_out(hh, 3)
                spread_v(5)
                state(0)
                dec_out(hh, 4)
                spread_v(6)
                state(1)
                dec_out(hh, 5)
                spread_v(7)

            head(0)
            with pe.Fori(1, HEADS) as hh:
                head(hh)

            last = HEADS - 1

            def out_part(n, k):
                if k == 0:
                    pe.wait_ge(s_wlo, C_OO + n + 1)
                if n == 0:
                    pe.wait_ge(s_olo, k + 1)
                product(M_OO + n, (M_OO + n) % 2, [(OO_ORDER[k], OO_ORDER[k])], weights(n % 2, 0, P), (o_hi, o_lo),
                        k == 0, k == 15, count=k == 15)

            meanwhile = {0: lambda: dec_out(last, 6), 2: lambda: dec_out(last, 7), 4: lambda: turn_out(last),
                         6: lambda: finish_sum(last), 8: lambda: finish_spread(last)}
            for k in range(9):
                out_part(0, k)
                out_part(1, k)
                meanwhile.get(k, lambda: None)()
            for n, ks_ in ((0, (9, 10, 11)), (1, (9, 10)), (0, (12, 13, 14, 15)), (1, (11, 12, 13, 14, 15))):
                for k in ks_:
                    out_part(n, k)
            with pe.Fori(1, N_OO // 2) as i:
                for j in range(2):
                    n = 2 * i + j
                    pe.wait_ge(s_wlo, C_OO + n + 1)
                    product(M_OO + n, (M_OO + j) % 2, [(k, k) for k in OO_ORDER], weights(j, 0, P), (o_hi, o_lo), True,
                            True)
            ffn(1)
            for src, ready, count in ((acc, s_acc, 8 * 4 + 7), (sq, s_sql, 1)):
                pe.wait_ge(ready, count)
                for i, (a, _, _) in enumerate(BLOCKS):
                    ins = pe.matmul(ax[3][:, 64 + i:65 + i], src[:, a:a + P], ones[:, 0:1], start=(src is acc and i == 0),
                                    stop=(src is sq), skip_group_check=True)
            ins.then_inc(s_ms, 1)
            norm_spread(4)


def columns(w, n):
    k = w.shape[0] // P
    return w.reshape(k, P, -1, n).transpose(2, 1, 0, 3).reshape(-1, P, k * n)


def down_chunks(w):
    return w.reshape(2, 11, P, KT, P).transpose(3, 0, 2, 1, 4).reshape(N_D, P, W_DOWN)


def gate_up(gate, up):
    g, u = (m.reshape(KT, P, FT, P) for m in (gate, up))
    return np.stack([g, u], axis=3).transpose(2, 1, 0, 3, 4).reshape(FT, P, W_FULL)


def tables():
    f = np.float32
    angle = (1.0 / (f(10000.0) ** np.linspace(0.0, 1.0, P, dtype=f))).astype(f)
    pos = np.concatenate([np.arange(NP_), np.full(NS, 4096)]).astype(f)
    ang = (angle[:, None] * pos[None, :]).astype(f).astype(np.float64)
    cs = np.stack([np.cos(ang), np.sin(ang)], axis=1).astype(f)
    gamma = 1.0 - 2.0 ** (-5.0 - np.arange(HEADS))
    s, t = np.arange(P)[:, None], np.arange(NP_)[None, :]
    dec = np.stack([np.where(t >= s, g ** np.maximum(t - s, 0).astype(np.float64), 0.0) / 16 for g in gamma]).astype(f)
    kscale = np.stack([g ** (NP_ - 1.0 - P * b - np.arange(P)) / 16 for g in gamma for b in range(BLK)], axis=1)
    gm = np.tile(gamma[None, :], (P, 1))
    reset = np.ones((P, NP_), f)
    reset[:, ::CH] = 0
    inv = np.stack([1.0 / np.minimum(2 << g, np.arange(16) + 1.0) for g in range(4)])
    return dict(cs=cs, dec=dec, kscale=kscale.astype(f), gm=gm.astype(f), reset=reset,
                invc=np.tile(inv[None], (P, 1, 1)).astype(f), ident=np.eye(P, dtype=f),
                ones=np.concatenate([np.full((P, 1), 1.0 / DM), np.ones((P, 7)),
                                     (np.arange(P)[:, None] % 32 == np.arange(8)) & (np.arange(P)[:, None] < 64)],
                                    axis=1).astype(f))


def kernel(**inputs):
    import concourse.bacc as bacc
    from concourse.bass_utils import run_bass_kernel_spmd

    v = {k: np.asarray(a) for k, a in inputs.items()}
    c = tables()
    tiles = lambda a: a.reshape(-1, P).T
    we, wo = v["w_in_even"][0], v["w_in_odd"][0]
    cols = []
    for hh in range(HEADS):
        q, k = hh * 256, 1024 + hh * 256
        cols += [np.arange(2048 + 512 * hh, 2560 + 512 * hh)]
        cols += [np.arange(s + e, s + 256, 2) for s in (q, k) for e in (0, 1)]
        cols += [np.arange(4096 + 512 * hh, 4608 + 512 * hh)]
    arrays = dict(
        x=np.concatenate([v["x_prompt"][0], v["x_sample"][:, 0]]).T.reshape(KT, P, T).transpose(1, 0, 2),
        vec=np.concatenate([tiles(v["norm_mix"][0]), tiles(v["norm_ffn"][0]), tiles(v["norm_mix"][1]),
                            tiles(v["norm_ffn"][1]), tiles(v["norm_final"]), tiles(v["gla_gain"][0]),
                            tiles(v["pool_scale"][0]), tiles(v["b_gate"][0]), c["kscale"], c["gm"]], axis=1),
        w_a=np.pad(we[:, 1536:1552], ((0, 0), (0, P - 16))).reshape(KT, P, P).transpose(1, 0, 2).reshape(P, KT * P),
        w_e=columns(np.concatenate([we[:, 0:1024], we[:, 1552:2064], we[:, 1024:1536]], axis=1), 256),
        w_eo=columns(v["w_out_even"][0], 256),
        w_f0=gate_up(v["w_ffn_gate"][0], v["w_ffn_up"][0]), w_d0=down_chunks(v["w_ffn_down"][0]),
        w_oi=columns(wo[:, np.concatenate(cols)], 256), w_oo=columns(v["w_out_odd"][0], P),
        w_f1=gate_up(v["w_ffn_gate"][1], v["w_ffn_up"][1]), w_d1=down_chunks(v["w_ffn_down"][1]),
        wgb=v["w_gate_b"][0], poolw=v["pool_w"][0].transpose(1, 0, 2),
        gs=v["state_gla"][0].reshape(NS, 2, P, P).transpose(2, 1, 0, 3),
        pbuf=v["state_pool"][0].reshape(NS, 15, 4, P).transpose(3, 2, 0, 1),
        ret_in=v["state_ret"][0].reshape(NS * HEADS, P, 1024),
        cs=c["cs"], dec=c["dec"], reset=c["reset"], invc=c["invc"], ident=c["ident"], ones=c["ones"])
    outs = dict(y=(P, KT, T), gla_p=(P, 2, P), gla_s=(P, 2, NS, P), rows=(P, 4, NS + 1, 15),
                ret_p=(HEADS, P, 1024), ret_s=(NS * HEADS, P, 1024))
    nc = bacc.Bacc("TRN2", target_bir_lowering=False, num_devices=1)
    arrays = {"in_" + n: np.ascontiguousarray(a) for n, a in arrays.items()}
    io = {n[3:]: nc.dram_tensor(n, a.shape, F32, kind="ExternalInput").ap() for n, a in arrays.items()}
    io.update({n: nc.dram_tensor("out_" + n, s, F32, kind="ExternalOutput").ap() for n, s in outs.items()})
    build(nc, io)
    r = run_bass_kernel_spmd(nc, [arrays], core_ids=[0]).results[0]
    y = r["out_y"].transpose(2, 1, 0).reshape(T, DM)
    rows = r["out_rows"].transpose(2, 3, 1, 0).reshape(NS + 1, 15, 512)
    return (y[None, :NP_], y[NP_:, None],
            r["out_gla_p"].transpose(1, 0, 2).reshape(1, 1, HEADS, 64, P),
            r["out_gla_s"].transpose(2, 1, 0, 3).reshape(1, NS, HEADS, 64, P),
            rows[None, NS:], rows[None, :NS],
            r["out_ret_p"].reshape(1, 1, HEADS, 256, 512),
            r["out_ret_s"].reshape(1, NS, HEADS, 256, 512))
```

```python
from contextlib import ExitStack

import numpy as np

import concourse.bass as bass
from concourse import mybir

F32 = mybir.dt.float32
F32R = mybir.dt.float32r
ACT = mybir.ActivationFunctionType
ALU = mybir.AluOpType
ds = bass.ds

P = 128
DM, KT = 1024, 8
NP_, NS, T = 512, 8, 520
HT = T // 2
BLK = NP_ // P
FT = 22
CH = 64
N_PROB = NP_ * (BLK + 1) // 2
NCH = NP_ // CH
W_FULL, W_HALF, W_DOWN = 2048, 1024, 11 * P
HEADS = 4
EPS = 1e-6

N_E, N_EO, N_F, N_D, N_OI, N_OO = 8, 4, FT, 16, 24, 8
C_E = 0
C_EO = C_E + N_E
C_F = [C_EO + N_EO, 0]
C_D = [C_F[0] + N_F, 0]
C_OI = C_D[0] + N_D
C_OO = C_OI + N_OI
C_F[1] = C_OO + N_OO
C_D[1] = C_F[1] + N_F
E_ORDER = ["a", "q0", "q1", "k0", "z0", "k1", "z1", "v0", "v1", "v2", "v3", "u0", "u1", "p0", "u2", "p1",
           "u3", "g0", "p2", "g1", "p3", "g2", "g3"]
E_AT = {n: i for i, n in enumerate(E_ORDER)}
E_TILES = ["q0", "q1", "k0", "k1", "v0", "v1", "v2", "v3", "u0", "u1", "u2", "u3", "g0", "g1", "g2", "g3"]
M_EO = len(E_ORDER)
M_F = [M_EO + 8, 0]
M_D = [M_F[0] + 2 * FT, 0]
M_OI = M_D[0] + 8
M_OO = M_OI + 48
M_F[1] = M_OO + 8
M_D[1] = M_F[1] + 2 * FT
OO_ORDER = [8, 9, 10, 11, 4, 5, 0, 1, 2, 3, 6, 7, 12, 13, 14, 15]
Y_DVE, Y_POOL, Y_STORES = (0, 1, 2, 3, 4, 7), (5, 6), ((0, 1), (5, 6), (2, 3), (4, 7))
Y_AFTER = (4, 9)
Y_PARTS = ((0, 2 * P, (0, 1)), (2 * P, T, (2, 3, 4)))
NORM_0_AFTER, GLA_SUM_AFTER, GLA_SPREAD_AFTER = (2, 5), (2, 3, 4, 5), (0, 4)
AFTER_O = "g1"
OO_ALONE = 4
V_GAIN, V_GLA, V_PS, V_BG, V_KS, V_GM, V_N = 0, 40, 41, 45, 47, 63, 67


def build(nc, io):
    at = nc.alloc_sbuf_tensor_at
    cursor = [16544]

    def fixed(name, shape, dt):
        t = at(name, shape, dt, offset=cursor[0])
        cursor[0] += (int(np.prod(shape[1:])) * 4 + 31) // 32 * 32
        return t

    TB = T * 4
    raw = [fixed(f"raw{i}", [P, W_FULL], F32) for i in range(2)]
    whi = [fixed(f"whi{i}", [P, W_FULL], F32R) for i in range(2)]
    wlo = [fixed(f"wlo{i}", [P, W_FULL], F32R) for i in range(2)]
    X_OFF = cursor[0]
    x = fixed("x", [P, KT, T], F32)
    h = [fixed("h_hi", [P, KT, T], F32R), fixed("h_lo", [P, KT, T], F32R)]
    rstd, acc, sq, rs, t0, t1, t2, t3 = [fixed(n, [P, T], F32)
                                         for n in ("rstd", "acc", "sq", "rs", "t0", "t1", "t2", "t3")]
    tmp = [t0, t1, t2, t3]
    PROB_AT = [sum(NP_ - P * i for i in range(j)) for j in range(BLK + 1)]
    osq = [sq, t0, rs, acc]
    qbuf = [sq, acc]
    RS_OFF = cursor[0] - 5 * ((TB + 31) // 32 * 32)
    ident = fixed("ident", [P, P], F32)
    ones = fixed("ones", [P, 16], F32)
    vec = fixed("vec", [P, V_N], F32)
    eps = fixed("eps", [P, 8], F32)
    rt = fixed("rt", [P, 20], F32)
    rr = fixed("rr", [P, 20], F32)
    R, TOP = cursor[0], 229344

    def region(name, shape, dt, off):
        size = int(np.prod(shape[1:])) * 4
        assert R + off + size <= TOP, (name, R + off + size - TOP)
        return at(name, shape, dt, offset=R + off), off + size

    hid_hi, o = region("hid_hi", [P, FT, T], F32R, 0)
    hid_lo, o = region("hid_lo", [P, FT, T], F32R, o)
    eq, o = region("eq", [P, 2, T], F32, 0)
    ek, o = region("ek", [P, 2, T], F32, o)
    eb, o2 = region("eb", [P, 2, T], F32, o)
    et, o3 = region("et", [P, 2, T], F32, o2)
    states, _ = region("states", [P, 2, NCH, P], F32, o)
    ex, o = region("ex", [P, 2, T], F32, o3)
    kdtok, _ = region("kdtok", [P, BLK, 256], F32, o3)
    ke, o = region("ke", [P, 2, T], F32, o)
    ev, op_off = region("ev", [P, 4, T], F32, o)
    op_hi, o = region("op_hi", [P, KT, T], F32R, op_off)
    gsil, _ = region("gsil", [P, 4, T], F32, o)
    op_lo, end = region("op_lo", [P, KT, T], F32R, o)
    pbuf, o = region("pbuf", [P, 4, NS, 15], F32, op_off)
    wa_raw, o2 = region("wa_raw", [P, KT * P], F32, o)
    evs, _ = region("evs", [NS, 512], F32, o)
    wa_hi, o = region("wa_hi", [P, KT * P], F32R, o2)
    wa_lo, o = region("wa_lo", [P, KT * P], F32R, o)
    reset, o = region("reset", [P, NP_], F32, o)
    wgb, o = region("wgb", [16, 256], F32, o)
    a16, o = region("a16", [16, T], F32, o)
    assert o <= end
    att, o = region("att", [P, 4, BLK, P], F32, end)
    evtok, o = region("evtok", [P, BLK, 512], F32, o)
    gs, o = region("gs", [P, 2, NS, P], F32, o)
    poolw, o = region("poolw", [P, 4, P], F32, o)
    elast, o = region("elast", [P, 2, NCH], F32, o)
    eas, o = region("eas", [P, 2, NS], F32, o)
    invc, o = region("invc", [P, 4, 16], F32, o)
    qmask, o = region("qmask", [P, 2, NS, 2], F32, o)
    pout, o = region("pout", [P, 4, NS + 1, 15], F32, o)
    o32, oh = region("o32", [P, 16, T], F32, 0)
    o_lo, _ = region("o_lo", [P, 16, T], F32R, 0)
    o_hi, _ = region("o_hi", [P, 16, T], F32R, oh)
    rq, o = region("rq", [P, 2, T], F32, oh)
    ktok_lo, _ = region("ktok_lo", [P, BLK, 256], F32R, oh)
    rst, _ = region("rst", [P, 2, 512], F32, o)
    rk, o = region("rk", [P, 2, T], F32, o)
    PROB_OFF = o
    prob, _ = region("prob_hi", [P, N_PROB], F32R, o)
    rv, o = region("rv", [P, 4, T], F32, o)
    vtok, o = region("vtok_hi", [P, BLK, 512], F32R, o)
    ktok, o = region("ktok_hi", [P, BLK, 256], F32R, o)
    rg, o = region("rg", [P, 4, T], F32, o)
    dec, o = region("dec", [P, NP_], F32, o)
    cs, o = region("cs", [P, 2, T], F32, o)
    sring, o = region("sring", [P, 4, 2, 512], F32, o)
    vs, o = region("vs", [64, 512], F32R, o)
    ks, o = region("ks", [P, 2, NS], F32, o)
    qs, o = region("qs", [P, 2, NS], F32, o)
    vsel, o = region("vsel", [P, NS], F32R, o)
    osel, o = region("osel", [P, P + NS], F32R, o)
    TAIL = 5632
    assert TAIL >= N_PROB * 4 and TAIL + 2048 <= 4 * TB
    th, _ = region("th", [P, 512], F32R, PROB_OFF + TAIL)
    vtok_lo = at("vtok_lo", [P, BLK, 512], F32R, offset=X_OFF)
    prob_raw = at("prob_raw", [P, N_PROB], F32, offset=X_OFF + BLK * 512 * 4)
    prob_lo = at("prob_lo", [P, N_PROB], F32R, offset=X_OFF + BLK * 512 * 4)
    tl = at("tl", [P, 512], F32R, offset=RS_OFF)

    with ExitStack() as ctx:
        def sem(name):
            return ctx.enter_context(nc.semaphore(name))

        ps = [ctx.enter_context(nc.psum_tensor(f"ps{i}", [P, 2, 512], F32)) for i in range(2)]
        ax = [ctx.enter_context(nc.psum_tensor(f"ax{i}", [P, 512], F32)) for i in range(4)]
        s_raw = [sem("raw0_loaded"), sem("raw1_loaded")]
        s_whi, s_wlo = sem("weights_hi"), sem("weights_lo")
        s_whi0, s_wlo0 = sem("first_half_chunk_hi"), sem("first_half_chunk_lo")
        s_mm, s_out, s_half = sem("mtile_done"), sem("mtile_taken"), sem("half_mtile_done")
        s_x = [sem(f"x{i}_loaded") for i in range(4)]
        s_vec, s_ones, s_id, s_wa = sem("vec_loaded"), sem("ones_loaded"), sem("ident_loaded"), sem("wa_loaded")
        s_reset, s_wgb, s_gsl, s_poolw, s_pbuf, s_invc = [sem(n + "_loaded") for n in
                                                         ("reset", "wgb", "gs", "poolw", "pbuf", "invc")]
        s_eps, s_qz, s_qm = sem("eps_set"), sem("gla_dec_q_zeroed"), sem("gla_dec_q_masked")
        s_hhi, s_hlo = sem("h_hi_written"), sem("h_lo_written")
        s_sq, s_acc, s_sq0 = sem("x_squared"), sem("squares_summed"), sem("x_squared_by_vector")
        s_ms, s_rt, s_rr, s_bc, s_rstd = (sem("mean_square"), sem("rms"), sem("rms_inverted"),
                                          sem("rstd_spread"), sem("rstd_written"))
        s_sg, s_hid, s_hidhi, s_hidlo = sem("silu_gate"), sem("hidden"), sem("hidden_hi"), sem("hidden_lo")
        s_wah, s_wal, s_z1, s_sp, s_la, s_b, s_eb, s_enb = [sem(n) for n in (
            "wa_hi_written", "wa_lo_written", "z_written", "softplus_step", "log_decay", "decay_summed",
            "decay_exp", "decay_exp_inv")]
        s_qe, s_ke, s_dl, s_edl, s_kd, s_gsd = [sem(n) for n in (
            "q_decayed", "k_decayed", "decay_to_end", "decay_to_end_exp", "k_decayed_to_end", "gla_dec_decayed")]
        s_vt, s_vtc, s_at, s_atc, s_am = [sem(n) for n in (
            "gla_v_turned", "gla_v_taken", "gla_att", "gla_att_taken", "gla_att_masked")]
        s_kt, s_ktc, s_vb, s_dn, s_u, s_st = [sem(n) for n in (
            "gla_kv_turned", "gla_kv_taken", "gla_v_spread", "gla_dec_state", "gla_chunk_kv", "gla_states")]
        s_o, s_oc, s_od, s_odc, s_osq = [sem(n) for n in (
            "gla_o", "gla_o_taken", "gla_dec_o", "gla_dec_o_taken", "gla_o_squared")]
        s_oms, s_ort, s_orr, s_obc, s_on = [sem(n) for n in (
            "gla_ms", "gla_rms", "gla_rms_inverted", "gla_rstd_spread", "gla_o_normed")]
        s_gs, s_og, s_ophi, s_oplo = sem("gla_silu"), sem("gla_gated"), sem("op_hi_written"), sem("op_lo_written")
        s_pl, s_pm, s_rows = sem("pool_step"), sem("pooled"), sem("pool_rows_written")
        s_es = sem("even_stores")
        r_cs, r_csr, r_d = sem("ret_tables_loaded"), sem("ret_tables_scaled"), sem("ret_decay_loaded")
        r_rot, r_ks = sem("ret_rotated"), sem("ret_dec_k")
        r_tr, r_trc, r_sc, r_p = sem("ret_turned"), sem("ret_turned_taken"), sem("ret_scores"), sem("ret_probs")
        r_pv, r_pvc, r_st, r_stc, r_sto = [sem(n) for n in (
            "ret_pv", "ret_pv_taken", "ret_state", "ret_state_taken", "ret_state_stored")]
        r_in = [sem(f"ret_dec_in{i}") for i in range(4)]
        r_so = [sem(f"ret_dec_stored{i}") for i in range(4)]
        r_g, r_vb, r_sn, r_os, r_osc = [sem(n) for n in (
            "ret_dec_decayed", "ret_v_spread", "ret_dec_state", "ret_dec_o", "ret_dec_o_taken")]
        r_z = sem("ret_dec_v_zeroed")
        r_vh, r_vsc, r_kh, r_ktc, r_ph, r_pl = [sem(n) for n in (
            "ret_v_hi", "ret_dec_v_hi", "ret_k_hi", "ret_k_taken", "ret_probs_hi", "ret_probs_lo")]
        s_xs, s_xl = sem("residual_stored"), sem("residual_loaded")
        r_vl, r_sel, r_ta, r_qs, r_th, r_tl, r_osr, r_ot, r_rc = [sem(n) for n in (
            "ret_dec_v_lo", "ret_selectors", "ret_dec_q0", "ret_dec_qsum", "ret_dec_sum_hi", "ret_dec_sum_lo",
            "ret_dec_o_rows", "ret_dec_o_turned", "ret_rstd_copied")]
        r_sq, r_acc, r_ms, r_rt, r_rr, r_bc = [sem(n) for n in (
            "ret_o_squared", "ret_squares", "ret_ms", "ret_rms", "ret_rms_inverted", "ret_rstd_spread")]
        r_sg, r_on, r_gd = sem("ret_silu"), sem("ret_normed"), sem("ret_gated")
        s_ohi, s_olo = sem("o_hi_written"), sem("o_lo_written")
        s_x7, s_sql, s_xg = sem("last_x"), sem("last_x_squared"), sem("x_gained")
        s_y, s_yp, s_yst = sem("y_written"), sem("y_written_by_gpsimd"), sem("y_stored")
        s_astep, s_pstep, s_tstep = sem("scalar_step"), sem("gpsimd_step"), sem("tensor_step")
        block = ctx.enter_context(nc.Block())

        def halves(t, i):
            return t[:, ds(i, 1), :].rearrange("p a (b n) -> p (a b) n", b=2)

        def flat(t, i):
            return t[:, ds(i, 1), :].rearrange("p a n -> p (a n)")

        def two(t):
            return t[:].rearrange("p (b n) -> p b n", b=2)

        def mt(m):
            return ps[m % 2][:, :, 0:HT]

        def want(eng, s, v):
            if not isinstance(v, int) or v > 0:
                eng.wait_ge(s, v)

        def gain(n, m):
            return vec[:, ds(V_GAIN + 8 * n + m, 1)]

        BLOCKS = [(0, 0, P), (P, 0, P), (2 * P, 0, P), (3 * P, 0, P), (T - P, P - NS, NS)]

        @block.sync
        def _(sp):
            def load(c, slot, src, idx, n):
                if not isinstance(c, int) or c >= 2:
                    sp.wait_ge(s_whi, c - 1)
                    sp.wait_ge(s_wlo, c - 1)
                sp.dma_start(raw[slot][:, 0:n],
                             src[ds(idx, 1)].rearrange("a p n -> p (a n)")).then_inc(s_raw[slot], 16)

            def phase(c0, n, src, size, first=0):
                with sp.Fori(first // 2, n // 2) as i:
                    for j in range(2):
                        load(c0 + 2 * i + j, j, src, 2 * i + j, size)

            sp.dma_start(vec[:], io["vec"]).then_inc(s_vec, 16)
            sp.dma_start(wa_raw[:], io["w_a"]).then_inc(s_wa, 16)
            for q in range(4):
                sp.dma_start(x[:, 2 * q:2 * q + 2, :], io["x"][:, 2 * q:2 * q + 2, :]).then_inc(s_x[q], 16)
            for c in range(2):
                load(c, c, io["w_e"], c, W_FULL)
            for dst, name, s in ((ones, "ones", s_ones), (ident, "ident", s_id), (reset, "reset", s_reset),
                                 (wgb, "wgb", s_wgb), (gs, "gs", s_gsl), (poolw, "poolw", s_poolw),
                                 (pbuf, "pbuf", s_pbuf), (invc, "invc", s_invc)):
                sp.dma_start(dst[:], io[name]).then_inc(s, 16)
            phase(C_E, N_E, io["w_e"], W_FULL, 2)
            phase(C_EO, N_EO, io["w_eo"], W_FULL)
            phase(C_F[0], N_F, io["w_f0"], W_FULL)
            phase(C_D[0], N_D, io["w_d0"], W_DOWN)
            for j in range(2):
                load(C_OI + j, j, io["w_oi"], j, W_FULL)
            sp.wait_ge(s_mm, M_OI)
            sp.dma_start(cs[:], io["cs"]).then_inc(r_cs, 16)
            sp.wait_ge(s_hhi, 3 * KT)
            sp.wait_ge(s_hlo, 3 * KT)
            sp.wait_ge(s_acc, 3 * KT)
            sp.dma_start(io["y"], x[:]).then_inc(s_xs, 16)
            phase(C_OI, N_OI, io["w_oi"], W_FULL, 2)
            for n in range(4):
                load(C_OO + n, n % 2, io["w_oo"], n, W_FULL)
            sp.wait_ge(s_xs, 16)
            sp.wait_ge(r_st, 2 * HEADS)
            sp.dma_start(x[:], io["y"]).then_inc(s_xl, 16)
            phase(C_OO, N_OO, io["w_oo"], W_FULL, 4)
            phase(C_F[1], N_F, io["w_f1"], W_FULL)
            phase(C_D[1], N_D, io["w_d1"], W_DOWN)
            for part, (a, b, _) in enumerate(Y_PARTS):
                for m0, m1 in Y_STORES:
                    if m1 in Y_POOL:
                        sp.wait_ge(s_yp, len(Y_POOL) * part + Y_POOL.index(m1) + 1)
                    else:
                        sp.wait_ge(s_y, len(Y_DVE) * part + Y_DVE.index(m1) + 1)
                    pair = slice(m0, m1 + 1, m1 - m0)
                    sp.dma_start(io["y"][:, pair, a:b], x[:, pair, a:b]).then_inc(s_yst, 16)
            sp.wait_ge(s_yst, 16 * KT)
            sp.wait_ge(s_es, 16 * 3)
            sp.wait_ge(r_sto, 16 * HEADS)
            for q in range(4):
                sp.wait_ge(r_so[q], 16 * HEADS * NS // 4)

        @block.scalar
        def _(act):
            def hi(c, slot, size, used):
                act.wait_ge(s_raw[slot], 8 * (c - slot) + 16)
                if used is not None:
                    act.wait_ge(*used)
                act.activation(whi[slot][:, 0:size], raw[slot][:, 0:size], ACT.Copy).then_inc(s_whi, 1)

            def settled():
                act.sem_inc(s_astep, 1)

            def h_hi(n, m, ready):
                act.wait_ge(*ready)
                settled()
                act.activation(flat(h[0], m), flat(x, m), ACT.Copy, scale=gain(n, m)).then_inc(s_hhi, 1)

            def root(n):
                act.wait_ge(s_ms, n + 1)
                act.activation(rt[:, 0:5], ax[3][:, 64:69], ACT.Sqrt, bias=eps[:, 0:1]).then_inc(s_rt, 1)
                act.wait_ge(s_bc, n + 1)
                act.activation(rstd[:, 0:NP_], ax[2][:], ACT.Copy)
                act.activation(rstd[:, NP_:T], ax[3][:, 72:72 + NS], ACT.Copy).then_inc(s_rstd, 1)

            act.wait_ge(s_wa, 16)
            act.activation(wa_hi[:], wa_raw[:], ACT.Copy).then_inc(s_wah, 1)
            act.wait_ge(s_vec, 16)
            for m in range(KT):
                h_hi(0, m, (s_x[m // 2], 16))
            act.wait_ge(s_raw[0], 16)
            act.activation(whi[0][:, 0:W_HALF], raw[0][:, 0:W_HALF], ACT.Copy).then_inc(s_whi0, 1)
            act.activation(whi[0][:, W_HALF:], raw[0][:, W_HALF:], ACT.Copy).then_inc(s_whi, 1)
            hi(1, 1, W_FULL, None)
            act.wait_ge(s_eps, 1)
            act.activation(t1[:, 0:8], eps[:], ACT.Sqrt)
            root(0)

            def e_hi(n):
                hi(n + 2, n % 2, W_FULL, (s_mm, E_AT[E_TILES[2 * n + 1]] + 1))

            e_hi(0)
            e_hi(1)
            act.wait_ge(s_z1, 2)
            act.activation(et[:], ex[:], ACT.Abs).then_inc(s_sp, 1)
            act.wait_ge(s_sp, 1)
            act.activation(et[:], et[:], ACT.Exp, scale=-1.0).then_inc(s_sp, 1)
            act.wait_ge(s_sp, 2)
            act.activation(et[:], et[:], ACT.Ln, bias=1.0).then_inc(s_sp, 1)
            e_hi(2)
            act.wait_ge(s_b, 3)
            act.activation(eb[:], et[:], ACT.Exp, scale=1.0 / 16).then_inc(s_eb, 1)
            act.activation(ex[:], et[:], ACT.Exp, scale=-1.0 / 16).then_inc(s_enb, 1)
            act.wait_ge(s_dl, 2)
            act.activation(ex[:, :, 0:NP_], ex[:, :, 0:NP_], ACT.Exp, scale=1.0 / 16).then_inc(s_edl, 1)
            e_hi(3)
            for b in range(BLK):
                act.wait_ge(s_vt, b + 1)
                act.activation(evtok[:, b, :], ax[b][:], ACT.Copy).then_inc(s_vtc, 1)
            e_hi(4)

            def silu_g(q):
                act.wait_ge(s_out, E_AT[f"g{q}"] + 1)
                act.activation(gsil[:, q, :], gsil[:, q, :], ACT.Silu).then_inc(s_gs, 1)

            def pool_hi(q):
                act.wait_ge(s_mm, E_AT[f"p{q}"] + 1)
                act.activation(halves(op_hi, 4 + q), mt(E_AT[f"p{q}"]), ACT.Copy,
                               scale=vec[:, V_PS + q:V_PS + q + 1]).then_inc(s_ophi, 1)

            for q in range(4):
                act.wait_ge(s_at, q + 1)
                act.activation(att[:, q].rearrange("p b n -> p (b n)"), ax[q][:], ACT.Copy).then_inc(s_atc, 1)
            for q in range(2):
                act.wait_ge(s_kt, q + 1)
                act.activation(kdtok[:, 2 * q:2 * q + 2, :].rearrange("p b n -> p (b n)"), ax[q][:],
                               ACT.Copy).then_inc(s_ktc, 1)
                if q == 0:
                    pool_hi(0)
            act.wait_ge(s_kt, 3)
            act.activation(evs[:], ax[2][0:NS, :], ACT.Copy).then_inc(s_ktc, 1)
            pool_hi(1)
            e_hi(5)

            silu_g(0)
            pool_hi(2)
            act.wait_ge(s_od, 1)
            for i in range(2):
                a = act.activation(ev[:, 2 * i:2 * i + 2, NP_:T],
                                   ax[3][:, 16 * i:16 * i + 16].rearrange("p (b r) -> p r b", r=2), ACT.Copy)
            a.then_inc(s_odc, 1)
            e_hi(6)
            for k in range(HEADS):
                act.wait_ge(s_o, k + 1)
                act.activation(ev[:, k, 0:NP_], ax[k][:], ACT.Copy).then_inc(s_oc, 1)
                if k == 1:
                    silu_g(1)
            pool_hi(3)
            act.wait_ge(s_oms, 4)
            act.activation(rt[:], ax[3][:, 64:84], ACT.Sqrt, bias=eps[:, 0:1], scale=8.0).then_inc(s_ort, 1)
            silu_g(2)

            def head_hi(q):
                act.wait_ge(s_og, q + 1)
                act.activation(op_hi[:, q, :], tmp[q][:], ACT.Copy).then_inc(s_ophi, 1)

            for q in range(3):
                head_hi(q)
            silu_g(3)
            head_hi(3)
            e_hi(7)
            for n in range(N_EO):
                for j in range(2):
                    h_hi(1, 2 * n + j, (s_out, M_EO + 2 * n + j + 1))
                hi(C_EO + n + 2, n % 2, W_FULL, (s_mm, M_EO + 2 * n + 2))

            def ffn(l):
                c0, m0, d0, dm = C_F[l], M_F[l], C_D[l], M_D[l]

                def pair(i, size, first=False):
                    for j in range(2):
                        n = 2 * i + j
                        g = FT * l + n
                        if first and j == 0:
                            root(1 + 2 * l)
                        act.wait_ge(s_out, m0 + 2 * n + 1)
                        want(act, s_hid, g)
                        act.activation(t1[:], t0[:], ACT.Silu).then_inc(s_sg, 1)
                        hi(c0 + n + 2, j, size, (s_mm, m0 + 2 * n + 2))
                        act.wait_ge(s_hid, g + 1)
                        settled()
                        act.activation(flat(hid_hi, n), t3[:], ACT.Copy).then_inc(s_hidhi, 1)

                pair(0, W_FULL, first=True)
                with act.Fori(1, N_F // 2 - 1) as i:
                    pair(i, W_FULL)
                pair(N_F // 2 - 1, W_DOWN)

                def down(m, size):
                    if size:
                        hi(d0 + 2 * m + 2, 0, size, (s_half, KT * l + m + 1))
                    if l == 0:
                        h_hi(2, m, (s_out, dm + m + 1))
                    if size:
                        hi(d0 + 2 * m + 3, 1, size, (s_mm, dm + m + 1))

                with act.Fori(0, KT - 1) as m:
                    down(m, W_DOWN)
                down(KT - 1, W_FULL if l == 0 else 0)

            ffn(0)

            act.wait_ge(s_mm, M_OI)
            act.activation(vsel[:], ones[:, 8:16], ACT.Copy).then_inc(r_sel, 1)
            act.wait_ge(s_out, M_OI)
            act.activation(osel[:], rstd[:, 0:P + NS], ACT.Copy, scale=0.0).then_inc(r_sel, 1)
            act.wait_ge(r_sel, 2)
            act.activation(osel[:, NS - 1:NS], ones[:, 1:2], ACT.Copy).then_inc(r_sel, 1)

            def finish_rows(hp):
                act.wait_ge(r_sg, 4 * hp + 4)
                act.wait_ge(r_os, 8 * hp + 8)
                act.activation(t2[0:NS, 0:512], ax[3][0:NS, :], ACT.Copy).then_inc(r_osr, 1)

            def finish_turned(hp):
                act.wait_ge(r_ot, hp + 1)
                settled()
                act.activation(o32[:, ds(4 * hp, 4), NP_:T], ax[3][:, 0:32].rearrange("p (d b) -> p d b", d=4),
                               ACT.Copy).then_inc(r_osc, 1)

            def finish_root(hp):
                act.wait_ge(r_ms, hp + 1)
                act.activation(rt[:, 0:5], ax[3][:, 64:69], ACT.Sqrt, bias=eps[:, 0:1], scale=2.0).then_inc(r_rt, 1)

            def finish_copy(hp):
                act.wait_ge(r_bc, hp + 1)
                act.activation(rs[:, 0:NP_], ax[2][:], ACT.Copy)
                act.activation(rs[:, NP_:T], ax[3][:, 72:72 + NS], ACT.Copy).then_inc(r_rc, 1)

            def decay(hh, b):
                n = 8 * hh + b
                act.wait_ge(r_in[b % 4], 16 * (2 * hh + b // 4 + 1))
                settled()
                act.activation(sring[:, b % 4].rearrange("p t n -> p (t n)"), sring[:, b % 4].rearrange("p t n -> p (t n)"),
                               ACT.Copy, scale=vec[:, ds(V_GM + hh, 1)]).then_inc(r_g, 1)

            def q_first(hh, b):
                act.wait_ge(r_sn, 8 * hh + b + 1)
                act.activation(qbuf[b % 2][:, 0:512], sring[:, b % 4, 0, :], ACT.Copy, scale=qs[:, 0, b:b + 1]).then_inc(r_ta, 1)

            def sum_hi(hh, b):
                want(act, r_os, 8 * hh + b)
                act.wait_ge(r_qs, 8 * hh + b + 1)
                act.activation(th[:], qbuf[b % 2][:, 0:512], ACT.Copy).then_inc(r_th, 1)

            def last_chunk(hp):
                hi(C_OI + 6 * hp + 7, 1, W_FULL, (s_mm, M_OI + 12 * hp + 12))

            def head(hh):
                m0 = M_OI + 12 * hh
                first = isinstance(hh, int) and hh == 0

                def chunk(n):
                    hi(C_OI + 6 * hh + n + 2, n % 2, W_FULL, (s_mm, m0 + 2 * n + 2))

                if first:
                    root(2)
                else:
                    sum_hi(hh - 1, 7)
                    last_chunk(hh - 1)
                    finish_rows(hh - 1)
                chunk(0)
                if not first:
                    finish_turned(hh - 1)
                chunk(1)
                if not first:
                    finish_root(hh - 1)
                for b in range(BLK):
                    act.wait_ge(r_tr, 7 * hh + b + 1)
                    act.activation(vtok[:, b, :], ax[b % 2][:], ACT.Copy).then_inc(r_vh, 1)
                    if b == 1:
                        chunk(2)
                    if b == 0 and not first:
                        finish_copy(hh - 1)
                chunk(3)
                act.wait_ge(r_tr, 7 * hh + 5)
                if first:
                    act.wait_ge(r_z, 1)
                act.activation(vs[0:NS, :], ax[3][0:NS, :], ACT.Copy).then_inc(r_vsc, 1)

                def prob_hi(j):
                    act.wait_ge(r_p, 4 * hh + j + 1)
                    a, b = PROB_AT[j], PROB_AT[j + 1]
                    act.activation(prob[:, a:b], prob_raw[:, a:b], ACT.Copy).then_inc(r_ph, 1)

                decay(hh, 0)
                decay(hh, 1)

                def silu(q):
                    act.wait_ge(s_out, m0 + 8 + q + 1)
                    if not first:
                        act.wait_ge(r_gd, 4 * hh)
                    act.activation(rg[:, q, :], tmp[q][:], ACT.Silu).then_inc(r_sg, 1)

                silu(0)
                q_first(hh, 0)
                prob_hi(0)
                prob_hi(1)
                decay(hh, 2)
                sum_hi(hh, 0)
                q_first(hh, 1)
                silu(1)
                prob_hi(2)
                prob_hi(3)
                decay(hh, 3)
                sum_hi(hh, 1)
                q_first(hh, 2)
                chunk(4)
                for q in range(2):
                    act.wait_ge(r_tr, 7 * hh + 6 + q)
                    settled()
                    for b in range(2):
                        a = act.activation(ktok[:, 2 * q + b, :], ax[q][:, 256 * b:256 * b + 256], ACT.Copy,
                                           scale=vec[:, ds(V_KS + 4 * hh + 2 * q + b, 1)])
                    a.then_inc(r_kh, 1)
                decay(hh, 4)
                sum_hi(hh, 2)
                q_first(hh, 3)
                silu(2)
                sum_hi(hh, 3)
                q_first(hh, 4)

                def pv(q):
                    act.wait_ge(r_pv, 4 * hh + q + 1)
                    settled()
                    act.activation(o32[:, ds(4 * hh + q, 1), 0:NP_].rearrange("p a n -> p (a n)"), ax[q % 2][:],
                                   ACT.Copy).then_inc(r_pvc, 1)

                def state(q):
                    act.wait_ge(r_st, 2 * hh + q + 1)
                    act.activation(rst[:, q, :], ax[q][:], ACT.Copy).then_inc(r_stc, 1)

                pv(0)
                decay(hh, 5)
                pv(1)
                silu(3)
                sum_hi(hh, 4)
                q_first(hh, 5)
                decay(hh, 6)
                pv(2)
                pv(3)
                sum_hi(hh, 5)
                q_first(hh, 6)
                decay(hh, 7)
                state(0)
                sum_hi(hh, 6)
                q_first(hh, 7)
                state(1)

            head(0)
            with act.Fori(1, HEADS) as hh:
                head(hh)

            def out_hi(n):
                k = OO_ORDER[n]
                act.activation(o_hi[:, k, :], o32[:, k, :], ACT.Copy).then_inc(s_ohi, 1)

            out_hi(0)
            sum_hi(HEADS - 1, 7)
            out_hi(1)
            out_hi(2)
            finish_rows(HEADS - 1)
            out_hi(3)
            out_hi(4)
            last_chunk(HEADS - 1)
            finish_turned(HEADS - 1)
            out_hi(5)
            out_hi(6)
            finish_root(HEADS - 1)
            out_hi(7)
            act.wait_ge(r_sto, 16 * HEADS)
            for n in range(8, 12):
                out_hi(n)
            finish_copy(HEADS - 1)
            for q in range(4):
                act.wait_ge(r_on, 4 * (HEADS - 1) + q + 1)
                out_hi(12 + q)
            with act.Fori(0, N_OO // 2) as i:
                hi(C_OO + 2 * i + 2, 0, W_FULL, (s_mm, M_OO + 2 * i + 1))
                h_hi(3, 2 * i, (s_out, M_OO + 2 * i + 1))
                h_hi(3, 2 * i + 1, (s_out, M_OO + 2 * i + 2))
                hi(C_OO + 2 * i + 3, 1, W_FULL, (s_mm, M_OO + 2 * i + 2))
            ffn(1)
            act.activation(t1[:, 0:8], eps[:], ACT.Sqrt)
            for m in Y_POOL:
                act.wait_ge(s_acc, 8 * 4 + m + 1)
                act.activation(x[:, m, :], x[:, m, :], ACT.Copy, scale=gain(4, m)).then_inc(s_xg, 1)
            act.wait_ge(s_ms, 5)
            act.activation(rt[:, 0:2], ax[3][:, 64:66], ACT.Sqrt, bias=eps[:, 0:1]).then_inc(s_rt, 1)
            act.wait_ge(s_bc, 5)
            act.activation(rstd[:, 0:2 * P], ax[2][:, 0:2 * P], ACT.Copy).then_inc(s_rstd, 1)
            act.wait_ge(s_ms, 6)
            act.activation(rt[:, 2:5], ax[0][:, 66:69], ACT.Sqrt, bias=eps[:, 0:1]).then_inc(s_rt, 1)
            act.wait_ge(s_bc, 6)
            act.activation(rstd[:, 2 * P:NP_], ax[1][:, 2 * P:NP_], ACT.Copy)
            act.activation(rstd[:, NP_:T], ax[0][:, 72:72 + NS], ACT.Copy).then_inc(s_rstd, 1)

        @block.vector
        def _(dve):
            def lo(c, slot, size):
                dve.wait_ge(s_whi, c + 1)
                dve.tensor_tensor(wlo[slot][:, 0:size], raw[slot][:, 0:size], whi[slot][:, 0:size].bitcast(F32),
                                  ALU.subtract).then_inc(s_wlo, 1)

            def h_lo(n, m):
                dve.wait_ge(s_hhi, 8 * n + m + 1)
                dve.scalar_tensor_tensor(out=flat(h[1], m), in0=flat(x, m), scalar=gain(n, m),
                                         in1=flat(h[0], m).bitcast(F32), op0=ALU.mult,
                                         op1=ALU.subtract).then_inc(s_hlo, 1)

            def invert(n):
                dve.wait_ge(s_rt, n + 1)
                dve.reciprocal(rr[:, 0:5], rt[:, 0:5]).then_inc(s_rr, 1)

            def taken(m, par, out, other=None, op=ALU.mult):
                dve.wait_ge(s_mm, m + 1)
                dve.tensor_tensor(out, ps[par][:, :, 0:HT], two(rstd) if other is None else other, op).then_inc(s_out, 1)

            dve.wait_ge(s_wah, 1)
            dve.tensor_tensor(wa_lo[:], wa_raw[:], wa_hi[:].bitcast(F32), ALU.subtract).then_inc(s_wal, 1)
            dve.wait_ge(s_vec, 16)
            for m in range(KT):
                h_lo(0, m)
            dve.wait_ge(s_whi0, 1)
            dve.tensor_tensor(wlo[0][:, 0:W_HALF], raw[0][:, 0:W_HALF], whi[0][:, 0:W_HALF].bitcast(F32),
                              ALU.subtract).then_inc(s_wlo0, 1)
            dve.wait_ge(s_whi, 1)
            dve.tensor_tensor(wlo[0][:, W_HALF:], raw[0][:, W_HALF:], whi[0][:, W_HALF:].bitcast(F32),
                              ALU.subtract).then_inc(s_wlo, 1)
            for m, t in ((KT - 2, t2), (KT - 1, t3)):
                dve.tensor_tensor(t[:], x[:, m, :], x[:, m, :], ALU.mult).then_inc(s_sq0, 1)
            lo(1, 1, W_FULL)
            invert(0)
            dve.wait_ge(s_rstd, 1)

            def e_take(name, out):
                i = E_AT[name]
                taken(i, i % 2, out)

            def z_tile(i):
                m = E_AT[f"z{i}"]
                dve.wait_ge(s_mm, m + 1)
                dve.tensor_scalar(halves(ex, i), mt(m), vec[:, V_BG + i:V_BG + i + 1], None, ALU.add).then_inc(s_out, 1)
                dve.wait_ge(s_out, m + 1)
                dve.sem_inc(s_z1, 1)

            e_take("q0", halves(eq, 0))
            dve.wait_ge(s_mm, E_AT["a"] + 1)
            for t in range(2):
                a = dve.tensor_tensor(a16[:, HT * t:HT * t + HT], ax[t][0:16, 0:HT], rstd[0:16, HT * t:HT * t + HT], ALU.mult)
            a.then_inc(s_out, 1)
            e_take("q1", halves(eq, 1))
            lo(2, 0, W_FULL)
            e_take("k0", halves(ek, 0))
            z_tile(0)
            e_take("k1", halves(ek, 1))
            lo(3, 1, W_FULL)
            z_tile(1)
            e_take("v0", halves(ev, 0))
            dve.wait_ge(s_sp, 3)
            dve.scalar_tensor_tensor(out=eb[:], in0=ex[:], scalar=0.0, in1=et[:], op0=ALU.min,
                                     op1=ALU.subtract).then_inc(s_la, 1)
            dve.wait_ge(s_la, 1)
            dve.wait_ge(s_reset, 16)
            for i in range(2):
                dve.tensor_tensor_scan(et[:, i, 0:NP_], reset[:], eb[:, i, 0:NP_], 0.0, ALU.mult, ALU.add).then_inc(s_b, 1)
            dve.tensor_copy(et[:, :, NP_:T], eb[:, :, NP_:T]).then_inc(s_b, 1)
            e_take("v1", halves(ev, 1))
            lo(4, 0, W_FULL)
            dve.wait_ge(s_eb, 1)
            dve.scalar_tensor_tensor(out=eq[:, :, 0:NP_], in0=eq[:, :, 0:NP_], scalar=0.125, in1=eb[:, :, 0:NP_],
                                     op0=ALU.mult, op1=ALU.mult).then_inc(s_qe, 1)
            dve.tensor_scalar(eq[:, :, NP_:T], eq[:, :, NP_:T], 0.125, None, ALU.mult).then_inc(s_qe, 1)
            dve.wait_ge(s_qz, 1)
            dve.wait_ge(s_qe, 2)
            for r in range(2):
                half = slice(CH * r, CH * r + CH)
                a = dve.tensor_copy(qmask[half, :, :, r], eq[half, :, NP_:T])
            a.then_inc(s_qm, 1)
            dve.tensor_copy(elast[:], eb[:, :, CH - 1:NP_:CH]).then_inc(s_qe, 1)
            dve.tensor_copy(eas[:], eb[:, :, NP_:T]).then_inc(s_qe, 1)
            dve.wait_ge(s_enb, 1)
            dve.tensor_tensor(ke[:, :, 0:NP_], ek[:, :, 0:NP_], ex[:, :, 0:NP_], ALU.mult).then_inc(s_ke, 1)
            dve.wait_ge(s_ke, 1)
            for i in range(2):
                dve.tensor_tensor(ex[:, i, 0:NP_].rearrange("p (c n) -> p c n", n=CH),
                                  et[:, i, CH - 1:NP_:CH].unsqueeze(2).to_broadcast([P, NCH, CH]),
                                  et[:, i, 0:NP_].rearrange("p (c n) -> p c n", n=CH), ALU.subtract).then_inc(s_dl, 1)
            e_take("v2", halves(ev, 2))
            dve.wait_ge(s_edl, 1)
            dve.tensor_tensor(ek[:, :, 0:NP_], ek[:, :, 0:NP_], ex[:, :, 0:NP_], ALU.mult).then_inc(s_kd, 1)
            dve.wait_ge(s_gsl, 16)
            dve.wait_ge(s_qe, 4)
            dve.tensor_tensor(gs[:].rearrange("p i b n -> p (i b) n"), gs[:].rearrange("p i b n -> p (i b) n"),
                              eas[:].rearrange("p i b -> p (i b)").unsqueeze(2).to_broadcast([P, 2 * NS, P]),
                              ALU.mult).then_inc(s_gsd, 1)
            e_take("v3", halves(ev, 3))
            lo(5, 1, W_FULL)

            pools = [0]

            def step(ins):
                pools[0] += 1
                ins.then_inc(s_pl, 1)
                dve.wait_ge(s_pl, pools[0])

            def pool_group(g):
                u, wdw = tmp[g % 2], 2 << g
                pooled = (rs, acc)[g % 2]
                dve.wait_ge(s_out, E_AT[f"u{g}"] + 1)
                if g == 0:
                    dve.wait_ge(s_pbuf, 16)
                    dve.wait_ge(s_invc, 16)
                if g >= 2:
                    dve.wait_ge(s_mm, E_AT[f"p{g - 2}"] + 1)
                dve.tensor_copy(pout[:, g, NS, :], u[:, NP_ - 15:NP_])
                dve.tensor_copy(pout[:, g, 0:NS, 14:15].rearrange("p b n -> p (b n)"), u[:, NP_:T])
                dve.tensor_copy(pout[:, g, 0:NS, 0:14], pbuf[:, g, :, 1:15]).then_inc(s_rows, 1)
                cur = u
                for lv in range(g + 1):
                    d, nxt = 1 << lv, (t2, t3)[lv % 2]
                    dve.tensor_copy(nxt[:, 0:d], cur[:, 0:d])
                    step(dve.tensor_tensor(nxt[:, d:NP_], cur[:, d:NP_], cur[:, 0:NP_ - d], ALU.add))
                    cur = nxt
                dve.scalar_tensor_tensor(out=pooled[:, 16:NP_], in0=cur[:, 16:NP_], scalar=1.0 / wdw, in1=u[:, 16:NP_],
                                         op0=ALU.mult, op1=ALU.subtract)
                step(dve.tensor_tensor(cur[:, 0:16], cur[:, 0:16], invc[:, g, :], ALU.mult))
                dve.tensor_tensor(pooled[:, 0:16], cur[:, 0:16], u[:, 0:16], ALU.subtract)
                step(dve.tensor_reduce(cur[:, 16:24], pbuf[:, g, :, 16 - wdw:15], mybir.AxisListType.X, ALU.add))
                step(dve.tensor_tensor(cur[:, 16:24], cur[:, 16:24], u[:, NP_:T], ALU.add))
                dve.scalar_tensor_tensor(out=pooled[:, NP_:T], in0=cur[:, 16:24], scalar=1.0 / wdw, in1=u[:, NP_:T],
                                         op0=ALU.mult, op1=ALU.subtract).then_inc(s_pm, 1)

            def pool_lo(q):
                dve.wait_ge(s_ophi, q + 1)
                m = E_AT[f"p{q}"]
                dve.scalar_tensor_tensor(out=halves(op_lo, 4 + q), in0=mt(m), scalar=vec[:, V_PS + q:V_PS + q + 1],
                                         in1=halves(op_hi, 4 + q).bitcast(F32), op0=ALU.mult, op1=ALU.subtract)\
                   .then_inc(s_out, 1)
                dve.wait_ge(s_out, m + 1)
                dve.sem_inc(s_oplo, 1)

            e_take("u0", two(tmp[0]))
            pool_group(0)
            e_take("u1", two(tmp[1]))
            lo(6, 0, W_FULL)
            pool_group(1)
            pool_lo(0)
            e_take("u2", two(tmp[0]))
            pool_group(2)
            pool_lo(1)
            e_take("u3", two(tmp[1]))
            lo(7, 1, W_FULL)
            for b in range(NS):
                dve.wait_ge(s_vb, b // 2 + 1)
                for i in range(2):
                    dve.scalar_tensor_tensor(out=gs[:, i, b, :],
                                             in0=ax[b // 2][:, 256 * (b % 2) + 128 * i:256 * (b % 2) + 128 * i + 128],
                                             scalar=ek[:, i, NP_ + b:NP_ + b + 1], in1=gs[:, i, b, :], op0=ALU.mult,
                                             op1=ALU.add).then_inc(s_dn, 1)
            e_take("g0", halves(gsil, 0))
            dve.wait_ge(s_kd, 1)
            dve.wait_ge(s_u, 4)
            n = 0
            for c in range(NCH):
                for i in range(2):
                    u = ax[2 * i + c % 2][:, 128 * (c // 2):128 * (c // 2) + 128]
                    if c == 0:
                        dve.tensor_copy(states[:, i, 0, :], u).then_inc(s_st, 1)
                    else:
                        dve.wait_ge(s_st, n - 1)
                        dve.scalar_tensor_tensor(out=states[:, i, c, :], in0=states[:, i, c - 1, :],
                                                 scalar=elast[:, i, c:c + 1], in1=u, op0=ALU.mult,
                                                 op1=ALU.add).then_inc(s_st, 1)
                    n += 1
            pool_group(3)

            pool_lo(2)
            e_take("g1", halves(gsil, 1))
            lo(8, 0, W_FULL)
            pool_lo(3)
            dve.wait_ge(s_ort, 1)
            dve.reciprocal(rr[:], rt[:]).then_inc(s_orr, 1)
            e_take("g2", halves(gsil, 2))

            def head_gate(q):
                dve.wait_ge(s_obc, q + 1)
                dve.scalar_tensor_tensor(out=ev[:, q, 0:NP_], in0=ev[:, q, 0:NP_], scalar=vec[:, V_GLA:V_GLA + 1],
                                         in1=ax[q % 3][:], op0=ALU.mult, op1=ALU.mult)
                dve.scalar_tensor_tensor(out=ev[:, q, NP_:T], in0=ev[:, q, NP_:T], scalar=vec[:, V_GLA:V_GLA + 1],
                                         in1=ax[3][:, 96 + 8 * q:104 + 8 * q], op0=ALU.mult, op1=ALU.mult).then_inc(s_on, 1)
                dve.wait_ge(s_on, q + 1)
                dve.wait_ge(s_gs, q + 1)
                dve.tensor_tensor(tmp[q][:], ev[:, q, :], gsil[:, q, :], ALU.mult).then_inc(s_og, 1)

            def head_lo(q):
                dve.wait_ge(s_ophi, 5 + q)
                dve.tensor_tensor(op_lo[:, q, :], tmp[q][:], op_hi[:, q, :].bitcast(F32), ALU.subtract).then_inc(s_oplo, 1)

            head_gate(0)
            head_gate(1)
            head_lo(0)
            head_gate(2)
            head_lo(1)
            e_take("g3", halves(gsil, 3))
            head_lo(2)
            head_gate(3)
            head_lo(3)
            lo(9, 1, W_FULL)

            def residual(m, par, row):
                taken(m, par, halves(x, row), halves(x, row), ALU.add)

            for n in range(N_EO):
                for j in range(2):
                    m = 2 * n + j
                    residual(M_EO + m, (M_EO + m) % 2, m)
                    h_lo(1, m)
                lo(C_EO + n + 2, n % 2, W_FULL)

            def ffn(l):
                c0, m0, d0, dm = C_F[l], M_F[l], C_D[l], M_D[l]

                def pair(i, size, first=False):
                    for j in range(2):
                        n = 2 * i + j
                        g = FT * l + n
                        if first and j == 0:
                            invert(1 + 2 * l)
                            dve.wait_ge(s_rstd, 2 + 2 * l)
                            if l == 0:
                                dve.wait_ge(s_es, 48)
                            else:
                                for q in range(4):
                                    dve.wait_ge(r_so[q], 16 * HEADS * NS // 4)
                        want(dve, s_sg, g)
                        taken(m0 + 2 * n, m0 % 2, two(t0))
                        taken(m0 + 2 * n + 1, (m0 + 1) % 2, two(t2))
                        dve.wait_ge(s_out, m0 + 2 * n + 2)
                        dve.wait_ge(s_sg, g + 1)
                        want(dve, s_hidhi, g)
                        dve.tensor_tensor(t3[:], t2[:], t1[:], ALU.mult).then_inc(s_hid, 1)
                        lo(c0 + n + 2, j, size)
                        dve.wait_ge(s_hidhi, g + 1)
                        dve.tensor_tensor(flat(hid_lo, n), t3[:], flat(hid_hi, n).bitcast(F32),
                                          ALU.subtract).then_inc(s_hidlo, 1)

                pair(0, W_FULL, first=True)
                with dve.Fori(1, N_F // 2 - 1) as i:
                    pair(i, W_FULL)
                pair(N_F // 2 - 1, W_DOWN)

                def down(m, par, size):
                    if size:
                        lo(d0 + 2 * m + 2, 0, size)
                    residual(dm + m, par, m)
                    if l == 0:
                        h_lo(2, m)
                    if size:
                        lo(d0 + 2 * m + 3, 1, size)

                with dve.Fori(0, KT // 2 - 1) as i:
                    for j in range(2):
                        down(2 * i + j, (dm + j) % 2, W_DOWN)
                down(KT - 2, dm % 2, W_DOWN)
                if l == 0:
                    down(KT - 1, (dm + 1) % 2, W_FULL)

            ffn(0)

            def finish_invert(hp):
                dve.wait_ge(r_rt, hp + 1)
                dve.reciprocal(rr[:, 0:5], rt[:, 0:5]).then_inc(r_rr, 1)

            def finish_gate(hp, q):
                o = flat(o32, 4 * hp + q)
                dve.wait_ge(r_acc, 5 * hp + 5)
                dve.wait_ge(r_sg, 4 * hp + q + 1)
                dve.tensor_tensor(o, o, flat(rg, q), ALU.mult).then_inc(r_gd, 1)

            def finish_norm(hp, q):
                o = flat(o32, 4 * hp + q)
                dve.wait_ge(r_rc, hp + 1)
                dve.wait_ge(r_gd, 4 * hp + q + 1)
                dve.tensor_tensor(o, o, rs[:], ALU.mult).then_inc(r_on, 1)

            def new_state(hh, b):
                dve.wait_ge(r_vb, 8 * hh + b + 1)
                dve.wait_ge(r_g, 8 * hh + b + 1)
                dve.wait_ge(r_ks, hh + 1)
                for t in range(2):
                    a = dve.scalar_tensor_tensor(out=sring[:, b % 4, t, :], in0=ax[2][:], scalar=ks[:, t, b:b + 1],
                                                 in1=sring[:, b % 4, t, :], op0=ALU.mult, op1=ALU.add)
                a.then_inc(r_sn, 1)

            def q_sum(hh, b):
                dve.wait_ge(r_ta, 8 * hh + b + 1)
                buf = qbuf[b % 2][:, 0:512]
                dve.scalar_tensor_tensor(out=buf, in0=sring[:, b % 4, 1, :], scalar=qs[:, 1, b:b + 1], in1=buf,
                                         op0=ALU.mult, op1=ALU.add).then_inc(r_qs, 1)

            def sum_lo(hh, b):
                want(dve, r_os, 8 * hh + b)
                dve.wait_ge(r_th, 8 * hh + b + 1)
                dve.tensor_tensor(tl[:], qbuf[b % 2][:, 0:512], th[:].bitcast(F32), ALU.subtract).then_inc(r_tl, 1)

            def head(hh):
                m0 = M_OI + 12 * hh
                first = isinstance(hh, int) and hh == 0

                def chunk(n):
                    lo(C_OI + 6 * hh + n + 2, n % 2, W_FULL)

                if first:
                    invert(2)
                    dve.wait_ge(s_rstd, 3)
                    dve.wait_ge(r_cs, 16)
                    for i in range(2):
                        dve.tensor_tensor(cs[:, i, :], cs[:, i, :], rstd[:], ALU.mult).then_inc(r_csr, 1)
                for t in range(4):
                    if t == 2 and not first:
                        dve.wait_ge(r_os, 8 * hh)
                    if t == 0 and not first:
                        sum_lo(hh - 1, 7)
                    taken(m0 + t, (M_OI + t) % 2, halves(rv, t))
                    if t == 0 and not first:
                        lo(C_OI + 6 * (hh - 1) + 7, 1, W_FULL)
                    if t == 1:
                        chunk(0)
                    if t == 3:
                        chunk(1)
                dve.wait_ge(r_csr, 2)
                if first:
                    dve.wait_ge(s_xs, 16)
                if not first:
                    finish_invert(hh - 1)

                def v_lo(b):
                    dve.wait_ge(r_vh, 4 * hh + b + 1)
                    dve.tensor_tensor(vtok_lo[:, b, :], ax[b % 2][:], vtok[:, b, :].bitcast(F32), ALU.subtract).then_inc(r_trc, 1)

                def rope(t, dst, k):
                    want(dve, r_rot, 4 * hh + 2 * k)
                    want(dve, r_sg, 4 * hh)
                    for u in range(2):
                        dve.wait_ge(s_mm, m0 + t + u + 1)
                        src = ps[(M_OI + t + u) % 2][:, :, 0:HT]
                        dve.tensor_tensor(two(tmp[u]), src, halves(cs, 0), ALU.mult)
                        dve.tensor_tensor(two(tmp[2 + u]), src, halves(cs, 1), ALU.mult).then_inc(s_out, 1)
                        if k == 0 and u == 0:
                            v_lo(0)
                            v_lo(1)
                        if k == 1 and u == 0 and not first:
                            for q in range(4):
                                finish_gate(hh - 1, q)
                            finish_norm(hh - 1, 0)
                            finish_norm(hh - 1, 1)
                    if k == 0:
                        want(dve, r_stc, 2 * hh)
                    dve.wait_ge(s_out, m0 + t + 2)
                    dve.tensor_tensor(dst[:, 0, :], t0[:], t3[:], ALU.subtract).then_inc(r_rot, 1)
                    dve.tensor_tensor(dst[:, 1, :], t1[:], t2[:], ALU.add).then_inc(r_rot, 1)

                rope(4, rq, 0)
                v_lo(2)
                v_lo(3)
                chunk(2)
                if not first:
                    dve.wait_ge(r_sto, 16 * hh)
                rope(6, rk, 1)
                chunk(3)
                dve.wait_ge(r_rot, 4 * hh + 4)
                dve.tensor_copy(qs[:], rq[:, :, NP_:T])
                dve.tensor_scalar(ks[:], rk[:, :, NP_:T], 1.0 / 16, None, ALU.mult).then_inc(r_ks, 1)
                dve.wait_ge(r_vsc, hh + 1)
                dve.wait_ge(r_z, 1)
                dve.tensor_tensor(vs[32:32 + NS, :], ax[3][0:NS, :], vs[0:NS, :].bitcast(F32), ALU.subtract).then_inc(r_vl, 1)
                if not first:
                    finish_norm(hh - 1, 2)
                    finish_norm(hh - 1, 3)

                def g_tile(q):
                    taken(m0 + 8 + q, (M_OI + q) % 2, two(tmp[q]))

                def probs(j):
                    dve.wait_ge(r_sc, 4 * hh + j + 1)
                    dve.wait_ge(r_d, 16 * (hh + 1))
                    n = NP_ - P * j
                    dve.tensor_tensor(prob_raw[:, PROB_AT[j]:PROB_AT[j + 1]], ax[j % 2][:, 0:n], dec[:, 0:n],
                                      ALU.mult).then_inc(r_p, 1)

                def probs_lo(j):
                    dve.wait_ge(r_ph, 4 * hh + j + 1)
                    a, b = PROB_AT[j], PROB_AT[j + 1]
                    dve.tensor_tensor(prob_lo[:, a:b], prob_raw[:, a:b], prob[:, a:b].bitcast(F32),
                                      ALU.subtract).then_inc(r_pl, 1)

                def k_lo(q):
                    dve.wait_ge(r_kh, 2 * hh + q + 1)
                    for b in range(2):
                        i = 2 * q + b
                        a = dve.scalar_tensor_tensor(out=ktok_lo[:, i, :], in0=ax[q][:, 256 * b:256 * b + 256],
                                                     scalar=vec[:, ds(V_KS + 4 * hh + i, 1)],
                                                     in1=ktok[:, i, :].bitcast(F32), op0=ALU.mult, op1=ALU.subtract)
                    a.then_inc(r_ktc, 1)

                g_tile(0)
                probs(0)
                probs(1)
                new_state(hh, 0)
                q_sum(hh, 0)
                probs_lo(0)
                probs_lo(1)

                def sequence(b):
                    new_state(hh, b)
                    sum_lo(hh, b - 1)
                    q_sum(hh, b)

                sequence(1)
                g_tile(1)
                probs(2)
                probs(3)
                sequence(2)
                probs_lo(2)
                probs_lo(3)
                chunk(4)
                sequence(3)
                k_lo(0)
                k_lo(1)
                g_tile(2)
                sequence(4)
                g_tile(3)
                sequence(5)
                sequence(6)
                sequence(7)

            head(0)
            with dve.Fori(1, HEADS) as hh:
                head(hh)

            def out_lo(n):
                k = OO_ORDER[n]
                dve.wait_ge(s_ohi, n + 1)
                dve.tensor_tensor(o_lo[:, k, :], o32[:, k, :], o_hi[:, k, :].bitcast(F32), ALU.subtract).then_inc(s_olo, 1)

            out_lo(0)
            sum_lo(HEADS - 1, 7)
            for n in range(1, 5):
                out_lo(n)
            lo(C_OO + 1, 1, W_FULL)
            out_lo(5)
            for q in range(4):
                finish_gate(HEADS - 1, q)
            out_lo(6)
            finish_invert(HEADS - 1)
            for n in range(7, 12):
                out_lo(n)
            finish_norm(HEADS - 1, 0)
            for q in range(1, 4):
                finish_norm(HEADS - 1, q)
                out_lo(11 + q)
            out_lo(15)
            with dve.Fori(0, N_OO // 2) as i:
                for j in range(2):
                    n = 2 * i + j
                    dve.wait_ge(s_xl, 16)
                    residual(M_OO + n, (M_OO + j) % 2, n)
                    if j == 0:
                        lo(C_OO + n + 2, 0, W_FULL)
                    h_lo(3, n)
                    if j == 1:
                        lo(C_OO + n + 2, 1, W_FULL)
            ffn(1)
            def last_squares(part, c0, c1):
                dve.wait_ge(*((s_half, 2 * KT), (s_mm, M_D[1] + KT))[part])
                dve.tensor_tensor(x[:, KT - 1, c0:c1], ps[(M_D[1] + KT - 1) % 2][:, part, 0:HT], x[:, KT - 1, c0:c1],
                                  ALU.add).then_inc(s_x7, 1)
                dve.wait_ge(s_x7, part + 1)
                dve.wait_ge(s_acc, 8 * 4 + 7)
                dve.tensor_tensor(sq[:, c0:c1], x[:, KT - 1, c0:c1], x[:, KT - 1, c0:c1], ALU.mult).then_inc(s_sql, 1)

            for part, (a, b, blocks) in enumerate(Y_PARTS):
                last_squares(part, HT * part, HT * part + HT)
                dve.wait_ge(s_rt, 5 + part)
                dve.reciprocal(rr[:, blocks[0]:blocks[-1] + 1], rt[:, blocks[0]:blocks[-1] + 1]).then_inc(s_rr, 1)
                dve.wait_ge(s_rstd, 5 + part)
                for m in Y_DVE:
                    dve.scalar_tensor_tensor(out=x[:, m, a:b], in0=x[:, m, a:b], scalar=gain(4, m), in1=rstd[:, a:b],
                                             op0=ALU.mult, op1=ALU.mult).then_inc(s_y, 1)

        @block.gpsimd
        def _(pool):
            pool.memset(eps[:], EPS).then_inc(s_eps, 1)
            pool.memset(qmask[:], 0.0).then_inc(s_qz, 1)

            def squares(n, m, ready):
                pool.wait_ge(*ready)
                if m == 0:
                    if n:
                        pool.wait_ge(s_ms, n)
                    pool.tensor_tensor(acc[:], x[:, m, :], x[:, m, :], ALU.mult).then_inc(s_acc, 1)
                elif n == 0 and m >= KT - 2:
                    pool.wait_ge(s_acc, m)
                    pool.wait_ge(s_sq0, m - (KT - 2) + 1)
                    pool.tensor_tensor(acc[:], acc[:], (t2, t3)[m % 2][:], ALU.add).then_inc(s_acc, 1)
                else:
                    pool.wait_ge(s_acc, 8 * n + m)
                    pool.tensor_tensor(sq[:], x[:, m, :], x[:, m, :], ALU.mult).then_inc(s_sq, 1)
                    pool.wait_ge(s_sq, 7 * n + m - (2 if n else 0))
                    pool.tensor_tensor(acc[:], acc[:], sq[:], ALU.add).then_inc(s_acc, 1)

            for m in range(KT):
                squares(0, m, (s_x[m // 2], 16))
            for q in range(HEADS):
                pool.wait_ge(s_atc, q + 1)
                pool.affine_select(out=att[:, q], in_=att[:, q], compare_op=ALU.is_ge, fill=0.0, base=0,
                                   pattern=[[0, BLK], [1, P]], channel_multiplier=-1).then_inc(s_am, 1)
                pool.wait_ge(s_am, 2 * q + 1)
                pool.memset(att[0:CH, q, :, CH:P], 0.0).then_inc(s_am, 1)
            pool.wait_ge(s_dn, 2 * NS)
            pool.dma_start(io["gla_s"], gs[:]).then_inc(s_es, 16)
            pool.wait_ge(s_st, 2 * NCH)
            pool.dma_start(io["gla_p"], states[:, :, NCH - 1, :]).then_inc(s_es, 16)
            pool.wait_ge(s_rows, 4)
            pool.dma_start(io["rows"], pout[:]).then_inc(s_es, 16)
            pool.wait_ge(s_odc, 1)
            for q in range(HEADS):
                pool.wait_ge(s_oc, q + 1)
                if q == 1:
                    pool.wait_ge(s_pm, 3)
                if q > 1:
                    pool.wait_ge(s_mm, E_AT[f"p{q}"] + 1)
                pool.tensor_tensor(osq[q][:], ev[:, q, :], ev[:, q, :], ALU.mult).then_inc(s_osq, 1)
            pool.wait_ge(s_oms, 4)
            for n, m0 in ((1, M_EO), (2, M_D[0])):
                for m in range(KT):
                    squares(n, m, (s_out, m0 + m + 1))

            def dec_load(hh, b):
                pool.dma_start(sring[:, b % 4, :, :].rearrange("p t n -> p (t n)"),
                               io["ret_in"][ds(4 * b + hh, 1)].rearrange("a p n -> p (a n)")).then_inc(r_in[b % 4], 16)

            def squares_prompt(hh, q):
                src = o32[:, ds(4 * hh + q, 1), 0:NP_].rearrange("p a n -> p (a n)")
                if q == 0:
                    pool.wait_ge(r_sg, 4 * hh + 4)
                else:
                    pool.wait_ge(r_acc, 5 * hh + q)
                pool.wait_ge(r_pvc, 4 * hh + q + 1)
                dst = (t1 if q else t0)[:, 0:NP_]
                pool.tensor_tensor(dst, src, src, ALU.mult).then_inc(r_sq if q else r_acc, 1)
                if q:
                    pool.wait_ge(r_sq, 5 * hh + q)
                    pool.tensor_tensor(t0[:, 0:NP_], t0[:, 0:NP_], t1[:, 0:NP_], ALU.add).then_inc(r_acc, 1)

            def squares_decode(hp):
                pool.wait_ge(r_acc, 5 * hp + 4)
                pool.wait_ge(r_osc, hp + 1)
                src = o32[:, ds(4 * hp, 4), NP_:T]
                pool.tensor_tensor(t1[:, 0:4 * NS].rearrange("p (d b) -> p d b", d=4), src, src, ALU.mult).then_inc(r_sq, 1)
                pool.wait_ge(r_sq, 5 * hp + 4)
                pool.tensor_tensor(t1[:, 4 * NS:6 * NS], t1[:, 0:2 * NS], t1[:, 2 * NS:4 * NS], ALU.add).then_inc(r_sq, 1)
                pool.wait_ge(r_sq, 5 * hp + 5)
                pool.tensor_tensor(t0[:, NP_:T], t1[:, 4 * NS:5 * NS], t1[:, 5 * NS:6 * NS], ALU.add).then_inc(r_acc, 1)

            def head(hh, last=False):
                first = isinstance(hh, int) and hh == 0
                if not first:
                    squares_decode(hh - 1)
                for b in range(NS):
                    pool.wait_ge(r_sn, 8 * hh + b + 1)
                    pool.sem_inc(s_pstep, 1)
                    pool.dma_start(io["ret_s"][ds(4 * b + hh, 1)].rearrange("a p n -> p (a n)"),
                                   sring[:, b % 4, :, :].rearrange("p t n -> p (t n)")).then_inc(r_so[b % 4], 16)
                    if b + 3 < NS or not last:
                        if b or not first:
                            pool.wait_ge(r_so[(b + 3) % 4], 16 * (2 * hh + (b + 3) // 4))
                            pool.wait_ge(r_qs, 8 * hh + b)
                            pool.sem_inc(s_pstep, 1)
                        dec_load(hh + (b + 3) // NS, (b + 3) % NS)
                    if b == 1 and not last:
                        pool.wait_ge(r_p, 4 * hh + 4)
                        pool.sem_inc(s_pstep, 1)
                        pool.dma_start(dec[:], io["dec"][ds(hh + 1, 1)].rearrange("a p n -> p (a n)")).then_inc(r_d, 16)
                    for q in {5: (0, 1), 6: (2,), 7: (3,)}.get(b, ()):
                        squares_prompt(hh, q)
                pool.wait_ge(r_stc, 2 * hh + 2)
                pool.sem_inc(s_pstep, 1)
                pool.dma_start(io["ret_p"][ds(hh, 1)].rearrange("a p n -> p (a n)"),
                               rst[:].rearrange("p t n -> p (t n)")).then_inc(r_sto, 16)

            pool.wait_ge(s_mm, M_OI)
            pool.memset(vs[:].bitcast(F32), 0.0).then_inc(r_z, 1)
            pool.dma_start(dec[:], io["dec"][0]).then_inc(r_d, 16)
            for b in range(3):
                dec_load(0, b)
            pool.wait_ge(s_ms, 3)
            head(0)
            with pool.Fori(1, HEADS - 1) as hh:
                head(hh)
            head(HEADS - 1, last=True)
            squares_decode(HEADS - 1)
            pool.wait_ge(r_ms, 4)
            for n, m0 in ((3, M_OO), (4, M_D[1])):
                for m in range(KT if n == 3 else KT - 1):
                    squares(n, m, (s_out, m0 + m + 1))
            pool.wait_ge(s_xg, len(Y_POOL))
            for part, (a, b, _) in enumerate(Y_PARTS):
                pool.wait_ge(s_rstd, 5 + part)
                for m in Y_POOL:
                    pool.tensor_tensor(x[:, m, a:b], x[:, m, a:b], rstd[:, a:b], ALU.mult).then_inc(s_yp, 1)

        @block.tensor
        def _(pe):
            def product(m, par, ks_, lhs, rhs, first, last, before=None, after=None, count=True, banks=None, free=None):
                dst = banks or [ps[par][:, t, 0:HT] for t in range(2)]
                if first:
                    want(pe, s_out, m - 1 if free is None else free)
                for n, (kw, kx) in enumerate(ks_):
                    if before:
                        before(kx)
                    for q, (a, b) in enumerate(((0, 0), (0, 1), (1, 0))):
                        for t in range(2):
                            ins = pe.matmul(dst[t], lhs(a, kw), rhs[b][:, kx, HT * t:HT * t + HT],
                                            start=(first and n == 0 and q == 0), stop=(last and n == len(ks_) - 1 and q == 2))
                    if after:
                        after(n)
                if count:
                    ins.then_inc(s_mm if last else s_half, 1)

            def weights(slot, col, cols, rows=None):
                def lhs(a, k):
                    return (whi, wlo)[a][slot][:, k * cols + col:k * cols + col + P]
                return lhs

            KS = [(k, k) for k in range(KT)]

            def mean_square(src, col, sem_):
                for i, (a, _, _) in enumerate(BLOCKS):
                    ins = pe.matmul(ax[3][:, col + i:col + i + 1], src[:, a:a + P], ones[:, 0:1], start=True, stop=True)
                ins.then_inc(sem_, 1)

            def spread_blocks(bank, col, rcol, blocks):
                for i in blocks:
                    a, c, n = BLOCKS[i]
                    dst = ax[bank][:, a:a + P] if i < BLK else ax[3][:, col:col + NS]
                    ins = pe.matmul(dst, rr[:, rcol + i:rcol + i + 1].to_broadcast([P, P]), ident[:, c:c + n],
                                    start=True, stop=True)
                return ins

            def spread(bank, col, rcol, sem_):
                spread_blocks(bank, col, rcol, range(BLK + 1)).then_inc(sem_, 1)

            def norm_sum(n):
                pe.wait_ge(s_acc, 8 * n + 8)
                if n == 0:
                    pe.wait_ge(s_ones, 16)
                    pe.wait_ge(s_id, 16)
                mean_square(acc, 64, s_ms)

            def norm_spread(n):
                pe.wait_ge(s_rr, n + 1)
                spread(2, 72, 0, s_bc)

            pe.wait_ge(s_wal, 1)

            def h_ready(n):
                return lambda k: pe.wait_ge(s_hlo, 8 * n + k + 1)

            def wa(a, k):
                return (wa_hi, wa_lo)[a][:, k * P:k * P + P]

            def e_tile(name):
                m = E_AT[name]
                if name == "a":
                    product(m, m % 2, KS, wa, h, True, True, before=h_ready(0), banks=[ax[t][:, 0:HT] for t in range(2)])
                elif name[0] == "z":
                    i = int(name[1])
                    want(pe, s_out, m - 1)
                    if i == 0:
                        pe.wait_ge(s_wgb, 16)
                        pe.wait_ge(s_out, 2)
                    for t in range(2):
                        ins = pe.matmul(ps[m % 2][:, t, 0:HT], wgb[:, P * i:P * i + P], a16[:, HT * t:HT * t + HT],
                                        start=True, stop=True)
                    ins.then_inc(s_mm, 1)
                elif name[0] == "p":
                    g = int(name[1])
                    want(pe, s_out, m - 1)
                    if g == 0:
                        pe.wait_ge(s_poolw, 16)
                    pe.wait_ge(s_pm, g + 1)
                    src = (rs, acc)[g % 2]
                    for t in range(2):
                        ins = pe.matmul(ps[m % 2][:, t, 0:HT], poolw[:, g, :], src[:, HT * t:HT * t + HT],
                                        start=True, stop=True)
                    ins.then_inc(s_mm, 1)
                else:
                    i = E_TILES.index(name)
                    c = i // 2
                    before = None
                    if name == "q0":
                        before = lambda k: pe.wait_ge(*((s_wlo0, 1) if k < KT // 2 else (s_wlo, 1)))
                    else:
                        pe.wait_ge(s_wlo, c + 1)
                    after = {"q1": lambda k: {NORM_0_AFTER[0]: norm_sum, NORM_0_AFTER[1]: norm_spread}
                                   .get(k, lambda n: None)(0),
                             "g1": lambda k: gla_dec_out(k - 4) if k >= 4 else None,
                             "g2": lambda k: gla_sum(GLA_SUM_AFTER.index(k)) if k in GLA_SUM_AFTER else None,
                             "g3": lambda k: gla_spread(GLA_SPREAD_AFTER.index(k)) if k in GLA_SPREAD_AFTER else None}\
                        .get(name)
                    product(m, m % 2, KS, weights(c % 2, P * (i % 2), 256), h, True, True, before=before,
                            after=after, free={"q1": 0, "k0": 1}.get(name))

            def gla_turn_v():
                for b in range(BLK):
                    pe.wait_ge(s_out, E_AT["v3"] + 1)
                    if b == 3:
                        pe.wait_ge(s_rstd, 1)
                    for q in range(4):
                        ins = pe.transpose(ax[b][:, P * q:P * q + P], ev[:, q, P * b:P * b + P], ident[:])
                    ins.then_inc(s_vt, 1)

            def gla_att():
                pe.wait_ge(s_qe, 2)
                pe.wait_ge(s_ke, 1)
                for q in range(HEADS):
                    pe.wait_ge(s_vtc, q + 1)
                    r = 64 * (q % 2)
                    for b in range(BLK):
                        ins = pe.matmul(ax[q][:, P * b:P * b + P], ke[r:r + 64, q // 2, P * b:P * b + P],
                                        eq[r:r + 64, q // 2, P * b:P * b + P], start=True, stop=True)
                    ins.then_inc(s_at, 1)

            def gla_turn_k():
                pe.wait_ge(s_kd, 1)
                for q in range(2):
                    pe.wait_ge(s_atc, q + 1)
                    for b in range(2):
                        for i in range(2):
                            ins = pe.transpose(ax[q][:, 256 * b + P * i:256 * b + P * i + P],
                                               ek[:, i, P * (2 * q + b):P * (2 * q + b) + P], ident[:])
                    ins.then_inc(s_kt, 1)
                pe.wait_ge(s_atc, 3)
                for q in range(4):
                    ins = pe.transpose(ax[2][0:NS, P * q:P * q + P], ev[:, q, NP_:T], ident[:])
                ins.then_inc(s_kt, 1)

            def gla_spread_v():
                pe.wait_ge(s_ktc, 3)
                pe.wait_ge(s_atc, 4)
                pe.wait_ge(s_gsd, 1)
                for b in range(NS):
                    for r in range(2):
                        v = evs[:].rearrange("p (i r n) -> p i r n", i=2, r=2)[:, :, r, :]
                        ins = pe.matmul(ax[b // 2][64 * r:64 * r + 64, 256 * (b % 2):256 * (b % 2) + 256],
                                        ident[0:NS, b:b + 1].to_broadcast([NS, 64]), v, start=True, stop=True)
                    if b % 2:
                        ins.then_inc(s_vb, 1)

            def gla_chunk_kv():
                pe.wait_ge(s_dn, 2 * NS)
                for i in range(2):
                    for par in range(2):
                        rows = slice(64 * par, 64 * par + 64)
                        for b in range(BLK):
                            for r in range(2):
                                q = 2 * i + r
                                ins = pe.matmul(ax[2 * i + par][64 * r:64 * r + 64, P * b:P * b + P],
                                                kdtok[rows, b, 64 * q:64 * q + 64], evtok[rows, b, P * q:P * q + P],
                                                start=True, stop=True)
                        ins.then_inc(s_u, 1)

            def gla_out():
                pe.wait_ge(s_st, 2 * NCH)
                for q in range(HEADS):
                    pe.wait_ge(s_am, 2 * q + 2)
                    if q == 3:
                        pe.wait_ge(s_odc, 1)
                    r = 64 * (q % 2)
                    for b in range(BLK):
                        pe.matmul(ax[q][:, P * b:P * b + P], evtok[:, b, P * q:P * q + P], att[:, q, b, :],
                                  start=(b == 0), stop=False, skip_group_check=True)
                    for c in range(1, NCH):
                        ins = pe.matmul(ax[q][:, CH * c:CH * c + CH], states[r:r + 64, q // 2, c - 1, :],
                                        eq[r:r + 64, q // 2, CH * c:CH * c + CH], start=False, stop=(c == NCH - 1),
                                        skip_group_check=True)
                    ins.then_inc(s_o, 1)

            def gla_dec_out(part):
                if part == 0:
                    pe.wait_ge(s_st, 2 * NCH)
                    pe.wait_ge(s_qm, 1)
                for b in (2 * part, 2 * part + 1):
                    for i in range(2):
                        at_ = 2 * (NS * i + b)
                        ins = pe.matmul(ax[3][:, at_:at_ + 2], gs[:, i, b, :], qmask[:, i, b, :], start=True, stop=True)
                if part == 3:
                    ins.then_inc(s_od, 1)

            def gla_sum(q):
                if q == 0:
                    pe.wait_ge(s_oc, 4)
                pe.wait_ge(s_osq, q + 1)
                mean_square(osq[q], 64 + 5 * q, s_oms)

            def gla_spread(part):
                if part == 0:
                    pe.wait_ge(s_orr, 1)
                    pe.wait_ge(s_odc, 1)
                    for q in range(HEADS):
                        spread_blocks(3, 96 + 8 * q, 5 * q, [BLK])
                else:
                    pe.wait_ge(s_on, 1)
                for q in (range(3) if part == 0 else (3,)):
                    spread_blocks(q % 3, 0, 5 * q, range(BLK)).then_inc(s_obc, 1)

            for name in E_ORDER:
                e_tile(name)
                if name == "u0":
                    gla_turn_v()
                if name == "u1":
                    gla_att()
                if name == "u2":
                    gla_turn_k()
                if name == "u3":
                    gla_spread_v()
                if name == "g0":
                    gla_chunk_kv()
                if name == AFTER_O:
                    gla_out()
            EO_POOL, EO_HEADS = (4, 5, 6, 7), (0, 1, 2, 3)

            def eo_part(n, j, ks_, before=None):
                m = M_EO + 2 * n + j
                product(m, m % 2, [(k, k) for k in ks_], weights(n % 2, P * j, 256), (op_hi, op_lo), ks_[0] == 4,
                        ks_[-1] == 3, before=before, count=ks_[-1] == 3)

            pe.wait_ge(s_wlo, C_EO + 1)
            pe.wait_ge(s_oplo, 4)
            for j in range(2):
                eo_part(0, j, EO_POOL)
            for j in range(2):
                eo_part(0, j, EO_HEADS, before=(lambda k: pe.wait_ge(s_oplo, k + 5)) if j == 0 else None)
            for n in range(1, N_EO):
                pe.wait_ge(s_wlo, C_EO + n + 1)
                for j in range(2):
                    eo_part(n, j, EO_POOL + EO_HEADS)

            def norm_inside(n):
                def after(k):
                    if k == 4:
                        norm_sum(n)
                    if k == KT - 1:
                        norm_spread(n)
                return after

            def ffn(l):
                c0, m0, d0, dm = C_F[l], M_F[l], C_D[l], M_D[l]

                def pair(i, first=False):
                    for j in range(2):
                        n = 2 * i + j
                        pe.wait_ge(s_wlo, c0 + n + 1)
                        for u in range(2):
                            start = first and j == 0 and u == 0
                            product(m0 + 2 * n + u, (m0 + u) % 2, KS, weights(j, P * u, 256), h, True, True,
                                    before=h_ready(1 + 2 * l) if start else None,
                                    after=norm_inside(1 + 2 * l) if start else None)

                pair(0, first=True)
                with pe.Fori(1, N_F // 2) as i:
                    pair(i)

                def hid_ready(k):
                    if k >= FT - 4:
                        pe.wait_ge(s_hidlo, FT * l + k + 1)

                def down(m, u, check=False):
                    for half in range(2):
                        pe.wait_ge(s_wlo, d0 + 2 * m + half + 1)
                        product(dm + m, (dm + u) % 2, [(k, 11 * half + k) for k in range(11)], weights(half, 0, P),
                                (hid_hi, hid_lo), half == 0, half == 1, before=hid_ready if check else None)

                with pe.Fori(0, KT // 2 - l) as i:
                    for u in range(2):
                        down(2 * i + u, u, check=u == 0)
                if l == 1:
                    down(KT - 2, 0)

            ffn(0)

            def dec_out(hh, b):
                if b == 0:
                    pe.wait_ge(r_vl, hh + 1)
                    if isinstance(hh, int) and hh == 0:
                        pe.wait_ge(r_sel, 3)
                pe.wait_ge(r_tl, 8 * hh + b + 1)
                for part in (th, tl):
                    ins = pe.matmul(ax[3][:], osel[:, NS - 1 - b:NS - 1 - b + P], part[:], start=(b == 0 and part is th),
                                    stop=(b == NS - 1 and part is tl))
                ins.then_inc(r_os, 1)

            def turn_out(hp):
                pe.wait_ge(r_osr, hp + 1)
                pe.sem_inc(s_tstep, 1)
                for d in range(4):
                    ins = pe.transpose(ax[3][:, NS * d:NS * d + NS], t2[0:NS, P * d:P * d + P], ident[0:NS, 0:NS])
                ins.then_inc(r_ot, 1)

            def finish_sum(hp):
                pe.wait_ge(r_acc, 5 * hp + 5)
                mean_square(t0, 64, r_ms)

            def finish_spread(hp):
                pe.wait_ge(r_rr, hp + 1)
                spread(2, 72, 0, r_bc)

            def head(hh):
                m0 = M_OI + 12 * hh
                first = isinstance(hh, int) and hh == 0

                def tile_(t, inside=None):
                    if t % 2 == 0:
                        pe.wait_ge(s_wlo, C_OI + 6 * hh + t // 2 + 1)
                    start = first and t == 0
                    product(m0 + t, (M_OI + t) % 2, KS, weights((t // 2) % 2, P * (t % 2), 256), h, True, True,
                            before=h_ready(2) if start else None, after=norm_inside(2) if start else inside)

                def turn_v(b):
                    if b < 2:
                        if not first:
                            pe.wait_ge(r_stc, 2 * hh - 1 + b)
                    else:
                        pe.wait_ge(r_trc, 4 * hh + b - 1)
                    pe.wait_ge(s_out, m0 + 4)
                    for q in range(4):
                        ins = pe.transpose(ax[b % 2][:, P * q:P * q + P], rv[:, q, P * b:P * b + P], ident[:])
                    ins.then_inc(r_tr, 1)

                def turn_vs():
                    if not first:
                        pe.wait_ge(r_rc, hh)
                    for q in range(4):
                        ins = pe.transpose(ax[3][0:NS, P * q:P * q + P], rv[:, q, NP_:T], ident[:])
                    ins.then_inc(r_tr, 1)

                def scores(j):
                    pe.wait_ge(r_rot, 4 * hh + 4)
                    pe.wait_ge(*((r_trc, 4 * hh + 3 + j) if j < 2 else (r_p, 4 * hh + j - 1)))
                    for t in range(2):
                        ins = pe.matmul(ax[j % 2][:, 0:NP_ - P * j], rk[:, t, P * j:P * j + P], rq[:, t, P * j:NP_],
                                        start=(t == 0), stop=(t == 1))
                    ins.then_inc(r_sc, 1)

                def turn_k(q):
                    pe.wait_ge(r_p, 4 * hh + 3 + q)
                    for b in range(2):
                        for i in range(2):
                            ins = pe.transpose(ax[q][:, 256 * b + P * i:256 * b + P * i + P],
                                               rk[:, i, P * (2 * q + b):P * (2 * q + b) + P], ident[:])
                    ins.then_inc(r_tr, 1)

                def pv(q):
                    pe.wait_ge(*((r_ktc, 2 * hh + q + 1) if q < 2 else (r_pvc, 4 * hh + q - 1)))
                    if q == 0:
                        pe.wait_ge(r_pl, 4 * hh + 4)
                    for j in range(BLK):
                        for n, (v, p_) in enumerate(((vtok, prob), (vtok_lo, prob), (vtok, prob_lo))):
                            ins = pe.matmul(ax[q % 2][:, P * j:NP_], v[:, j, P * q:P * q + P],
                                            p_[:, PROB_AT[j]:PROB_AT[j + 1]], start=(j == 0 and n == 0),
                                            stop=(j == BLK - 1 and n == 2))
                    ins.then_inc(r_pv, 1)

                def state(q):
                    pe.wait_ge(r_pvc, 4 * hh + 3 + q)
                    for j in range(BLK):
                        for n, (k, v) in enumerate(((ktok, vtok), (ktok_lo, vtok), (ktok, vtok_lo))):
                            ins = pe.matmul(ax[q][:], k[:, j, P * q:P * q + P], v[:, j, :], start=(j == 0 and n == 0),
                                            stop=(j == BLK - 1 and n == 2))
                    ins.then_inc(r_st, 1)

                def spread_v(b):
                    want(pe, r_sn, 8 * hh + b)
                    if b == 0:
                        pe.wait_ge(r_vl, hh + 1)
                        if first:
                            pe.wait_ge(r_sel, 3)
                            pe.wait_ge(s_rstd, 3)
                    pe.matmul(ax[2][:], vsel[0:64, b:b + 1].to_broadcast([64, P]), vs[:], start=True, stop=True).then_inc(r_vb, 1)

                tile_(0)
                if not first:
                    dec_out(hh - 1, 7)
                tile_(1)
                if not first:
                    turn_out(hh - 1)
                tile_(2)
                tile_(3)
                if not first:
                    finish_sum(hh - 1)
                tile_(4)
                if not first:
                    finish_spread(hh - 1)
                turn_v(0)
                turn_v(1)
                tile_(5)
                turn_v(2)
                turn_v(3)
                tile_(6)
                tile_(7)
                turn_vs()
                tile_(8)
                scores(0)
                scores(1)
                spread_v(0)
                tile_(9, lambda k: spread_v(1) if k == KT // 2 else None)
                scores(2)
                scores(3)
                dec_out(hh, 0)
                spread_v(2)
                tile_(10)
                turn_k(0)
                turn_k(1)
                dec_out(hh, 1)
                spread_v(3)
                tile_(11)
                dec_out(hh, 2)
                spread_v(4)
                pv(0)
                pv(1)
                dec_out(hh, 3)
                spread_v(5)
                pv(2)
                pv(3)
                dec_out(hh, 4)
                spread_v(6)
                state(0)
                dec_out(hh, 5)
                spread_v(7)
                state(1)
                dec_out(hh, 6)

            head(0)
            with pe.Fori(1, HEADS) as hh:
                head(hh)

            last = HEADS - 1

            def out_part(n, k):
                if k == 0:
                    pe.wait_ge(s_wlo, C_OO + n + 1)
                if n == 0:
                    pe.wait_ge(s_olo, k + 1)
                product(M_OO + n, (M_OO + n) % 2, [(OO_ORDER[k], OO_ORDER[k])], weights(n % 2, 0, P), (o_hi, o_lo),
                        k == 0, k == 15, count=k == 15)

            meanwhile = {1: lambda: dec_out(last, 7), 3: lambda: turn_out(last), 5: lambda: finish_sum(last),
                         7: lambda: finish_spread(last)}
            for k in range(9):
                out_part(0, k)
                if k > OO_ALONE:
                    out_part(1, k)
                meanwhile.get(k, lambda: None)()
                if k == OO_ALONE:
                    for k1 in range(OO_ALONE + 1):
                        out_part(1, k1)
            for n, ks_ in ((0, (9, 10, 11)), (1, (9, 10)), (0, (12, 13, 14, 15)), (1, (11, 12, 13, 14, 15))):
                for k in ks_:
                    out_part(n, k)
            with pe.Fori(1, N_OO // 2) as i:
                for j in range(2):
                    n = 2 * i + j
                    pe.wait_ge(s_wlo, C_OO + n + 1)
                    product(M_OO + n, (M_OO + j) % 2, [(k, k) for k in OO_ORDER], weights(j, 0, P), (o_hi, o_lo), True,
                            True)
            ffn(1)
            def y_sum(part):
                bank = ax[(3, 0)[part]]
                blocks = Y_PARTS[part][2]
                for src, ready, count in ((acc, s_acc, 8 * 4 + 7), (sq, s_sql, part + 1)):
                    pe.wait_ge(ready, count)
                    for i in blocks:
                        a = BLOCKS[i][0]
                        ins = pe.matmul(bank[:, 64 + i:65 + i], src[:, a:a + P], ones[:, 0:1],
                                        start=(src is acc and i == blocks[0]), stop=(src is sq), skip_group_check=True)
                ins.then_inc(s_ms, 1)

            def y_spread(part):
                pe.wait_ge(s_rr, 5 + part)
                for i in Y_PARTS[part][2]:
                    a, c, n = BLOCKS[i]
                    dst = ax[2 - part][:, a:a + P] if i < BLK else ax[0][:, 72:72 + NS]
                    ins = pe.matmul(dst, rr[:, i:i + 1].to_broadcast([P, P]), ident[:, c:c + n], start=True, stop=True)
                ins.then_inc(s_bc, 1)

            m = M_D[1] + KT - 1
            pe.wait_ge(s_out, m - 1)
            for t in range(2):
                for n in range(FT):
                    if n % 11 == 0:
                        pe.wait_ge(s_wlo, C_D[1] + N_D - 1 + n // 11)
                    for q, (a, b) in enumerate(((0, 0), (0, 1), (1, 0))):
                        ins = pe.matmul(ps[m % 2][:, t, 0:HT], weights(n // 11, 0, P)(a, n % 11),
                                        (hid_hi, hid_lo)[b][:, n, HT * t:HT * t + HT], start=(n == 0 and q == 0),
                                        stop=(n == FT - 1 and q == 2))
                    if t == 1 and n == Y_AFTER[0]:
                        y_sum(0)
                    if t == 1 and n == Y_AFTER[1]:
                        y_spread(0)
                ins.then_inc((s_half, s_mm)[t], 1)
            y_sum(1)
            y_spread(1)


def columns(w, n):
    k = w.shape[0] // P
    return w.reshape(k, P, -1, n).transpose(2, 1, 0, 3).reshape(-1, P, k * n)


def down_chunks(w):
    return w.reshape(2, 11, P, KT, P).transpose(3, 0, 2, 1, 4).reshape(N_D, P, W_DOWN)


def gate_up(gate, up):
    g, u = (m.reshape(KT, P, FT, P) for m in (gate, up))
    return np.stack([g, u], axis=3).transpose(2, 1, 0, 3, 4).reshape(FT, P, W_FULL)


def tables():
    f = np.float32
    angle = (1.0 / (f(10000.0) ** np.linspace(0.0, 1.0, P, dtype=f))).astype(f)
    pos = np.concatenate([np.arange(NP_), np.full(NS, 4096)]).astype(f)
    ang = (angle[:, None] * pos[None, :]).astype(f).astype(np.float64)
    cs = np.stack([np.cos(ang), np.sin(ang)], axis=1).astype(f)
    gamma = 1.0 - 2.0 ** (-5.0 - np.arange(HEADS))
    s, t = np.arange(P)[:, None], np.arange(NP_)[None, :]
    dec = np.stack([np.where(t >= s, g ** np.maximum(t - s, 0).astype(np.float64), 0.0) / 16 for g in gamma]).astype(f)
    kscale = np.stack([g ** (NP_ - 1.0 - P * b - np.arange(P)) / 16 for g in gamma for b in range(BLK)], axis=1)
    gm = np.tile(gamma[None, :], (P, 1))
    reset = np.ones((P, NP_), f)
    reset[:, ::CH] = 0
    inv = np.stack([1.0 / np.minimum(2 << g, np.arange(16) + 1.0) for g in range(4)])
    return dict(cs=cs, dec=dec, kscale=kscale.astype(f), gm=gm.astype(f), reset=reset,
                invc=np.tile(inv[None], (P, 1, 1)).astype(f), ident=np.eye(P, dtype=f),
                ones=np.concatenate([np.full((P, 1), 1.0 / DM), np.ones((P, 7)),
                                     (np.arange(P)[:, None] % 32 == np.arange(8)) & (np.arange(P)[:, None] < 64)],
                                    axis=1).astype(f))


def kernel(**inputs):
    import concourse.bacc as bacc
    from concourse.bass_utils import run_bass_kernel_spmd

    v = {k: np.asarray(a) for k, a in inputs.items()}
    c = tables()
    tiles = lambda a: a.reshape(-1, P).T
    we, wo = v["w_in_even"][0], v["w_in_odd"][0]
    cols = []
    for hh in range(HEADS):
        q, k = hh * 256, 1024 + hh * 256
        cols += [np.arange(2048 + 512 * hh, 2560 + 512 * hh)]
        cols += [np.arange(s + e, s + 256, 2) for s in (q, k) for e in (0, 1)]
        cols += [np.arange(4096 + 512 * hh, 4608 + 512 * hh)]
    arrays = dict(
        x=np.concatenate([v["x_prompt"][0], v["x_sample"][:, 0]]).T.reshape(KT, P, T).transpose(1, 0, 2),
        vec=np.concatenate([tiles(v["norm_mix"][0]), tiles(v["norm_ffn"][0]), tiles(v["norm_mix"][1]),
                            tiles(v["norm_ffn"][1]), tiles(v["norm_final"]), tiles(v["gla_gain"][0]),
                            tiles(v["pool_scale"][0]), tiles(v["b_gate"][0]), c["kscale"], c["gm"]], axis=1),
        w_a=np.pad(we[:, 1536:1552], ((0, 0), (0, P - 16))).reshape(KT, P, P).transpose(1, 0, 2).reshape(P, KT * P),
        w_e=columns(np.concatenate([we[:, 0:1024], we[:, 1552:2064], we[:, 1024:1536]], axis=1), 256),
        w_eo=columns(v["w_out_even"][0], 256),
        w_f0=gate_up(v["w_ffn_gate"][0], v["w_ffn_up"][0]), w_d0=down_chunks(v["w_ffn_down"][0]),
        w_oi=columns(wo[:, np.concatenate(cols)], 256), w_oo=columns(v["w_out_odd"][0], P),
        w_f1=gate_up(v["w_ffn_gate"][1], v["w_ffn_up"][1]), w_d1=down_chunks(v["w_ffn_down"][1]),
        wgb=v["w_gate_b"][0], poolw=v["pool_w"][0].transpose(1, 0, 2),
        gs=v["state_gla"][0].reshape(NS, 2, P, P).transpose(2, 1, 0, 3),
        pbuf=v["state_pool"][0].reshape(NS, 15, 4, P).transpose(3, 2, 0, 1),
        ret_in=v["state_ret"][0].reshape(NS * HEADS, P, 1024),
        cs=c["cs"], dec=c["dec"], reset=c["reset"], invc=c["invc"], ident=c["ident"], ones=c["ones"])
    outs = dict(y=(P, KT, T), gla_p=(P, 2, P), gla_s=(P, 2, NS, P), rows=(P, 4, NS + 1, 15),
                ret_p=(HEADS, P, 1024), ret_s=(NS * HEADS, P, 1024))
    nc = bacc.Bacc("TRN2", target_bir_lowering=False, num_devices=1)
    arrays = {"in_" + n: np.ascontiguousarray(a) for n, a in arrays.items()}
    io = {n[3:]: nc.dram_tensor(n, a.shape, F32, kind="ExternalInput").ap() for n, a in arrays.items()}
    io.update({n: nc.dram_tensor("out_" + n, s, F32, kind="ExternalOutput").ap() for n, s in outs.items()})
    build(nc, io)
    r = run_bass_kernel_spmd(nc, [arrays], core_ids=[0]).results[0]
    y = r["out_y"].transpose(2, 1, 0).reshape(T, DM)
    rows = r["out_rows"].transpose(2, 3, 1, 0).reshape(NS + 1, 15, 512)
    return (y[None, :NP_], y[NP_:, None],
            r["out_gla_p"].transpose(1, 0, 2).reshape(1, 1, HEADS, 64, P),
            r["out_gla_s"].transpose(2, 1, 0, 3).reshape(1, NS, HEADS, 64, P),
            rows[None, NS:], rows[None, :NS],
            r["out_ret_p"].reshape(1, 1, HEADS, 256, 512),
            r["out_ret_s"].reshape(1, NS, HEADS, 256, 512))
```
